# Optimizing a Trainium2 kernel written in Bass

```python
import math
import jax, jax.numpy as jnp
from jax import lax
import numpy as np

D_MODEL = 2048
BATCH = 1
SEQ = 256
DEPTH = 2

CHUNK = 64
HEAD_DIM = 64
ROPE_THETA = 10000.0
NORM_EPS = 1e-6
NEG_INF = -1e30

GLA_HEADS = 4
GLA_DK = 128
GLA_DV = 256
GLA_RANK = 16
GLA_TAU = 16.0
GLA_BLOCK = 16

DIFF_HEADS = 4
DIFF_DV = 2 * HEAD_DIM
DIFF_Q_BLOCK = 128

SWA_Q_HEADS = 8
SWA_KV_HEADS = 2
SWA_GROUP = SWA_Q_HEADS // SWA_KV_HEADS
SWA_WINDOW = 128
SWA_WINDOW_CHUNKS = SWA_WINDOW // CHUNK

GLA_WIDTH = GLA_HEADS * GLA_DV
DIFF_WIDTH = DIFF_HEADS * DIFF_DV
SWA_WIDTH = SWA_Q_HEADS * HEAD_DIM
MIX_WIDTH = GLA_WIDTH + DIFF_WIDTH + SWA_WIDTH

D_FF = -(-8 * D_MODEL // (3 * 256)) * 256
PLE_DIM = 256

IN_SIZES = (
    GLA_HEADS * GLA_DK, GLA_HEADS * GLA_DK, GLA_WIDTH, GLA_WIDTH, GLA_RANK,
    DIFF_HEADS * 2 * HEAD_DIM, DIFF_HEADS * 2 * HEAD_DIM, DIFF_WIDTH,
    SWA_Q_HEADS * HEAD_DIM, SWA_KV_HEADS * HEAD_DIM, SWA_KV_HEADS * HEAD_DIM,
)
N_IN = sum(IN_SIZES)

kernel_name = "hybrid_gla_diff_swa_chunk_causal_trunk"

def rms_norm(t, g):
    tf = t.astype(jnp.float32)
    y = tf * lax.rsqrt(jnp.mean(tf * tf, axis=-1, keepdims=True) + NORM_EPS)
    return (y * g.astype(jnp.float32)).astype(t.dtype)

def rope_tables(positions):
    inv = 1.0 / (ROPE_THETA ** (jnp.arange(0, HEAD_DIM, 2, dtype=jnp.float32) / HEAD_DIM))
    ang = positions.astype(jnp.float32)[..., None] * inv
    ang = jnp.concatenate([ang, ang], axis=-1)
    return jnp.cos(ang), jnp.sin(ang)

def apply_rope(t, cos, sin):
    bshape = cos.shape[:2] + (1,) * (t.ndim - 3) + (HEAD_DIM,)
    c, s = cos.reshape(bshape), sin.reshape(bshape)
    half = HEAD_DIM // 2
    rot = jnp.concatenate([-t[..., half:], t[..., :half]], axis=-1)
    return (t.astype(jnp.float32) * c + rot.astype(jnp.float32) * s).astype(t.dtype)

def gla_mixer(q, k, v, a_lr, g_out, w_alpha, b_alpha, norm_g):
    B, S = q.shape[0], q.shape[1]
    n = S // GLA_BLOCK
    log_a = jax.nn.log_sigmoid((a_lr @ w_alpha + b_alpha).astype(jnp.float32)) / GLA_TAU
    log_a = log_a.reshape(B, S, GLA_HEADS, GLA_DK)

    def blk(t):
        return t.reshape(B, n, GLA_BLOCK, GLA_HEADS, t.shape[-1]).transpose(1, 0, 3, 2, 4)

    qc = blk(q * (GLA_DK ** -0.5))
    kc, vc = blk(k), blk(v)
    b = jnp.cumsum(blk(log_a), axis=-2)
    b_last = b[..., -1:, :]
    q_dec = qc * jnp.exp(b)
    k_inv = kc * jnp.exp(-b)
    k_to_end = kc * jnp.exp(b_last - b)
    causal = jnp.tril(jnp.ones((GLA_BLOCK, GLA_BLOCK), dtype=bool))
    attn = jnp.where(causal, jnp.einsum('nbhtd,nbhsd->nbhts', q_dec, k_inv), 0.0)
    o_intra = jnp.einsum('nbhts,nbhsv->nbhtv', attn, vc)

    def step(state, inp):
        q_d, k_e, v_b, dec = inp
        o = jnp.einsum('bhtd,bhdv->bhtv', q_d, state)
        state = state * dec[..., 0, :, None] + jnp.einsum('bhsd,bhsv->bhdv', k_e, v_b)
        return state, o

    state0 = jnp.zeros((B, GLA_HEADS, GLA_DK, GLA_DV), jnp.float32)
    _, o_inter = lax.scan(step, state0, (q_dec, k_to_end, vc.astype(jnp.float32), jnp.exp(b_last)))
    o = (o_intra + o_inter).transpose(1, 0, 3, 2, 4).reshape(B, S, GLA_HEADS, GLA_DV)
    o = rms_norm(o, norm_g) * jax.nn.silu(g_out.astype(jnp.float32))
    return o.reshape(B, S, GLA_WIDTH)

def diff_attention(q, k, v, lam, lam_init, subln_g):
    B, S = q.shape[0], q.shape[1]
    nq = S // DIFF_Q_BLOCK
    scale = HEAD_DIM ** -0.5
    q_blocks = jnp.moveaxis(q.reshape(B, nq, DIFF_Q_BLOCK, DIFF_HEADS, 2, HEAD_DIM), 1, 0)
    key_chunk = jnp.arange(S) // CHUNK

    def one_block(args):
        q_blk, j = args
        s = jnp.einsum('bqhcd,bkhcd->bhcqk', q_blk, k).astype(jnp.float32) * scale
        q_chunk = (j * DIFF_Q_BLOCK + jnp.arange(DIFF_Q_BLOCK)) // CHUNK
        allowed = key_chunk[None, :] <= q_chunk[:, None]
        probs = jax.nn.softmax(jnp.where(allowed, s, NEG_INF), axis=-1)
        w = probs[:, :, 0] - lam * probs[:, :, 1]
        return jnp.einsum('bhqk,bkhv->bqhv', w.astype(v.dtype), v)

    o = lax.map(one_block, (q_blocks, jnp.arange(nq)))
    o = jnp.moveaxis(o, 0, 1).reshape(B, S, DIFF_HEADS, DIFF_DV)
    o = rms_norm(o, subln_g) * (1.0 - lam_init)
    return o.reshape(B, S, DIFF_WIDTH)

def swa_sink_attention(q, k, v, sinks):
    B, S = q.shape[0], q.shape[1]
    n = S // CHUNK
    W = SWA_WINDOW_CHUNKS
    scale = HEAD_DIM ** -0.5
    qc = q.reshape(B, n, CHUNK, SWA_KV_HEADS, SWA_GROUP, HEAD_DIM)

    def band(t):
        tc = t.reshape(B, n, CHUNK, SWA_KV_HEADS, HEAD_DIM)
        tp = jnp.concatenate([jnp.zeros_like(tc[:, :W - 1]), tc], axis=1)
        return jnp.concatenate([tp[:, w:w + n] for w in range(W)], axis=2)

    kb, vb = band(k), band(v)
    s = jnp.einsum('bnqhgd,bnkhd->bnhgqk', qc, kb).astype(jnp.float32) * scale
    slot_chunk = jnp.arange(n)[:, None] - (W - 1) + jnp.arange(W * CHUNK)[None, :] // CHUNK
    s = jnp.where((slot_chunk >= 0)[None, :, None, None, None, :], s, NEG_INF)
    sink = jnp.broadcast_to(
        sinks.astype(jnp.float32).reshape(1, 1, SWA_KV_HEADS, SWA_GROUP, 1, 1), s.shape[:-1] + (1,))
    probs = jax.nn.softmax(jnp.concatenate([s, sink], axis=-1), axis=-1)[..., :-1]
    o = jnp.einsum('bnhgqk,bnkhd->bnqhgd', probs.astype(v.dtype), vb)
    return o.reshape(B, S, SWA_WIDTH)

def setup_inputs(seed: int = 0) -> dict:
    key = jax.random.key(seed)
    ks = jax.random.split(key, 32)
    f32 = jnp.float32

    def nrm(k, shape, scale):
        return jax.random.normal(k, shape, f32) * scale

    def gain(k, shape):
        return 1.0 + 0.05 * jax.random.normal(k, shape, f32)

    offsets = jax.random.randint(ks[2], (BATCH,), 0, 8192, dtype=jnp.int32)
    positions = offsets[:, None] + jnp.arange(SEQ, dtype=jnp.int32)[None, :]
    return {
        "x": nrm(ks[0], (BATCH, SEQ, D_MODEL), 1.0),
        "p": nrm(ks[1], (DEPTH, BATCH, SEQ, PLE_DIM), 1.0),
        "positions": positions,
        "norm_mix_g": gain(ks[3], (DEPTH, D_MODEL)),
        "w_in": nrm(ks[4], (DEPTH, D_MODEL, N_IN), D_MODEL ** -0.5),
        "gla_w_alpha": nrm(ks[5], (DEPTH, GLA_RANK, GLA_HEADS * GLA_DK), GLA_RANK ** -0.5),
        "gla_b_alpha": nrm(ks[6], (DEPTH, GLA_HEADS * GLA_DK), 0.1),
        "gla_norm_g": gain(ks[7], (DEPTH, GLA_DV)),
        "diff_q_norm_g": gain(ks[8], (DEPTH, HEAD_DIM)),
        "diff_k_norm_g": gain(ks[9], (DEPTH, HEAD_DIM)),
        "diff_lambda_q1": nrm(ks[10], (DEPTH, HEAD_DIM), 0.1),
        "diff_lambda_k1": nrm(ks[11], (DEPTH, HEAD_DIM), 0.1),
        "diff_lambda_q2": nrm(ks[12], (DEPTH, HEAD_DIM), 0.1),
        "diff_lambda_k2": nrm(ks[13], (DEPTH, HEAD_DIM), 0.1),
        "diff_subln_g": gain(ks[14], (DEPTH, DIFF_DV)),
        "swa_q_norm_g": gain(ks[15], (DEPTH, HEAD_DIM)),
        "swa_k_norm_g": gain(ks[16], (DEPTH, HEAD_DIM)),
        "swa_sinks": nrm(ks[17], (DEPTH, SWA_Q_HEADS), 0.5),
        "w_out": nrm(ks[18], (DEPTH, MIX_WIDTH, D_MODEL), MIX_WIDTH ** -0.5),
        "norm_ffn_g": gain(ks[19], (DEPTH, D_MODEL)),
        "w_ffn_in": nrm(ks[20], (DEPTH, D_MODEL, 2 * D_FF), D_MODEL ** -0.5),
        "w_ffn_out": nrm(ks[21], (DEPTH, D_FF, D_MODEL), D_FF ** -0.5),
        "norm_ple_g": gain(ks[22], (DEPTH, D_MODEL)),
        "w_ple_gate": nrm(ks[23], (DEPTH, D_MODEL, D_MODEL), D_MODEL ** -0.5),
        "w_ple_proj": nrm(ks[24], (DEPTH, PLE_DIM, D_MODEL), PLE_DIM ** -0.5),
    }

def reference(x, p, positions, norm_mix_g, w_in, gla_w_alpha, gla_b_alpha, gla_norm_g,
              diff_q_norm_g, diff_k_norm_g, diff_lambda_q1, diff_lambda_k1, diff_lambda_q2,
              diff_lambda_k2, diff_subln_g, swa_q_norm_g, swa_k_norm_g, swa_sinks, w_out,
              norm_ffn_g, w_ffn_in, w_ffn_out, norm_ple_g, w_ple_gate, w_ple_proj):
    B, S, _ = x.shape
    cos, sin = rope_tables(positions)
    split_points = np.cumsum(IN_SIZES)[:-1].tolist()
    h = x
    for i in range(DEPTH):
        u = rms_norm(h, norm_mix_g[i])
        (g_q, g_k, g_v, g_gate, g_alr, d_q, d_k, d_v, s_q, s_k, s_v) = jnp.split(
            u @ w_in[i], split_points, axis=-1)

        o_gla = gla_mixer(
            g_q.reshape(B, S, GLA_HEADS, GLA_DK), g_k.reshape(B, S, GLA_HEADS, GLA_DK),
            g_v.reshape(B, S, GLA_HEADS, GLA_DV), g_alr, g_gate.reshape(B, S, GLA_HEADS, GLA_DV),
            gla_w_alpha[i], gla_b_alpha[i], gla_norm_g[i])

        dq = apply_rope(rms_norm(d_q.reshape(B, S, DIFF_HEADS, 2, HEAD_DIM), diff_q_norm_g[i]), cos, sin)
        dk = apply_rope(rms_norm(d_k.reshape(B, S, DIFF_HEADS, 2, HEAD_DIM), diff_k_norm_g[i]), cos, sin)
        lam_init = 0.8 - 0.6 * math.exp(-0.3 * i)
        lam = (jnp.exp(jnp.sum(diff_lambda_q1[i].astype(jnp.float32) * diff_lambda_k1[i].astype(jnp.float32)))
               - jnp.exp(jnp.sum(diff_lambda_q2[i].astype(jnp.float32) * diff_lambda_k2[i].astype(jnp.float32)))
               + lam_init)
        o_diff = diff_attention(dq, dk, d_v.reshape(B, S, DIFF_HEADS, DIFF_DV), lam, lam_init, diff_subln_g[i])

        sq = apply_rope(rms_norm(s_q.reshape(B, S, SWA_Q_HEADS, HEAD_DIM), swa_q_norm_g[i]), cos, sin)
        sk = apply_rope(rms_norm(s_k.reshape(B, S, SWA_KV_HEADS, HEAD_DIM), swa_k_norm_g[i]), cos, sin)
        o_swa = swa_sink_attention(sq, sk, s_v.reshape(B, S, SWA_KV_HEADS, HEAD_DIM), swa_sinks[i])

        mix = jnp.concatenate([o_gla.astype(h.dtype), o_diff.astype(h.dtype), o_swa.astype(h.dtype)], axis=-1)
        h = h + mix @ w_out[i]

        u = rms_norm(h, norm_ffn_g[i])
        gate, up = jnp.split(u @ w_ffn_in[i], 2, axis=-1)
        h = h + (jax.nn.silu(gate) * up) @ w_ffn_out[i]

        ple_gate = jax.nn.sigmoid((rms_norm(h, norm_ple_g[i]) @ w_ple_gate[i]).astype(jnp.float32))
        h = h + ((p[i] @ w_ple_proj[i]).astype(jnp.float32) * ple_gate).astype(h.dtype)
    return h


_drawn_inputs = setup_inputs


def setup_inputs(seed=0):
    import zlib

    import numpy as np

    out = dict(_drawn_inputs(seed))
    spreads = {}
    factors = {'diff_lambda_q1': 2.765,
     'diff_lambda_k1': 3.674,
     'swa_q_norm_g': 8.0,
     'swa_k_norm_g': 8.0,
     'swa_sinks': 8.0,
     'norm_ple_g': 5.282,
     'diff_lambda_q2': 2.766}
    for name, (base, spread) in spreads.items():
        noise = np.random.default_rng([zlib.crc32(name.encode()), seed]).standard_normal(out[name].shape)
        drawn = base * np.exp(spread * noise) if base else spread * noise
        out[name] = __import__('jax').numpy.asarray(drawn.astype(out[name].dtype))
    for name, factor in factors.items():
        out[name] = (out[name] * factor).astype(out[name].dtype)
    return out
```

```python
from contextlib import ExitStack, contextmanager

import concourse.bass as bass
from concourse import mybir

F32 = mybir.dt.float32
F32R = mybir.dt.float32r
I32 = mybir.dt.int32
ALU = mybir.AluOpType
ACT = mybir.ActivationFunctionType
AX = mybir.AxisListType

P = 128
D = 2048
S = 256
DEPTH = 2
HD = 64
HALF = HD // 2
CHUNK = 64
EPS = 1e-6
NEG = -1e30

GLA_H, DK, DV, RANK, BLK = 4, 128, 256, 16, 16
GLA_TAU = 16.0
DIFF_H = 4
SWA_H, SWA_KV = 8, 2
N_IN = 5392
MIX = 2048
D_FF = 5632
PLE = 256

KT = D // P
TT = S // P
G = 256
UK = 4
NBLK = S // BLK
SCALE = HD ** -0.5
GLA_SCALE = DK ** -0.5

C_GQ = 0
C_ALR = 2 * GLA_H * DK + 2 * GLA_H * DV
C_DQ = C_ALR + RANK
C_SKV = N_IN - 2 * SWA_KV * HD

ROUNDS = (16, 16, 12)
assert sum(ROUNDS) * P == D_FF

UNITS_WIN = 21 * 4
UNITS_PER_LAYER = UNITS_WIN + 2 * 8 * 2 + sum(ROUNDS) * 4 + sum(ROUNDS) // UK * 8 + 4 + 8 * 4
GROUPS_PER_LAYER = 22 + 16 + sum(ROUNDS) + 8 * len(ROUNDS) + 8 + 8
CROSSED = 22 + sum(ROUNDS) + 16
EV = 18
AHEAD = 3
RING = 4

K_ID, K_ROT, K_SEL, K_RSEL, K_BLK, K_TRI = 0, 128, 256, 512, 768, 896
K_INV, K_LAM, K_ONE_LAM = 1280, 1281, 1283
K_COLS = 1285

R_MIX, R_FFN, R_PLE, R_BAL, R_GLA, R_SUB, R_DQ, R_DK, R_SQ, R_SK = 0, 16, 32, 48, 52, 54, 55, 56, 57, 58
R_ALL = 59

INV_2PI = 0.15915494309189535
PI2_A, PI2_B = 6.28125, 0.0019350051879882812
PI2_C = 6.283185307179586 - PI2_A - PI2_B
MAGIC = 12582912.0
PI_LO = 3.1415925


class Count:

    def __init__(self):
        self.n, self.terms = 0, []

    def at(self, k=0):
        value = self.n + k
        for reg, per in self.terms:
            value = reg * per + value
        return value


def turns(eng, times, counts, began):
    @contextmanager
    def run():
        starts = [c.n for c, _ in counts]
        eng.sem_inc(began, 1)
        with eng.Fori(0, times) as i:
            for c, per in counts:
                c.terms.append((i, per))
            yield i
            for (c, per), n0 in zip(counts, starts):
                assert c.n - n0 == per, (c.n - n0, per)
                c.terms.pop()
                c.n = n0 + per * times
    return run()


def build(nc, x, p, positions, norm_mix_g, w_in, gla_w_alpha, gla_b_alpha, gla_norm_g, diff_q_norm_g,
          diff_k_norm_g, diff_lambda_q1, diff_lambda_k1, diff_lambda_q2, diff_lambda_k2, diff_subln_g,
          swa_q_norm_g, swa_k_norm_g, swa_sinks, w_out, norm_ffn_g, w_ffn_in, w_ffn_out, norm_ple_g,
          w_ple_gate, w_ple_proj, consts, out):
    ctx = ExitStack()
    with ctx:
        def sb(name, shape, dt=F32):
            return ctx.enter_context(nc.sbuf_tensor(name, shape, dt))

        def sem(name):
            return ctx.enter_context(nc.semaphore(name))

        def over(name, shape, dt, offset):
            return nc.alloc_sbuf_tensor_at(name, shape, dt, offset=offset)

        hid_at = -(-nc.sbuf_base // 32) * 32
        hid = sb("hid", [P, KT, 2, S], F32R)
        h = sb("h", [P, KT, S])
        u = sb("u", [P, KT, 2, S], F32R)
        raw = sb("raw", [P, RING, UK * G])
        wsp = sb("wsp", [P, RING, UK, 2, G], F32R)
        wide = sb("wide", [P, 2 * D])
        cst = sb("cst", [P, K_COLS])
        prm = sb("prm", [P, DEPTH * R_ALL])
        ones = sb("ones", [P, P])
        epst = sb("epst", [P, 2])
        walr_raw = sb("walr_raw", [P, KT, RANK])
        walr = sb("walr", [P, KT, 2, RANK], F32R)
        wal = sb("wal", [RANK, GLA_H * DK])
        lam = sb("lam", [P, 4, DEPTH])
        sinks = sb("sinks", [P, DEPTH, SWA_H])
        cosB = sb("cosB", [P, S])
        sinB = sb("sinB", [P, S])
        rstdB = sb("rstdB", [P, S])
        rstdC = sb("rstdC", [P, TT])
        sqt = sb("sqt", [P, S])
        ssq = sb("ssq", [P, S])
        cross = sb("cross", [P, 2, 2 * S])
        ta = sb("ta", [P, 2 * S])
        tb = sb("tb", [P, 2 * S])
        sg = sb("sg", [P, 2 * S])
        hf = sb("hf", [P, 2 * S])
        rsn = sb("rsn", [P, 2 * S])
        lnt = sg
        bc = sb("bc", [P, GLA_H, S + 1])
        pe_buf = sb("pe_buf", [P, 2, 2, S])
        st = sb("st", [P, 2, 16])

        early_at = hid_at + 8 * 2 * S * 4
        qg = over("qg", [P, GLA_H, S], F32, early_at)
        kg = over("kg", [P, GLA_H, S], F32, early_at + 4096)
        gt = over("gt", [P, GLA_H, S], F32, early_at + 8192)
        att = over("att", [P, 3 * P], F32, early_at + 12288)
        sk = over("sk", [P, S], F32, early_at + 13824)
        svT = over("svT", [P, S], F32, early_at + 14848)
        alr = over("alr", [P, TT, RANK], F32, early_at + 15872)
        prm_rows = over("prm_rows", [P, P], F32, early_at)
        pos_i = over("pos_i", [P, S], I32, early_at + 1024)
        lamv = over("lamv", [P, 4, DEPTH, HD], F32, early_at + 4096)
        lamp = over("lamp", [P, 2, DEPTH, HD], F32, early_at + 6144)

        kn_at = -(-nc.sbuf_base // 32) * 32
        kn = sb("kn", [P, 8, 2 * P])
        kd = over("kd", [P, 2, S], F32, kn_at)
        sv = over("sv", [P, TT, P], F32, kn_at + 2048)
        wT = over("wT", [P, 2, 4, P], F32, kn_at + 3072)

        dq_at = -(-nc.sbuf_base // 32) * 32
        dq = sb("dq", [P, DIFF_H, S])
        dk = sb("dk", [P, DIFF_H, S])
        dv = sb("dv", [P, TT, DIFF_H * P])
        sq = sb("sq", [P, SWA_H // 2, S])
        ptok = over("ptok", [P, TT, PLE], F32, dq_at)
        pT = over("pT", [P, 2, 2, S], F32R, dq_at + 4096)
        alrT = sb("alrT", [RANK, S])

        vg = wide[:, 0:D].rearrange("p (t c) -> p t c", t=TT)
        sgate = wide[:, D:2 * D].rearrange("p (j t) -> p j t", t=S)
        pleT = wide[:, :].rearrange("p (j t) -> p j t", t=S)
        xtok = wide[:, :].rearrange("p (t c) -> p t c", t=TT)

        ident = cst[:, K_ID:K_ID + P]

        pd = ctx.enter_context(nc.psum_tensor("pd", [P, 2, 2, 512], F32))
        pm = ctx.enter_context(nc.psum_tensor("pm", [P, 4, 512], F32))

        s_began = sem("s_began")
        s_small = sem("s_small")
        s_x = sem("s_x")
        s_raw = [sem(f"s_raw{i}") for i in range(RING)]
        s_hi = sem("s_hi")
        s_lo = sem("s_lo")
        s_used = sem("s_used")
        s_half = sem("s_half")
        s_lay = [sem(f"s_lay{i}") for i in range(3)]
        s_walr = sem("s_walr")
        s_p = sem("s_p")
        s_phi = sem("s_phi")
        s_plo = sem("s_plo")
        s_psfree = sem("s_psfree")
        s_cross = sem("s_cross")
        s_hnew = sem("s_hnew")
        s_uhi = sem("s_uhi")
        s_u = sem("s_u")
        s_sqt = sem("s_sqt")
        s_ssq = sem("s_ssq")
        s_nmm = sem("s_nmm")
        s_rln = sem("s_rln")
        s_rstd = sem("s_rstd")
        s_dve = sem("s_dve")
        s_act = sem("s_act")
        s_init = sem("s_init")
        s_inita = sem("s_inita")
        s_tr = sem("s_tr")
        s_trc = sem("s_trc")
        s_gate = sem("s_gate")
        s_silu = sem("s_silu")
        s_hf = sem("s_hf")
        s_hidhi = sem("s_hidhi")
        s_hid = sem("s_hid")
        s_ev = sem("s_ev")
        s_alrT = sem("s_alrT")
        s_alrTc = sem("s_alrTc")
        s_xa = sem("s_xa")
        s_xs = sem("s_xs")
        s_la = sem("s_la")
        s_bd = sem("s_bd")
        s_eq = sem("s_eq")
        s_qd = sem("s_qd")
        s_ke = sem("s_ke")
        s_kn = sem("s_kn")
        s_am = sem("s_am")
        s_att = sem("s_att")
        s_go = sem("s_go")
        s_gsq = sem("s_gsq")
        s_gss = sem("s_gss")
        s_grs = sem("s_grs")
        s_mf = sem("s_mf")
        s_mhi = sem("s_mhi")
        s_mix = sem("s_mix")
        s_nsq = sem("s_nsq")
        s_nss = sem("s_nss")
        s_nrs = sem("s_nrs")
        s_qn = sem("s_qn")
        s_rot = sem("s_rot")
        s_rope = sem("s_rope")
        s_svT = sem("s_svT")
        s_sv = sem("s_sv")
        s_sc = sem("s_sc")
        s_mx = sem("s_mx")
        s_ex = sem("s_ex")
        s_wt = sem("s_wt")
        s_tp = sem("s_tp")
        s_tpc = sem("s_tpc")
        s_pv = sem("s_pv")
        s_osq = sem("s_osq")
        s_oss = sem("s_oss")
        s_ors = sem("s_ors")
        s_out = sem("s_out")

        block = ctx.enter_context(nc.Block())

        @block.sync
        def _(sp):
            unit = Count()

            def load(dst_slot, src, shape):
                sp.wait_ge(s_lo, unit.at(1))
                sp.dma_start(raw[:, dst_slot, :].rearrange(shape[0], **shape[1]), src).then_inc(s_raw[dst_slot], 16)
                unit.n += 1

            def rows(w, layer, r0, c0):
                return w[layer, bass.ds(r0 * P, UK * P), bass.ds(c0, G)].rearrange("(k p) n -> p k n", p=P)

            kn_shape = ("p (k n) -> p k n", dict(k=UK))

            sp.dma_start(xtok, x.rearrange("b (t p) c -> p (b t) c", p=P)).then_inc(s_x, 16)
            for l in range(DEPTH):
                at = l * R_ALL
                for r, src, n in ((R_MIX, norm_mix_g[l].rearrange("(j p) -> j p", p=P), KT),
                                  (R_FFN, norm_ffn_g[l].rearrange("(j p) -> j p", p=P), KT),
                                  (R_PLE, norm_ple_g[l].rearrange("(j p) -> j p", p=P), KT),
                                  (R_BAL, gla_b_alpha[l].rearrange("(j p) -> j p", p=P), GLA_H),
                                  (R_GLA, gla_norm_g[l].rearrange("(j p) -> j p", p=P), DV // P),
                                  (R_SUB, diff_subln_g[l:l + 1, :], 1)):
                    sp.dma_start(prm_rows[at + r:at + r + n, :], src).then_inc(s_small, 16)
                for r, src in ((R_DQ, diff_q_norm_g), (R_DK, diff_k_norm_g), (R_SQ, swa_q_norm_g),
                               (R_SK, swa_k_norm_g)):
                    for c in range(2):
                        sp.dma_start(prm_rows[at + r:at + r + 1, c * HD:(c + 1) * HD],
                                     src[l:l + 1, :]).then_inc(s_small, 16)
            sp.dma_start(cst[:, :], consts).then_inc(s_small, 16)
            sp.dma_start(pos_i[:, :], positions.to_broadcast([P, S])).then_inc(s_small, 16)
            sp.dma_start(sinks[:, :, :].rearrange("p l h -> p (l h)"),
                         swa_sinks.rearrange("(a l) h -> a (l h)", a=1).to_broadcast([P, DEPTH * SWA_H])
                         ).then_inc(s_small, 16)
            for n, src in enumerate((diff_lambda_q1, diff_lambda_k1, diff_lambda_q2, diff_lambda_k2)):
                sp.dma_start(lamv[:, n, :, :].rearrange("p l h -> p (l h)"),
                             src.rearrange("(a l) h -> a (l h)", a=1).to_broadcast([P, DEPTH * HD])
                             ).then_inc(s_small, 16)

            with turns(sp, DEPTH, [(unit, UNITS_PER_LAYER)], s_began) as layer:
                sp.wait_ge(s_hnew, layer * 24 + 1)
                sp.dma_start(walr_raw[:, :, :], w_in[layer, :, C_ALR:C_ALR + RANK].rearrange("(k p) n -> p k n", p=P)
                             ).then_inc(s_lay[0], 16)
                sp.dma_start(wal[:, :], gla_w_alpha[layer, :, :]).then_inc(s_lay[1], 16)
                for k in range(4):
                    load(k, rows(w_in, layer, k * UK, C_SKV), kn_shape)
                with turns(sp, 12, [(unit, 4)], s_began) as i:
                    for k in range(4):
                        load(k, rows(w_in, layer, k * UK, i * G + C_GQ), kn_shape)
                with turns(sp, 8, [(unit, 4)], s_began) as i:
                    for k in range(4):
                        load(k, rows(w_in, layer, k * UK, i * G + C_DQ), kn_shape)
                for r in range(2):
                    with turns(sp, 4, [(unit, 4)], s_began) as i:
                        for g in range(2):
                            for k in range(2):
                                load(2 * g + k, rows(w_out, layer, r * 8 + k * UK, i * 2 * G + g * G), kn_shape)
                done = 0
                for n in ROUNDS:
                    with turns(sp, n // 2, [(unit, 8)], s_began) as i:
                        for c0 in (0, D_FF):
                            for k in range(4):
                                load(k, rows(w_ffn_in, layer, k * UK, i * G + (c0 + done * P)), kn_shape)
                    if n == 16:
                        with turns(sp, 8, [(unit, 4)], s_began) as i:
                            for k in range(4):
                                load(k, rows(w_ffn_out, layer, done + k * UK, i * G), kn_shape)
                    else:
                        with turns(sp, 2, [(unit, 12)], s_began) as i:
                            for g in range(4):
                                for k in range(3):
                                    load((3 * g + k) % RING, rows(w_ffn_out, layer, done + k * UK, i * 4 * G + g * G),
                                         kn_shape)
                    done += n
                sp.wait_ge(s_hnew, layer * 24 + 16)
                sp.dma_start(ptok[:, :, :], p[layer, 0, :, :].rearrange("(t p) c -> p t c", p=P)).then_inc(s_lay[2], 16)
                for k in range(4):
                    load(k, w_ple_proj[layer, :, k * 2 * G:(k + 1) * 2 * G].rearrange("(k p) n -> p k n", p=P),
                         ("p (k n) -> p k n", dict(k=2)))
                with turns(sp, 8, [(unit, 4)], s_began) as i:
                    for k in range(4):
                        load(k, rows(w_ple_gate, layer, k * UK, i * G), kn_shape)
            for k in range(AHEAD):
                sp.wait_ge(s_lo, unit.at(1 + k))
                sp.sem_inc(s_raw[k], 16)
            for g in range(8):
                sp.wait_ge(s_trc, 8 + g + 1)
                sp.dma_start(out.rearrange("b (t p) c -> p (b t) c", p=P)[:, :, g * G:(g + 1) * G],
                             xtok[:, :, g * G:(g + 1) * G]).then_inc(s_out, 16)
            sp.wait_ge(s_out, 8 * 16)

        n_small = 16 * (DEPTH * (6 + 8) + 7)

        @block.gpsimd
        def _(pool):
            norm = Count()
            step = Count()

            def squares():
                with turns(pool, 8, [(step, 4)], s_began) as g:
                    pool.wait_ge(s_hnew, norm.at() * 8 + g + 1)
                    for j in range(2):
                        hv = h[:, bass.ds(2 * g + j, 1), :].rearrange("p j t -> p (j t)")
                        nc.gpsimd.tensor_tensor(sqt[:, :], hv, hv, ALU.mult).then_inc(s_sqt, 1)
                        pool.wait_ge(s_sqt, step.at(1))
                        nc.gpsimd.tensor_tensor(ssq[:, :], ssq[:, :], sqt[:, :], ALU.add).then_inc(s_sqt, 1)
                        step.n += 2
                        pool.wait_ge(s_sqt, step.at())
                pool.sem_inc(s_ssq, 1)
                norm.n += 1

            nc.gpsimd.memset(ssq[:, :], 0.0).then_inc(s_sqt, 1)
            step.n += 1
            pool.wait_ge(s_sqt, 1)
            squares()
            with turns(pool, DEPTH, [(norm, 3), (step, 3 * 33)], s_began) as layer:
                for n in range(3):
                    pool.wait_ge(s_nmm, norm.at())
                    pool.sem_inc(s_began, 1)
                    nc.gpsimd.memset(ssq[:, :], 0.0).then_inc(s_sqt, 1)
                    step.n += 1
                    pool.wait_ge(s_sqt, step.at())
                    squares()

        @block.scalar
        def _(act):
            unit, group, norm, hn, chain = Count(), Count(), Count(), Count(), Count()
            silu, hidc = Count(), Count()

            def link(ins):
                chain.n += 1
                ins.then_inc(s_act, 1)
                act.wait_ge(s_act, chain.at())

            def split(slot):
                act.wait_ge(s_used, unit.at(1))
                act.wait_ge(s_raw[slot], raw_landed(slot))
                nc.scalar.activation(wsp[:, slot, :, 0, :], raw[:, slot, :].rearrange("p (k n) -> p k n", k=UK),
                                     ACT.Copy).then_inc(s_hi, 1)
                unit.n += 1

            def raw_landed(slot):
                assert unit.n % RING == slot
                value = (unit.n // RING + 1) * 16
                for reg, per in unit.terms:
                    assert per % RING == 0
                    value = reg * (per // RING * 16) + value
                return value

            def units(n):
                for _ in range(n):
                    split(unit.n % RING)

            def take_cross(scale=None, done=None):
                par = group.n % 2
                act.wait_ge(*(done or (s_used, unit.at(1))))
                if scale is None:
                    nc.scalar.activation(cross[:, par, :].rearrange("p (a t) -> p a t", a=2),
                                         pd[:, par, :, S:2 * S], ACT.Copy).then_inc(s_cross, 1)
                else:
                    for tt in range(TT):
                        ins = nc.scalar.activation(cross[:, par, tt * S:(tt + 1) * S], pd[:, par, tt, S:2 * S],
                                                   ACT.Copy, scale=rstdC[:, tt:tt + 1])
                    ins.then_inc(s_cross, 1)
                group.n += 1

            def make_u(g, gain, wait):
                act.wait_ge(s_hnew, wait)
                for j in range(2):
                    ins = nc.scalar.activation(u[:, bass.ds(2 * g + j, 1), 0, :], h[:, bass.ds(2 * g + j, 1), :],
                                               ACT.Copy, scale=gain(2 * g + j))
                ins.then_inc(s_uhi, 1)

            def rms(token_major):
                norm.n += 1
                act.wait_ge(s_nmm, norm.at())
                link(nc.scalar.activation(rstdB[:, :], pm[:, 0, 0:S], ACT.Ln, scale=1.0 / D, bias=epst[:, 0:1]))
                if token_major:
                    link(nc.scalar.activation(rstdC[:, :], pm[:, 0, S:S + TT], ACT.Ln, scale=1.0 / D,
                                              bias=epst[:, 0:1]))
                    link(nc.scalar.activation(rstdC[:, :], rstdC[:, :], ACT.Exp, scale=-0.5))
                nc.scalar.activation(rstdB[:, :], rstdB[:, :], ACT.Exp, scale=-0.5).then_inc(s_rstd, 1)
                act.wait_ge(s_rstd, norm.at())

            act.wait_ge(s_small, n_small)
            act.wait_ge(s_init, 1)
            nc.scalar.activation(sinB[:, :], sinB[:, :], ACT.Sin)
            nc.scalar.activation(cosB[:, :], cosB[:, :], ACT.Sin).then_inc(s_inita, 1)
            nc.scalar.activation(lam[:, 0:2, :], lam[:, 0:2, :], ACT.Exp).then_inc(s_inita, 1)
            act.wait_ge(s_init, 2)
            units(AHEAD)

            with turns(act, DEPTH, [(unit, UNITS_PER_LAYER), (group, GROUPS_PER_LAYER), (norm, 3), (hn, 24),
                                    (chain, ACT_LINKS), (silu, 34), (hidc, 22)], s_began) as layer:
                lp = layer * R_ALL

                def column(r):
                    return prm[:, bass.ds(lp + r, 1)]

                act.wait_ge(s_used, unit.at(1))
                with turns(act, 8, [(hn, 1)], s_began) as g:
                    hn.n += 1
                    make_u(g, lambda j: prm[:, bass.ds(j + (lp + R_MIX), 1)], hn.at())
                act.wait_ge(s_lay[0], layer * 16 + 16)
                nc.scalar.activation(walr[:, :, 0, :], walr_raw[:, :, :], ACT.Copy).then_inc(s_walr, 1)
                units(4)
                rms(True)
                take_cross()
                act.wait_ge(s_half, layer * 5 + 1)
                for tt in range(TT):
                    ins = nc.scalar.activation(cross[:, 1, tt * RANK:(tt + 1) * RANK], pd[:, 1, tt, RANK:2 * RANK],
                                               ACT.Copy, scale=rstdC[:, tt:tt + 1])
                ins.then_inc(s_cross, 1)
                group.n += 1

                with turns(act, 2, [(unit, 8), (group, 2)], s_began) as i:
                    for g in range(2):
                        units(4)
                        take_cross()
                with turns(act, 2, [(unit, 8), (group, 2)], s_began) as i:
                    for g in range(2):
                        units(4)
                        take_cross(rstdC)
                with turns(act, 2, [(unit, 8), (group, 2), (silu, 2)], s_began) as i:
                    for g in range(2):
                        units(4)
                        take_cross()
                        silu.n += 1
                        act.wait_ge(s_gate, silu.at())
                        gv = sgate[:, bass.ds(i * 4 + 2 * g, 2), :]
                        nc.scalar.activation(gv, gv, ACT.Silu).then_inc(s_silu, 1)
                for seg in range(2):
                    for g in range(2):
                        units(4)
                        take_cross()
                for g in range(2):
                    units(4)
                    take_cross(rstdC)
                for g in range(2):
                    units(4)
                    take_cross()

                act.wait_ge(s_alrT, layer + 1)
                nc.scalar.activation(alrT[:, :], pm[0:RANK, 0, 0:S], ACT.Copy).then_inc(s_alrTc, 1)
                act.wait_ge(s_xa, layer + 1)
                for hh in range(GLA_H):
                    ins = nc.scalar.activation(gt[:, hh, :], pm[:, 1 + hh // 2, hh % 2 * S:(hh % 2 + 1) * S],
                                               ACT.Identity, bias=column(R_BAL + hh))
                link(ins)
                link(nc.scalar.activation(bc[:, :, 1:], gt[:, :, :], ACT.Abs))
                link(nc.scalar.activation(bc[:, :, 1:], bc[:, :, 1:], ACT.Exp, scale=-1.0))
                nc.scalar.activation(bc[:, :, 1:], bc[:, :, 1:], ACT.Ln, bias=epst[:, 1:2]).then_inc(s_xs, 1)
                act.wait_ge(s_bd, layer + 1)
                nc.scalar.activation(gt[:, :, :], gt[:, :, :], ACT.Exp).then_inc(s_eq, 1)

                def key_decays(hh):
                    for n in range(NBLK):
                        idx = hh * NBLK + n
                        if idx >= 8:
                            act.wait_ge(s_am, layer * 64 + (idx - 7))
                        at, width = (P, BLK * (n + 1)) if n < 8 else (0, BLK * (n + 1))
                        nc.scalar.activation(kn[:, n % 8, at:at + width], bc[:, hh, 1:1 + width], ACT.Exp,
                                             bias=bc[:, hh, BLK * n:BLK * n + 1], scale=-1.0).then_inc(s_ke, 1)

                def gla_norm(hh):
                    act.wait_ge(s_go, layer * GLA_H + (hh + 1))
                    nc.scalar.activation(sqn(0), pm[:, 2 + hh % 2, :], ACT.Square).then_inc(s_gsq, 1)
                    act.wait_ge(s_gss, layer * GLA_H + (hh + 1))
                    link(nc.scalar.activation(lnt[:, 0:S], pm[:, hh % 2, 0:S], ACT.Ln, scale=1.0 / DV, bias=epst[:, 0:1]))
                    nc.scalar.activation(rsn[:, 0:S], lnt[:, 0:S], ACT.Exp, scale=-0.5).then_inc(s_grs, 1)

                def mixer_hi(tile, n, src, wait_for, value):
                    act.wait_ge(wait_for, value)
                    nc.scalar.activation(hid[:, tile:tile + n, 0, :], src, ACT.Copy).then_inc(s_mhi, 1)

                def sqn(b):
                    return pe_buf[:, b, :, :].rearrange("p a t -> p (a t)")

                for hh in range(GLA_H):
                    key_decays(hh)
                    gla_norm(hh)
                    mixer_hi(2 * hh, 2, hf[:, :].rearrange("p (a t) -> p a t", a=2), s_mf, layer * 8 + (hh + 1))

                act.wait_ge(s_ev, layer * EV + EV)
                for n, item in enumerate(items(dq, dk, sq, sk)):
                    w = item.shape[-1]
                    nc.scalar.activation(sqn(n % 2)[:, 0:w], item, ACT.Square).then_inc(s_nsq, 1)
                    act.wait_ge(s_nss, layer * 7 + (n + 1))
                    link(nc.scalar.activation(lnt[:, 0:w], pm[:, 0, 0:w], ACT.Ln, bias=epst[:, 0:1]))
                    nc.scalar.activation(rsn[:, 0:w], lnt[:, 0:w], ACT.Exp, scale=-0.5).then_inc(s_nrs, 1)
                    act.wait_ge(s_qn, layer * 7 + (n + 1))

                def exps(z, j):
                    act.wait_ge(s_mx, layer * 16 + (z + 1))
                    diff, k0 = z < 8, 0 if z < 8 or j == 0 else CHUNK
                    kw = (j + 1) * P
                    for c in range(2):
                        ins = nc.scalar.activation(pe_buf[:, z % 2, c, k0:kw], pm[:, c, k0:kw], ACT.Exp,
                                                   scale=SCALE, bias=st[:, z % 2, c:c + 1],
                                                   accum_out=st[:, z % 2, 2 + c:3 + c])
                    if not diff:
                        ins = nc.scalar.activation(st[:, z % 2, 4:6], st[:, z % 2, 6:8], ACT.Exp)
                    ins.then_inc(s_ex, 1)

                def weights_out(z, j):
                    act.wait_ge(s_tp, layer * 16 + (z + 1))
                    if z < 8:
                        nc.scalar.activation(wT[:, z % 2, 0:j + 1, :],
                                             pm[:, 2, 0:(j + 1) * P].rearrange("p (a t) -> p a t", t=P),
                                             ACT.Copy).then_inc(s_tpc, 1)
                    else:
                        nc.scalar.activation(wT[:, z % 2, :, :].rearrange("p (e k) t -> p e k t", e=2)[:, :, 0:j + 1, :],
                                             pm[:, 2, :].rearrange("p (e k t) -> p e k t", e=2, k=2)[:, :, 0:j + 1, :],
                                             ACT.Copy).then_inc(s_tpc, 1)

                for z in range(16):
                    j = z % 2
                    exps(z, j)
                    weights_out(z, j)
                    if j == 1 and z < 8:
                        hh = z // 2
                        act.wait_ge(s_pv, layer * 8 + (hh + 1))
                        nc.scalar.activation(lnt[:, 0:S], pm[:, 3, 0:S], ACT.Square).then_inc(s_osq, 1)
                        act.wait_ge(s_oss, layer * DIFF_H + (hh + 1))
                        link(nc.scalar.activation(lnt[:, S:2 * S], pm[:, 2, 0:S], ACT.Ln, scale=1.0 / P, bias=epst[:, 0:1]))
                        nc.scalar.activation(rsn[:, 0:S], lnt[:, S:2 * S], ACT.Exp, scale=-0.5).then_inc(s_ors, 1)
                        mixer_hi(8 + hh, 1, hf[:, 0:S], s_mf, layer * 8 + (GLA_H + hh + 1))
                    elif j == 1:
                        t = (z - 8) // 2
                        mixer_hi(12 + t, 1, pm[:, 3, 0:S], s_pv, layer * 8 + (DIFF_H + t + 1))

                with turns(act, 4, [(unit, 4), (group, 2)], s_began) as i:
                    units(4)
                    group.n += 2
                with turns(act, 4, [(unit, 4), (group, 2), (hn, 2)], s_began) as i:
                    for g in range(2):
                        units(2)
                        group.n += 1
                        hn.n += 1
                        make_u(i * 2 + g, lambda j: prm[:, bass.ds(j + (lp + R_FFN), 1)], hn.at())

                def hidden_pair(i, first=False):
                    units(4)
                    if first:
                        rms(False)
                    take_cross()
                    silu.n += 1
                    act.wait_ge(s_gate, silu.at())
                    nc.scalar.activation(sg[:, :], ta[:, :], ACT.Silu).then_inc(s_silu, 1)
                    units(4)
                    take_cross()
                    hidc.n += 1
                    act.wait_ge(s_hf, hidc.at())
                    nc.scalar.activation(hid[:, bass.ds(i * 2, 2), 0, :], hf[:, :].rearrange("p (a t) -> p a t", a=2),
                                         ACT.Copy).then_inc(s_hidhi, 1)

                for r, n in enumerate(ROUNDS):
                    peeled = int(r == 0)
                    if peeled:
                        hidden_pair(0, first=True)
                    with turns(act, n // 2 - peeled, [(unit, 8), (group, 2), (silu, 1), (hidc, 1)], s_began) as i:
                        hidden_pair(i + peeled)
                    last = r == len(ROUNDS) - 1
                    per = 2 if n == 16 else 4
                    with turns(act, 8 // per, [(unit, n // 4 * per), (group, per)] + [(hn, per)] * last, s_began) as i:
                        for g in range(per):
                            units(n // UK)
                            group.n += 1
                            if last:
                                hn.n += 1
                                make_u(i * per + g, lambda j: prm[:, bass.ds(j + (lp + R_PLE), 1)], hn.at())

                act.wait_ge(s_p, layer + 1)
                nc.scalar.activation(pT[:, :, 0, :], pm[:, 1, :].rearrange("p (a t) -> p a t", a=2),
                                     ACT.Copy).then_inc(s_phi, 1)
                for g in range(8):
                    if g % 2 == 0:
                        units(1)
                    take_cross(done=(s_half, layer * 5 + (2 + g // 2)) if g % 2 == 0 else None)

                def ple_group(g, first=False):
                    units(4)
                    if first:
                        rms(False)
                    take_cross()
                    silu.n += 1
                    act.wait_ge(s_gate, silu.at())
                    nc.scalar.activation(sg[:, :], ta[:, :], ACT.Sigmoid).then_inc(s_silu, 1)

                ple_group(0, first=True)
                ple_group(1)
                with turns(act, 3, [(unit, 8), (group, 2), (silu, 2)], s_began) as i:
                    ple_group(i * 2 + 2)
                    ple_group(i * 2 + 3)

        @block.vector
        def _(dve):
            unit, group, norm, hn, chain = Count(), Count(), Count(), Count(), Count()
            silu, hidc, evc, crossed = Count(), Count(), Count(), Count()

            def link(ins):
                chain.n += 1
                ins.then_inc(s_dve, 1)
                dve.wait_ge(s_dve, chain.at())

            def split(slot):
                dve.wait_ge(s_hi, unit.at(1))
                nc.vector.tensor_tensor(wsp[:, slot, :, 1, :], raw[:, slot, :].rearrange("p (k n) -> p k n", k=UK),
                                        wsp[:, slot, :, 0, :].bitcast(F32), ALU.subtract).then_inc(s_lo, 1)
                unit.n += 1

            def units(n):
                for _ in range(n):
                    split(unit.n % RING)

            def halves(t):
                return t[:, :].rearrange("p (a t) -> p a t", a=2)

            def both(t):
                return t[:, :].unsqueeze(1).to_broadcast([P, 2, S])

            def main_plus_cross(dst):
                par = group.n % 2
                crossed.n += 1
                dve.wait_ge(s_cross, crossed.at())
                group.n += 1
                nc.vector.tensor_tensor(dst, pd[:, par, :, 0:S], halves_of(cross[:, par, :]), ALU.add
                                        ).then_inc(s_psfree, 1)
                dve.wait_ge(s_psfree, group.at(2))

            def halves_of(ap):
                return ap.rearrange("p (a t) -> p a t", a=2)

            def feature_major(dst):
                main_plus_cross(halves(ta))
                nc.vector.tensor_tensor(dst, halves(ta), both(rstdB), ALU.mult).then_inc(s_ev, 1)
                evc.n += 1
                dve.wait_ge(s_ev, evc.at())

            def token_major(dst):
                par = group.n % 2
                crossed.n += 1
                dve.wait_ge(s_cross, crossed.at())
                for tt in range(TT):
                    ins = nc.vector.scalar_tensor_tensor(dst(tt), pd[:, par, tt, 0:S], rstdC[:, tt:tt + 1],
                                                         cross[:, par, tt * S:(tt + 1) * S], ALU.mult, ALU.add)
                ins.then_inc(s_psfree, 1)
                group.n += 1
                evc.n += 1
                dve.wait_ge(s_psfree, group.at(2))
                dve.sem_inc(s_ev, 1)

            def add_to_h(g):
                par = group.n % 2
                dve.wait_ge(s_used, unit.at(1))
                hv = h[:, bass.ds(2 * g, 2), :]
                link(nc.vector.tensor_tensor(hv, pd[:, par, :, 0:S], hv, ALU.add))
                ins = nc.vector.tensor_tensor(hv, pd[:, par, :, S:2 * S], hv, ALU.add)
                ins.then_inc(s_psfree, 1)
                group.n += 1
                dve.wait_ge(s_psfree, group.at(2))

            def make_u(g, gain):
                hn.n += 1
                dve.wait_ge(s_uhi, hn.at())
                for j in range(2):
                    k = bass.ds(2 * g + j, 1)
                    ins = nc.vector.scalar_tensor_tensor(u[:, k, 1, :], h[:, k, :], gain(2 * g + j),
                                                         u[:, k, 0, :].bitcast(F32), ALU.mult, ALU.subtract)
                ins.then_inc(s_u, 1)

            dve.memset(ones[:, :], 1.0)
            dve.memset(epst[:, 0:1], EPS)
            dve.memset(epst[:, 1:2], 1.0)
            dve.memset(bc[:, :, 0:1], 0.0)
            dve.memset(pe_buf[:, :, :, :], 0.0)
            dve.wait_ge(s_small, n_small)
            link(nc.vector.tensor_copy(ta[:, 0:S], pos_i[:, :]))
            link(nc.vector.tensor_scalar(ta[:, 0:S], ta[:, 0:S], cst[:, K_INV:K_INV + 1], None, ALU.mult))
            for dst, turn, shift in ((sinB, 0.0, 0.0), (cosB, 0.25, 1.5707963267948966)):
                link(nc.vector.tensor_scalar(tb[:, 0:S], ta[:, 0:S], INV_2PI, turn, ALU.mult, ALU.add))
                link(nc.vector.tensor_scalar(tb[:, 0:S], tb[:, 0:S], MAGIC, None, ALU.add))
                link(nc.vector.tensor_scalar(tb[:, 0:S], tb[:, 0:S], MAGIC, None, ALU.subtract))
                link(nc.vector.scalar_tensor_tensor(hf[:, 0:S], tb[:, 0:S], -PI2_A, ta[:, 0:S], ALU.mult, ALU.add))
                link(nc.vector.scalar_tensor_tensor(hf[:, 0:S], tb[:, 0:S], -PI2_B, hf[:, 0:S], ALU.mult, ALU.add))
                link(nc.vector.scalar_tensor_tensor(hf[:, 0:S], tb[:, 0:S], -PI2_C, hf[:, 0:S], ALU.mult, ALU.add))
                link(nc.vector.tensor_scalar(hf[:, 0:S], hf[:, 0:S], shift, PI_LO, ALU.add, ALU.min))
                link(nc.vector.tensor_scalar(dst[:, :], hf[:, 0:S], -PI_LO, None, ALU.max))
            link(nc.vector.tensor_tensor(lamp[:, 0], lamv[:, 0], lamv[:, 1], ALU.mult))
            link(nc.vector.tensor_tensor(lamp[:, 1], lamv[:, 2], lamv[:, 3], ALU.mult))
            link(nc.vector.tensor_reduce(lam[:, 0:2, :], lamp[:, :, :, :], AX.X, ALU.add))
            dve.sem_inc(s_init, 1)
            dve.wait_ge(s_inita, 2)
            link(nc.vector.tensor_tensor(lam[:, 2, :], lam[:, 0, :], lam[:, 1, :], ALU.subtract))
            link(nc.vector.tensor_tensor(lam[:, 2, :], lam[:, 2, :], cst[:, K_LAM:K_LAM + 2], ALU.add))
            link(nc.vector.tensor_scalar(lam[:, 3, :], lam[:, 2, :], -1.0, None, ALU.mult))
            dve.wait_ge(s_tr, 1)
            link(nc.vector.tensor_copy(prm[:, 0:DEPTH * R_ALL], pm[:, 0, 0:DEPTH * R_ALL]))
            for l in range(DEPTH):
                at = l * R_ALL + R_SUB
                link(nc.vector.tensor_tensor(prm[:, at:at + 1], prm[:, at:at + 1],
                                             cst[:, K_ONE_LAM + l:K_ONE_LAM + l + 1], ALU.mult))
            dve.sem_inc(s_init, 1)
            for g in range(8):
                dve.wait_ge(s_tr, 2 + g)
                link(nc.vector.tensor_copy(h[:, 2 * g:2 * g + 2, :], halves_of(pm[:, g % 4, :])))
                dve.sem_inc(s_trc, 1)
                dve.sem_inc(s_hnew, 1)
            dve.sem_inc(s_lo, RING)
            dve.sem_inc(s_psfree, 2)
            units(AHEAD)

            with turns(dve, DEPTH, [(unit, UNITS_PER_LAYER), (group, GROUPS_PER_LAYER), (norm, 3), (hn, 24),
                                    (chain, DVE_LINKS), (silu, 34), (hidc, 22), (evc, EV), (crossed, CROSSED)], s_began) as layer:
                lp = layer * R_ALL

                def column(r):
                    return prm[:, bass.ds(lp + r, 1)]

                with turns(dve, 8, [(hn, 1)], s_began) as g:
                    make_u(g, lambda j: prm[:, bass.ds(j + (lp + R_MIX), 1)])
                nc.vector.memset(kn[:, :, :], 0.0)
                dve.wait_ge(s_walr, layer * 2 + 1)
                nc.vector.tensor_tensor(walr[:, :, 1, :], walr_raw[:, :, :], walr[:, :, 0, :].bitcast(F32),
                                        ALU.subtract).then_inc(s_walr, 1)
                units(4)
                norm.n += 1
                dve.wait_ge(s_rstd, norm.at())
                main_plus_cross(halves(ta))
                link(nc.vector.tensor_tensor(sk[:, :], ta[:, 0:S], rstdB[:, :], ALU.mult))
                nc.vector.tensor_tensor(svT[:, :], ta[:, S:2 * S], rstdB[:, :], ALU.mult).then_inc(s_ev, 1)
                evc.n += 1
                dve.wait_ge(s_ev, evc.at())
                crossed.n += 1
                dve.wait_ge(s_cross, crossed.at())
                for tt in range(TT):
                    ins = nc.vector.scalar_tensor_tensor(alr[:, tt, :], pd[:, 1, tt, 0:RANK], rstdC[:, tt:tt + 1],
                                                         cross[:, 1, tt * RANK:(tt + 1) * RANK], ALU.mult, ALU.add)
                ins.then_inc(s_psfree, 1)
                group.n += 1
                evc.n += 1
                dve.wait_ge(s_psfree, group.at(2))
                dve.sem_inc(s_ev, 1)

                for dst in (qg, kg):
                    for g in range(2):
                        units(4)
                        feature_major(dst[:, 2 * g:2 * g + 2, :])
                with turns(dve, 2, [(unit, 8), (group, 2), (evc, 2), (crossed, 2)], s_began) as i:
                    for g in range(2):
                        units(4)
                        token_major(lambda tt: vg[:, tt, bass.ds(i * 2 * G + g * G, G)])
                with turns(dve, 2, [(unit, 8), (group, 2), (silu, 2), (crossed, 2)], s_began) as i:
                    for g in range(2):
                        units(4)
                        main_plus_cross(halves(ta))
                        nc.vector.tensor_tensor(sgate[:, bass.ds(i * 4 + 2 * g, 2), :], halves(ta), both(rstdB), ALU.mult
                                                ).then_inc(s_gate, 1)
                        silu.n += 1
                        dve.wait_ge(s_gate, silu.at())
                for dst in (dq, dk):
                    for g in range(2):
                        units(4)
                        feature_major(dst[:, 2 * g:2 * g + 2, :])
                for g in range(2):
                    units(4)
                    token_major(lambda tt: dv[:, tt, g * G:(g + 1) * G])
                for g in range(2):
                    units(4)
                    feature_major(sq[:, 2 * g:2 * g + 2, :])

                dve.wait_ge(s_xs, layer + 1)
                link(nc.vector.scalar_tensor_tensor(gt[:, :, :], gt[:, :, :], 0.0, bc[:, :, 1:], ALU.min, ALU.subtract))
                link(nc.vector.tensor_scalar(gt[:, :, :], gt[:, :, :], 1.0 / GLA_TAU, None, ALU.mult))
                for hh in range(GLA_H):
                    ins = nc.vector.tensor_tensor_scan(bc[:, hh, 1:], ones[:, 0:1].to_broadcast([P, S]), gt[:, hh, :], 0.0, ALU.mult, ALU.add)
                ins.then_inc(s_la, 1)
                dve.wait_ge(s_la, layer + 1)
                for hh in range(GLA_H):
                    start = bc[:, hh, 0:S].rearrange("p (n b) -> p n b", b=BLK)[:, :, 0:1].to_broadcast([P, NBLK, BLK])
                    ins = nc.vector.tensor_tensor(gt[:, hh, :].rearrange("p (n b) -> p n b", b=BLK),
                                                  bc[:, hh, 1:].rearrange("p (n b) -> p n b", b=BLK), start, ALU.subtract)
                ins.then_inc(s_bd, 1)
                dve.wait_ge(s_eq, layer + 1)
                nc.vector.scalar_tensor_tensor(qg[:, :, :], qg[:, :, :], GLA_SCALE, gt[:, :, :], ALU.mult, ALU.mult
                                               ).then_inc(s_qd, 1)

                dve.wait_ge(s_silu, silu.at())
                for hh in range(GLA_H):
                    for n in range(NBLK):
                        idx = hh * NBLK + n
                        at, width = (P, BLK * (n + 1)) if n < 8 else (0, BLK * (n + 1))
                        dve.wait_ge(s_ke, layer * 64 + (idx + 1))
                        kv = kn[:, n % 8, at:at + width]
                        nc.vector.tensor_tensor(kv, kv, kg[:, hh, 0:width], ALU.mult).then_inc(s_kn, 1)
                    if hh:
                        dve.wait_ge(s_go, layer * GLA_H + hh)
                    dve.wait_ge(s_am, layer * 64 + (hh + 1) * NBLK)
                    nc.vector.tensor_tensor(att[:, :], pm[:, hh % 2, 0:3 * P], cst[:, K_TRI:K_TRI + 3 * P],
                                            ALU.mult).then_inc(s_att, 1)
                    dve.wait_ge(s_grs, layer * GLA_H + (hh + 1))
                    for b in range(2):
                        ins = nc.vector.scalar_tensor_tensor(ta[:, b * S:(b + 1) * S], pm[:, 2 + hh % 2, b * S:(b + 1) * S],
                                                             column(R_GLA + b), rsn[:, 0:S], ALU.mult, ALU.mult)
                    link(ins)
                    nc.vector.tensor_tensor(halves(hf), halves(ta), sgate[:, 2 * hh:2 * hh + 2, :], ALU.mult
                                            ).then_inc(s_mf, 1)
                    dve.wait_ge(s_mhi, layer * 12 + (hh + 1))
                    nc.vector.tensor_tensor(hid[:, 2 * hh:2 * hh + 2, 1, :], halves(hf),
                                            hid[:, 2 * hh:2 * hh + 2, 0, :].bitcast(F32), ALU.subtract).then_inc(s_mix, 1)
                    dve.wait_ge(s_mix, layer * 12 + (hh + 1))

                gains = (R_DQ, R_DQ, R_DK, R_DK, R_SQ, R_SQ, R_SK)
                for n, item in enumerate(items(dq, dk, sq, sk)):
                    w = item.shape[-1]
                    dve.wait_ge(s_nrs, layer * 7 + (n + 1))
                    nc.vector.scalar_tensor_tensor(item, item, column(gains[n]), rsn[:, 0:w], ALU.mult, ALU.mult
                                                   ).then_inc(s_qn, 1)
                    dve.wait_ge(s_qn, layer * 7 + (n + 1))
                    if n < 6:
                        v = halves_of(item)
                        link(nc.vector.tensor_tensor(halves(ta), v, both(cosB), ALU.mult))
                        dve.wait_ge(s_rot, layer * 7 + (n + 1))
                        link(nc.vector.tensor_tensor(halves(tb), halves_of(pm[:, 1, :]), both(sinB), ALU.mult))
                        nc.vector.tensor_tensor(item, ta[:, :], tb[:, :], ALU.add).then_inc(s_rope, 1)
                    else:
                        dve.wait_ge(s_rot, layer * 7 + (n + 1))
                        link(nc.vector.tensor_tensor(halves(ta), halves_of(pm[:, 1, :]), both(cosB), ALU.mult))
                        link(nc.vector.tensor_tensor(halves(tb), halves_of(pm[:, 2, :]), both(sinB), ALU.mult))
                        nc.vector.tensor_tensor(kd[:, :, :], halves(ta), halves(tb), ALU.add).then_inc(s_rope, 1)
                    dve.wait_ge(s_rope, layer * 7 + (n + 1))
                dve.wait_ge(s_svT, layer + 1)
                nc.vector.tensor_copy(sv[:, :, :].rearrange("p a c -> p (a c)"), pm[:, 3, 0:2 * P]).then_inc(s_sv, 1)

                for z in range(16):
                    j, zp = z % 2, z % 2
                    kw = (j + 1) * P
                    dve.wait_ge(s_sc, layer * 16 + (z + 1))
                    if z == 8:
                        dve.wait_ge(s_tp, layer * 16 + 8)
                        nc.vector.memset(pe_buf[:, 1, :, 0:CHUNK], 0.0)
                    if z < 8:
                        hh = z // 2
                        tail = pm[0:CHUNK, 0:2, kw - CHUNK:kw]
                        link(nc.vector.tensor_scalar(tail, tail, NEG, None, ALU.add))
                        link(nc.vector.tensor_reduce(st[:, zp, 8:10], pm[:, 0:2, 0:kw], AX.X, ALU.max))
                        nc.vector.tensor_scalar(st[:, zp, 0:2], st[:, zp, 8:10], -SCALE, None, ALU.mult).then_inc(s_mx, 1)
                        dve.wait_ge(s_ex, layer * 16 + (z + 1))
                        link(nc.vector.reciprocal(st[:, zp, 8:10], st[:, zp, 2:4]))
                        link(nc.vector.tensor_tensor(st[:, zp, 10:11], st[:, zp, 9:10], lam[:, 3, bass.ds(layer, 1)], ALU.mult))
                        link(nc.vector.tensor_scalar(ta[:, 0:kw], pe_buf[:, zp, 1, 0:kw], st[:, zp, 10:11], None, ALU.mult))
                        nc.vector.scalar_tensor_tensor(pe_buf[:, zp, 0, 0:kw], pe_buf[:, zp, 0, 0:kw], st[:, zp, 8:9],
                                                       ta[:, 0:kw], ALU.mult, ALU.add).then_inc(s_wt, 1)
                        dve.wait_ge(s_wt, layer * 16 + (z + 1))
                        if j == 1:
                            dve.wait_ge(s_ors, layer * DIFF_H + (hh + 1))
                            nc.vector.scalar_tensor_tensor(hf[:, 0:S], pm[:, 3, 0:S], column(R_SUB), rsn[:, 0:S],
                                                           ALU.mult, ALU.mult).then_inc(s_mf, 1)
                            dve.wait_ge(s_mhi, layer * 12 + (GLA_H + hh + 1))
                            nc.vector.tensor_tensor(hid[:, 8 + hh, 1, :], hf[:, 0:S], hid[:, 8 + hh, 0, :].bitcast(F32),
                                                    ALU.subtract).then_inc(s_mix, 1)
                            dve.wait_ge(s_mix, layer * 12 + (GLA_H + hh + 1))
                    else:
                        t = (z - 8) // 2
                        k0 = CHUNK * j
                        tail = pm[0:CHUNK, 0:2, kw - CHUNK:kw]
                        link(nc.vector.tensor_scalar(tail, tail, NEG, None, ALU.add))
                        if j == 1:
                            head = pm[CHUNK:P, 0:2, k0:k0 + CHUNK]
                            link(nc.vector.tensor_scalar(head, head, NEG, None, ALU.add))
                        link(nc.vector.tensor_reduce(st[:, zp, 8:10], pm[:, 0:2, k0:kw], AX.X, ALU.max))
                        sink = sinks[:, bass.ds(layer, 1), 2 * t:2 * t + 2].rearrange("p a b -> p (a b)")
                        link(nc.vector.scalar_tensor_tensor(st[:, zp, 10:12], st[:, zp, 8:10], SCALE, sink, ALU.mult, ALU.max))
                        link(nc.vector.tensor_tensor(st[:, zp, 6:8], sink, st[:, zp, 10:12], ALU.subtract))
                        nc.vector.tensor_scalar(st[:, zp, 0:2], st[:, zp, 10:12], -1.0, None, ALU.mult).then_inc(s_mx, 1)
                        dve.wait_ge(s_ex, layer * 16 + (z + 1))
                        link(nc.vector.tensor_tensor(st[:, zp, 8:10], st[:, zp, 2:4], st[:, zp, 4:6], ALU.add))
                        link(nc.vector.reciprocal(st[:, zp, 10:12], st[:, zp, 8:10]))
                        for e in range(2):
                            pv = pe_buf[:, zp, e, k0:kw]
                            ins = nc.vector.tensor_scalar(pv, pv, st[:, zp, 10 + e:11 + e], None, ALU.mult)
                        ins.then_inc(s_wt, 1)
                        if j == 1:
                            dve.wait_ge(s_mhi, layer * 12 + (8 + t + 1))
                            nc.vector.tensor_tensor(hid[:, 12 + t, 1, :], pm[:, 3, 0:S], hid[:, 12 + t, 0, :].bitcast(F32),
                                                    ALU.subtract).then_inc(s_mix, 1)

                with turns(dve, 4, [(unit, 4), (group, 2), (chain, 2)], s_began) as i:
                    for g in range(2):
                        units(2)
                        add_to_h(i * 2 + g)
                with turns(dve, 4, [(unit, 4), (group, 2), (chain, 2), (hn, 2)], s_began) as i:
                    for g in range(2):
                        units(2)
                        add_to_h(i * 2 + g)
                        dve.sem_inc(s_hnew, 1)
                        make_u(i * 2 + g, lambda j: prm[:, bass.ds(j + (lp + R_FFN), 1)])

                norm.n += 1
                for r, n in enumerate(ROUNDS):
                    with turns(dve, n // 2, [(unit, 8), (group, 2), (silu, 1), (hidc, 1), (chain, 2), (crossed, 2)], s_began) as i:
                        units(4)
                        dve.wait_ge(s_rstd, norm.at())
                        main_plus_cross(halves(tb))
                        nc.vector.tensor_tensor(halves(ta), halves(tb), both(rstdB), ALU.mult).then_inc(s_gate, 1)
                        silu.n += 1
                        dve.wait_ge(s_silu, silu.at())
                        link(nc.vector.tensor_tensor(halves(sg), halves(sg), both(rstdB), ALU.mult))
                        units(4)
                        main_plus_cross(halves(tb))
                        nc.vector.tensor_tensor(hf[:, :], tb[:, :], sg[:, :], ALU.mult).then_inc(s_hf, 1)
                        hidc.n += 1
                        dve.wait_ge(s_hidhi, hidc.at())
                        hv = bass.ds(i * 2, 2)
                        link(nc.vector.tensor_tensor(hid[:, hv, 1, :], halves(hf), hid[:, hv, 0, :].bitcast(F32),
                                                     ALU.subtract))
                        dve.sem_inc(s_hid, 1)
                    last = r == len(ROUNDS) - 1
                    per = 2 if n == 16 else 4
                    with turns(dve, 8 // per, [(unit, n // 4 * per), (group, per), (chain, per)] + [(hn, per)] * last, s_began) as i:
                        for g in range(per):
                            units(n // UK)
                            add_to_h(i * per + g)
                            if last:
                                dve.sem_inc(s_hnew, 1)
                                make_u(i * per + g, lambda j: prm[:, bass.ds(j + (lp + R_PLE), 1)])

                dve.wait_ge(s_phi, layer + 1)
                nc.vector.tensor_tensor(pT[:, :, 1, :], halves_of(pm[:, 1, :]), pT[:, :, 0, :].bitcast(F32),
                                        ALU.subtract).then_inc(s_plo, 1)
                for g in range(8):
                    if g % 2 == 0:
                        units(1)
                    main_plus_cross(pleT[:, 2 * g:2 * g + 2, :])
                norm.n += 1
                with turns(dve, 4, [(unit, 8), (group, 2), (silu, 2), (chain, 4), (crossed, 2)], s_began) as i:
                    for g in range(2):
                        units(4)
                        dve.wait_ge(s_rstd, norm.at())
                        main_plus_cross(halves(tb))
                        nc.vector.tensor_tensor(halves(ta), halves(tb), both(rstdB), ALU.mult).then_inc(s_gate, 1)
                        silu.n += 1
                        dve.wait_ge(s_silu, silu.at())
                        gv = bass.ds(i * 4 + 2 * g, 2)
                        link(nc.vector.tensor_tensor(halves(tb), halves(sg), pleT[:, gv, :], ALU.mult))
                        link(nc.vector.tensor_tensor(h[:, gv, :], h[:, gv, :], halves(tb), ALU.add))
                        dve.sem_inc(s_hnew, 1)

            for g in range(8):
                dve.wait_ge(s_tr, 10 + g)
                nc.vector.tensor_copy(xtok[:, :, g * G:(g + 1) * G], halves_of(pm[:, g % 4, :])).then_inc(s_trc, 1)

        @block.tensor
        def _(pe):
            unit, group, norm, hn, hidc = Count(), Count(), Count(), Count(), Count()

            def mm(o, a, b, start, stop):
                return nc.tensor.matmul(o, a, b, start=start, stop=stop, skip_group_check=True)

            def stationary_weights(slot, k, x_pair, par, start, stop, cols=0, width=2):
                for n in range(2):
                    c = slice(cols + n * P, cols + (n + 1) * P)
                    mm(pd[:, par, n, :], wview(slot, k, 0, c, width), x_pair, start, False)
                    ins = mm(pd[:, par, n, 0:S], wview(slot, k, 1, c, width), x_pair[:, 0:S], False, stop)
                return ins

            def wview(slot, k, part, c, width):
                if width == 2:
                    return wsp[:, slot, k, part, c]
                col = c.start
                return wsp[:, slot, 2 * k + col // G, part, col % G:col % G + P]

            def moving_weights(slot, k, x_tile, par, start, stop):
                for tt in range(TT):
                    t = slice(tt * P, (tt + 1) * P)
                    mm(pd[:, par, tt, :], x_tile[:, 0, t], wsp[:, slot, k, :, :].rearrange("p a n -> p (a n)"), start, False)
                    ins = mm(pd[:, par, tt, 0:G], x_tile[:, 1, t], wsp[:, slot, k, 0, :], False, stop)
                return ins

            def dense(operand, n_units, tokens=False, ready=None):
                par = group.n % 2
                pe.wait_ge(s_psfree, group.at(1))
                for q in range(n_units):
                    slot = unit.n % RING
                    if ready:
                        ready(q)
                    pe.wait_ge(s_lo, unit.at(1 + RING))
                    for k in range(UK):
                        kk = q * UK + k
                        first, last = kk == 0, kk == n_units * UK - 1
                        if tokens:
                            ins = moving_weights(slot, k, operand[:, kk], par, first, last)
                        else:
                            ins = stationary_weights(slot, k, operand[:, kk, :, :].rearrange("p a t -> p (a t)"), par,
                                                     first, last)
                        if k == UK - 1:
                            ins.then_inc(s_used, 1)
                    unit.n += 1
                group.n += 1

            def u_ready(q):
                pe.wait_ge(s_u, hn.at(2 * (q + 1)))

            def norm_sums(token_major):
                norm.n += 1
                pe.wait_ge(s_ssq, norm.at())
                ins = mm(pm[:, 0, 0:S], ones[:, :], ssq[:, :], True, True)
                if token_major:
                    for tt in range(TT):
                        ins = mm(pm[:, 0, S + tt:S + tt + 1], ssq[:, tt * P:(tt + 1) * P], ones[:, 0:1], True, True)
                ins.then_inc(s_nmm, 1)

            pe.sem_inc(s_used, RING)
            pe.wait_ge(s_small, n_small)
            rows_n = DEPTH * R_ALL
            nc.tensor.transpose(pm[:, 0, 0:rows_n], prm_rows[0:rows_n, :], ident[0:rows_n, 0:rows_n]).then_inc(s_tr, 1)
            pe.wait_ge(s_x, 16)
            pe.wait_ge(s_init, 2)
            for g in range(8):
                if g >= 4:
                    pe.wait_ge(s_trc, g - 3)
                for j in range(2):
                    for tt in range(TT):
                        c = (2 * g + j) * P
                        ins = nc.tensor.transpose(pm[:, g % 4, j * S + tt * P:j * S + (tt + 1) * P], xtok[:, tt, c:c + P],
                                                  ident)
                ins.then_inc(s_tr, 1)
            pe.wait_ge(s_trc, 8)

            with turns(pe, DEPTH, [(unit, UNITS_PER_LAYER), (group, GROUPS_PER_LAYER), (norm, 3), (hn, 24),
                                   (hidc, 22)], s_began) as layer:
                dense(u, 4, ready=u_ready)
                hn.n += 8
                norm_sums(True)
                pe.wait_ge(s_walr, layer * 2 + 2)
                pe.wait_ge(s_psfree, group.at(1))
                for tt in range(TT):
                    t = slice(tt * P, (tt + 1) * P)
                    for k in range(KT):
                        wv = walr[:, k, :, :].rearrange("p a n -> p (a n)")
                        mm(pd[:, 1, tt, 0:2 * RANK], u[:, k, 0, t], wv, k == 0, False)
                        ins = mm(pd[:, 1, tt, 0:RANK], u[:, k, 1, t], wv[:, 0:RANK], False, k == KT - 1)
                ins.then_inc(s_half, 1)
                group.n += 1
                with turns(pe, 2, [(unit, 8), (group, 2)], s_began):
                    dense(u, 4)
                    dense(u, 4)
                with turns(pe, 2, [(unit, 8), (group, 2)], s_began):
                    dense(u, 4, tokens=True)
                    dense(u, 4, tokens=True)
                with turns(pe, 4, [(unit, 8), (group, 2)], s_began):
                    dense(u, 4)
                    dense(u, 4)
                dense(u, 4, tokens=True)
                dense(u, 4, tokens=True)
                dense(u, 4)
                dense(u, 4)

                pe.wait_ge(s_ev, layer * EV + 2)
                for tt in range(TT):
                    ins = nc.tensor.transpose(pm[0:RANK, 0, tt * P:(tt + 1) * P], alr[:, tt, :], ident)
                ins.then_inc(s_alrT, 1)
                pe.wait_ge(s_alrTc, layer + 1)
                pe.wait_ge(s_lay[1], layer * 16 + 16)
                for hh in range(GLA_H):
                    ins = mm(pm[:, 1 + hh // 2, hh % 2 * S:(hh % 2 + 1) * S], wal[:, hh * DK:(hh + 1) * DK], alrT[:, :], True, True)
                ins.then_inc(s_xa, 1)

                pe.wait_ge(s_ev, layer * EV + EV)
                pe.wait_ge(s_qd, layer + 1)
                for hh in range(GLA_H):
                    b = hh % 2
                    for n in range(NBLK):
                        pe.wait_ge(s_kn, layer * 64 + (hh * NBLK + n + 1))
                        q = qg[:, hh, BLK * n:BLK * (n + 1)]
                        if n < 8:
                            ins = mm(pm[:, b, BLK * n:BLK * (n + 1)], kn[:, n, P:2 * P], q, True, True)
                        else:
                            mm(pm[:, b, BLK * n:BLK * (n + 1)], kn[:, n - 8, 0:P], q, True, True)
                            ins = mm(pm[:, b, S + BLK * (n - 8):S + BLK * (n - 7)], kn[:, n - 8, P:2 * P], q, True, True)
                        ins.then_inc(s_am, 1)
                    pe.wait_ge(s_att, layer * GLA_H + (hh + 1))
                    for vb in range(2):
                        c = hh * DV + vb * P
                        mm(pm[:, 2 + b, vb * S:(vb + 1) * S], vg[:, 0, c:c + P], att[:, 0:S], True, False)
                        ins = mm(pm[:, 2 + b, vb * S + P:(vb + 1) * S], vg[:, 1, c:c + P], att[:, S:S + P], False, True)
                    ins.then_inc(s_go, 1)
                    pe.wait_ge(s_gsq, layer * GLA_H + (hh + 1))
                    mm(pm[:, b, 0:S], ones[:, :], pe_buf[:, 0, 0, :], True, False)
                    mm(pm[:, b, 0:S], ones[:, :], pe_buf[:, 0, 1, :], False, True).then_inc(s_gss, 1)

                for n, item in enumerate(items(dq, dk, sq, sk)):
                    w = item.shape[-1]
                    pe.wait_ge(s_nsq, layer * 7 + (n + 1))
                    mm(pm[:, 0, 0:w], cst[:, K_BLK:K_BLK + P], pe_buf[:, n % 2, :, :].rearrange("p a t -> p (a t)")[:, 0:w],
                       True, True).then_inc(s_nss, 1)
                    pe.wait_ge(s_qn, layer * 7 + (n + 1))
                    if n < 6:
                        ins = mm(pm[:, 1, 0:w], cst[:, K_ROT:K_ROT + P], item, True, True)
                    else:
                        for g in range(2):
                            mm(pm[:, 1, g * S:(g + 1) * S], cst[:, K_SEL + g * P:K_SEL + (g + 1) * P], item, True, True)
                            ins = mm(pm[:, 2, g * S:(g + 1) * S], cst[:, K_RSEL + g * P:K_RSEL + (g + 1) * P], item, True, True)
                    ins.then_inc(s_rot, 1)
                for tt in range(TT):
                    ins = nc.tensor.transpose(pm[:, 3, tt * P:(tt + 1) * P], svT[:, tt * P:(tt + 1) * P], ident)
                ins.then_inc(s_svT, 1)

                pe.wait_ge(s_rope, layer * 7 + 7)
                pe.wait_ge(s_sv, layer + 1)
                for z in range(16):
                    j, zp = z % 2, z % 2
                    kw = (j + 1) * P
                    for e in range(2):
                        r = slice(e * HD, (e + 1) * HD)
                        if z < 8:
                            ins = mm(pm[:, e, 0:kw], dq[r, z // 2, j * P:(j + 1) * P], dk[r, z // 2, 0:kw], True, True)
                        else:
                            t = (z - 8) // 2
                            k0 = CHUNK * j
                            ins = mm(pm[:, e, k0:kw], sq[r, t, j * P:(j + 1) * P], kd[r, t // 2, k0:kw], True, True)
                    ins.then_inc(s_sc, 1)
                    pe.wait_ge(s_wt, layer * 16 + (z + 1))
                    for e in range(1 if z < 8 else 2):
                        for kt in range(j + 1):
                            c = (2 * e + kt) * P
                            ins = nc.tensor.transpose(pm[:, 2, c:c + P], pe_buf[:, zp, e, kt * P:(kt + 1) * P], ident)
                    ins.then_inc(s_tp, 1)
                    pe.wait_ge(s_tpc, layer * 16 + (z + 1))
                    if j == 0 and z > 0:
                        pe.wait_ge(s_mix, layer * 12 + (GLA_H + z // 2))
                    for e in range(1 if z < 8 else 2):
                        for kt in range(j + 1):
                            if z < 8:
                                hh = z // 2
                                ins = mm(pm[:, 3, j * P:(j + 1) * P], dv[:, kt, hh * P:(hh + 1) * P], wT[:, zp, kt, :],
                                         kt == 0, kt == j)
                            else:
                                g = (z - 8) // 4
                                ins = mm(pm[e * HD:(e + 1) * HD, 3, j * P:(j + 1) * P], sv[:, kt, g * HD:(g + 1) * HD],
                                         wT[:, zp, 2 * e + kt, :], kt == 0, kt == j)
                    if j == 1:
                        ins.then_inc(s_pv, 1)
                        if z < 8:
                            pe.wait_ge(s_osq, layer * DIFF_H + (z // 2 + 1))
                            mm(pm[:, 2, 0:S], ones[:, :], lnt[:, 0:S], True, True).then_inc(s_oss, 1)

                pe.wait_ge(s_mix, layer * 12 + 4)
                with turns(pe, 4, [(unit, 4), (group, 2)], s_began):
                    dense(hid, 2)
                    dense(hid, 2)
                pe.wait_ge(s_mix, layer * 12 + 12)
                with turns(pe, 4, [(unit, 4), (group, 2)], s_began):
                    dense(hid[:, 8:16], 2)
                    dense(hid[:, 8:16], 2)

                for r, n in enumerate(ROUNDS):
                    pairs = n // 2
                    if r == 0:
                        dense(u, 4, ready=u_ready)
                        hn.n += 8
                        norm_sums(False)
                        dense(u, 4)
                        pairs -= 1
                    with turns(pe, pairs, [(unit, 8), (group, 2)], s_began):
                        dense(u, 4)
                        dense(u, 4)

                    def hid_ready(q):
                        pe.wait_ge(s_hid, hidc.at(2 * (q + 1)))

                    per = 2 if n == 16 else 4
                    dense(hid, n // UK, ready=hid_ready)
                    for _ in range(per - 1):
                        dense(hid, n // UK)
                    with turns(pe, 8 // per - 1, [(unit, n // 4 * per), (group, per)], s_began):
                        for _ in range(per):
                            dense(hid, n // UK)
                    hidc.n += n // 2

                pe.wait_ge(s_lay[2], layer * 16 + 16)
                for j in range(2):
                    for tt in range(TT):
                        ins = nc.tensor.transpose(pm[:, 1, j * S + tt * P:j * S + (tt + 1) * P],
                                                  ptok[:, tt, j * P:(j + 1) * P], ident)
                ins.then_inc(s_p, 1)
                pe.wait_ge(s_plo, layer + 1)
                for g in range(8):
                    par = group.n % 2
                    pe.wait_ge(s_psfree, group.at(1))
                    if g % 2 == 0:
                        pe.wait_ge(s_lo, unit.at(1 + RING))
                    for k in range(2):
                        xp = pT[:, k, :, :].rearrange("p a t -> p (a t)")
                        ins = stationary_weights(unit.n % RING, k, xp, par, k == 0, k == 1, cols=g % 2 * G, width=4)
                    if g % 2 == 1:
                        ins.then_inc(s_used, 1)
                        unit.n += 1
                    else:
                        ins.then_inc(s_half, 1)
                    group.n += 1
                dense(u, 4, ready=u_ready)
                hn.n += 8
                norm_sums(False)
                dense(u, 4)
                with turns(pe, 3, [(unit, 8), (group, 2)], s_began):
                    dense(u, 4)
                    dense(u, 4)

            pe.wait_ge(s_hnew, 8 + 24 * DEPTH)
            for g in range(8):
                if g >= 4:
                    pe.wait_ge(s_trc, 8 + g - 3)
                for tt in range(TT):
                    for j in range(2):
                        ins = nc.tensor.transpose(pm[:, g % 4, tt * S + j * P:tt * S + (j + 1) * P],
                                                  h[:, 2 * g + j, tt * P:(tt + 1) * P], ident)
                ins.then_inc(s_tr, 1)


ACT_LINKS = 23
DVE_LINKS = 213


def items(dq, dk, sq, sk):
    def pair(t, n):
        return t[:, 2 * n:2 * n + 2, :].rearrange("p a t -> p (a t)")
    return [pair(dq, 0), pair(dq, 1), pair(dk, 0), pair(dk, 1), pair(sq, 0), pair(sq, 1), sk[:, :]]


INPUTS = ["x", "p", "positions", "norm_mix_g", "w_in", "gla_w_alpha", "gla_b_alpha", "gla_norm_g",
          "diff_q_norm_g", "diff_k_norm_g", "diff_lambda_q1", "diff_lambda_k1", "diff_lambda_q2",
          "diff_lambda_k2", "diff_subln_g", "swa_q_norm_g", "swa_k_norm_g", "swa_sinks", "w_out",
          "norm_ffn_g", "w_ffn_in", "w_ffn_out", "norm_ple_g", "w_ple_gate", "w_ple_proj"]


def constants():
    import math

    import numpy as np
    c = np.zeros((P, K_COLS), np.float32)
    c[:, K_ID:K_ID + P] = np.eye(P)
    rot = np.zeros((P, P), np.float32)
    for m in range(P):
        d = m % HD
        if d < HALF:
            rot[m + HALF, m] = -1.0
        else:
            rot[m - HALF, m] = 1.0
    c[:, K_ROT:K_ROT + P] = rot
    for g in range(SWA_KV):
        sel = np.zeros((P, P), np.float32)
        for m in range(P):
            sel[g * HD + m % HD, m] = 1.0
        c[:, K_SEL + g * P:K_SEL + (g + 1) * P] = sel
        c[:, K_RSEL + g * P:K_RSEL + (g + 1) * P] = rot @ sel
    head = np.arange(P) // HD
    c[:, K_BLK:K_BLK + P] = (head[:, None] == head[None, :]) / HD
    tri = np.arange(P)[:, None] <= np.arange(P)[None, :]
    c[:, K_TRI:K_TRI + 3 * P] = np.concatenate([tri, np.ones((P, P)), tri], axis=1)
    inv = np.float32(1.0) / np.float32(10000.0) ** (np.arange(0, HD, 2, dtype=np.float32) / np.float32(HD))
    c[:, K_INV] = inv.astype(np.float32)[np.arange(P) % HALF]
    for i in range(DEPTH):
        c[:, K_LAM + i] = 0.8 - 0.6 * math.exp(-0.3 * i)
        c[:, K_ONE_LAM + i] = 1.0 - (0.8 - 0.6 * math.exp(-0.3 * i))
    return c


def kernel(**inputs):
    import numpy as np

    import concourse.bacc as bacc
    from concourse.bass_utils import run_bass_kernel_spmd as run

    nc = bacc.Bacc("TRN2", target_bir_lowering=False, num_devices=1)
    arrays = {f"in_{n}": np.ascontiguousarray(inputs[n]) for n in INPUTS}
    arrays["in_consts"] = constants()
    args = [nc.dram_tensor(n, a.shape, mybir.dt.from_np(a.dtype), kind="ExternalInput").ap() for n, a in arrays.items()]
    out = nc.dram_tensor("out", (1, S, D), F32, kind="ExternalOutput").ap()
    build(nc, *args, out)
    return run(nc, [arrays], core_ids=[0]).results[0]["out"]
```

```python
from contextlib import ExitStack, contextmanager

import concourse.bass as bass
from concourse import mybir

F32 = mybir.dt.float32
F32R = mybir.dt.float32r
I32 = mybir.dt.int32
ALU = mybir.AluOpType
ACT = mybir.ActivationFunctionType
AX = mybir.AxisListType

P = 128
D = 2048
S = 256
DEPTH = 2
HD = 64
HALF = HD // 2
CHUNK = 64
EPS = 1e-6
NEG = -1e30

GLA_H, DK, DV, RANK, BLK = 4, 128, 256, 16, 16
GLA_TAU = 16.0
DIFF_H = 4
SWA_H, SWA_KV = 8, 2
N_IN = 5392
MIX = 2048
D_FF = 5632
PLE = 256

KT = D // P
TT = S // P
G = 256
UK = 4
NBLK = S // BLK
SCALE = HD ** -0.5
GLA_SCALE = DK ** -0.5

C_GQ = 0
C_GV = 2 * GLA_H * DK
C_GATE = C_GV + GLA_H * DV
C_ALR = 2 * GLA_H * DK + 2 * GLA_H * DV
C_DQ = C_ALR + RANK
C_SKV = N_IN - 2 * SWA_KV * HD
C_SQ = C_SKV - SWA_H * HD

ROUNDS = (16, 16, 12)
assert sum(ROUNDS) * P == D_FF

UNITS_WIN = 21 * 4
UNITS_PER_LAYER = UNITS_WIN + 2 * 8 * 2 + sum(ROUNDS) * 4 + sum(ROUNDS) // UK * 8 + 4 + 8 * 4
GROUPS_PER_LAYER = 22 + 16 + sum(ROUNDS) + 8 * len(ROUNDS) + 8 + 8
CROSSED = 22 + sum(ROUNDS) + 16
EV = 18
EV_RANK, EV_DV, EV_GQ, EV_GV = 2, 10, 12, 14
EV_ITEM = (1, 3, 4, 5, 6, 7, 8)
AHEAD = 3
RING = 4

K_ID, K_ROT, K_SEL, K_RSEL, K_BLK, K_TRI = 0, 128, 256, 512, 768, 896
K_INV, K_LAM, K_ONE_LAM = 1280, 1281, 1283
K_COLS = 1285

R_MIX, R_FFN, R_PLE, R_BAL, R_GLA, R_SUB, R_DQ, R_DK, R_SQ, R_SK = 0, 16, 32, 48, 52, 54, 55, 56, 57, 58
R_ALL = 59

INV_2PI = 0.15915494309189535
PI2_A, PI2_B = 6.28125, 0.0019350051879882812
PI2_C = 6.283185307179586 - PI2_A - PI2_B
MAGIC = 12582912.0
PI_LO = 3.1415925


def schedule():
    beside = {}

    def at(slot, step, i=0):
        beside.setdefault(slot, []).append((step, i))

    for slot, step in ((5, "rank"), (6, "logits"), (7, "log_decay"), (8, "decay_sums"), (9, "block_decay")):
        at(slot, step)
    for n, slots in enumerate(((5, 6, 7), (9, 10, 11), (12, 13, 14), (16, 17, 18), (20, 21, 22), (24, 25, 26), (28, 29, 30))):
        for slot, step in zip(slots, ("squares", "norm", "rope")):
            at(slot, step, n)
    at(8, "swa_k")
    at(9, "swa_v")
    for z in range(8):
        for n, step in enumerate(("scores", "transpose", "values")):
            at(15 + 3 * z + n, step, z)
    for hh in range(DIFF_H):
        for j in range(2):
            for n, step in enumerate(("scores", "transpose", "values")):
                at(39 + 7 * hh + 3 * j + n, step, 8 + 2 * hh + j)
        at(45 + 7 * hh, "diff_norm", hh)
    at(46, "queries")
    at(68, "gate")
    for i in range(4 * GLA_H):
        at(69 + i, "keys", i)
        at(70 + i, "blocks", i)
    for hh in range(GLA_H):
        at(73 + 4 * hh, "mask", hh)
        at(74 + 4 * hh, "gla_out", hh)
        at(75 + 4 * hh, "gla_norm", hh)
    return beside


class Count:

    def __init__(self):
        self.n, self.terms = 0, []

    def at(self, k=0):
        value = self.n + k
        for reg, per in self.terms:
            value = reg * per + value
        return value


def turns(eng, times, counts, began):
    @contextmanager
    def run():
        starts = [c.n for c, _ in counts]
        eng.sem_inc(began, 1)
        with eng.Fori(0, times) as i:
            for c, per in counts:
                c.terms.append((i, per))
            yield i
            for (c, per), n0 in zip(counts, starts):
                assert c.n - n0 == per, (c.n - n0, per)
                c.terms.pop()
                c.n = n0 + per * times
    return run()


def build(nc, x, p, positions, norm_mix_g, w_in, gla_w_alpha, gla_b_alpha, gla_norm_g, diff_q_norm_g,
          diff_k_norm_g, diff_lambda_q1, diff_lambda_k1, diff_lambda_q2, diff_lambda_k2, diff_subln_g,
          swa_q_norm_g, swa_k_norm_g, swa_sinks, w_out, norm_ffn_g, w_ffn_in, w_ffn_out, norm_ple_g,
          w_ple_gate, w_ple_proj, consts, out):
    ctx = ExitStack()
    with ctx:
        def sb(name, shape, dt=F32):
            return ctx.enter_context(nc.sbuf_tensor(name, shape, dt))

        def sem(name):
            return ctx.enter_context(nc.semaphore(name))

        def over(name, shape, dt, offset):
            return nc.alloc_sbuf_tensor_at(name, shape, dt, offset=offset)

        hid_at = -(-nc.sbuf_base // 32) * 32
        hid = sb("hid", [P, KT, 2, S], F32R)
        h = sb("h", [P, KT, S])
        u = sb("u", [P, KT, 2, S], F32R)
        raw = sb("raw", [P, RING, UK * G])
        wsp = sb("wsp", [P, RING, UK, 2, G], F32R)
        wide = sb("wide", [P, 2 * D])
        cst = sb("cst", [P, K_COLS])
        prm = sb("prm", [P, DEPTH * R_ALL])
        ones = sb("ones", [P, P])
        epst = sb("epst", [P, 2])
        walr_raw = sb("walr_raw", [P, KT, RANK])
        walr = sb("walr", [P, KT, 2, RANK], F32R)
        wal = sb("wal", [RANK, GLA_H * DK])
        lam = sb("lam", [P, 4, DEPTH])
        sinks = sb("sinks", [P, DEPTH, SWA_H])
        cosB = sb("cosB", [P, S])
        sinB = sb("sinB", [P, S])
        rstdB = sb("rstdB", [P, S])
        rstdC = sb("rstdC", [P, TT])
        sqt = sb("sqt", [P, S])
        ssq = sb("ssq", [P, S])
        cross = sb("cross", [P, 2, 2 * S])
        ta = sb("ta", [P, 2 * S])
        tb = sb("tb", [P, 2 * S])
        sg = sb("sg", [P, 2 * S])
        hf = sb("hf", [P, 2 * S])
        rsn = sb("rsn", [P, 2 * S])
        lnt = sg
        bc = sb("bc", [P, GLA_H, S + 1])
        pe_buf = sb("pe_buf", [P, 2, 2, S])
        st = sb("st", [P, 2, 16])

        gl = over("gl", [P, GLA_H, 4 * S], F32, hid_at)
        qg, kg, gt = gl[:, :, 0:S], gl[:, :, S:2 * S], gl[:, :, 2 * S:3 * S]
        sk, svT = gl[:, 0, 3 * S:4 * S], gl[:, 1, 3 * S:4 * S]
        alr = gl[:, 2, 3 * S:3 * S + TT * RANK].rearrange("p (t r) -> p t r", t=TT)
        att = gl[:, 3, 2 * S:2 * S + 3 * P]
        prm_rows = over("prm_rows", [P, P], F32, hid_at)
        pos_i = over("pos_i", [P, S], I32, hid_at + 1024)
        lamv = over("lamv", [P, 4, DEPTH, HD], F32, hid_at + 4096)
        lamp = over("lamp", [P, 2, DEPTH, HD], F32, hid_at + 6144)

        kn = sb("kn", [P, 8, 2 * P])

        dq_at = -(-nc.sbuf_base // 32) * 32
        dq = sb("dq", [P, DIFF_H, S])
        dk = sb("dk", [P, DIFF_H, S])
        dv = sb("dv", [P, TT, DIFF_H * P])
        sq = sb("sq", [P, SWA_H // 2, S])
        ptok = over("ptok", [P, TT, PLE], F32, dq_at)
        pT = over("pT", [P, 2, 2, S], F32R, dq_at + 4096)
        alrT = sb("alrT", [RANK, S])

        vg = wide[:, 0:D].rearrange("p (t c) -> p t c", t=TT)
        sgate = wide[:, D:2 * D].rearrange("p (j t) -> p j t", t=S)
        pleT = wide[:, :].rearrange("p (j t) -> p j t", t=S)
        xtok = wide[:, :].rearrange("p (t c) -> p t c", t=TT)
        kd = wide[:, 0:2 * S].rearrange("p (g t) -> p g t", g=2)
        sv = wide[:, 2 * S:3 * S].rearrange("p (a c) -> p a c", a=TT)
        wT = wide[:, 3 * S:7 * S].rearrange("p (b e t) -> p b e t", b=2, e=4)
        osq = wide[:, 7 * S:8 * S]
        nsq = wide[:, D:D + 2 * S]

        ident = cst[:, K_ID:K_ID + P]

        pd = ctx.enter_context(nc.psum_tensor("pd", [P, 2, 2, 512], F32))
        pm = ctx.enter_context(nc.psum_tensor("pm", [P, 4, 512], F32))

        s_began = sem("s_began")
        s_small = sem("s_small")
        s_x = sem("s_x")
        s_raw = [sem(f"s_raw{i}") for i in range(RING)]
        s_hi = sem("s_hi")
        s_lo = sem("s_lo")
        s_used = sem("s_used")
        s_half = sem("s_half")
        s_lay = [sem(f"s_lay{i}") for i in range(3)]
        s_walr = sem("s_walr")
        s_p = sem("s_p")
        s_phi = sem("s_phi")
        s_plo = sem("s_plo")
        s_psfree = sem("s_psfree")
        s_cross = sem("s_cross")
        s_hnew = sem("s_hnew")
        s_uhi = sem("s_uhi")
        s_u = sem("s_u")
        s_sqt = sem("s_sqt")
        s_ssq = sem("s_ssq")
        s_nmm = sem("s_nmm")
        s_rln = sem("s_rln")
        s_rstd = sem("s_rstd")
        s_dve = sem("s_dve")
        s_act = sem("s_act")
        s_init = sem("s_init")
        s_inita = sem("s_inita")
        s_tr = sem("s_tr")
        s_trc = sem("s_trc")
        s_gate = sem("s_gate")
        s_silu = sem("s_silu")
        s_hf = sem("s_hf")
        s_hidhi = sem("s_hidhi")
        s_hid = sem("s_hid")
        s_ev = sem("s_ev")
        s_alrT = sem("s_alrT")
        s_alrTc = sem("s_alrTc")
        s_xa = sem("s_xa")
        s_xs = sem("s_xs")
        s_la = sem("s_la")
        s_bd = sem("s_bd")
        s_eq = sem("s_eq")
        s_qd = sem("s_qd")
        s_ke = sem("s_ke")
        s_kn = sem("s_kn")
        s_am = sem("s_am")
        s_att = sem("s_att")
        s_go = sem("s_go")
        s_gsq = sem("s_gsq")
        s_gss = sem("s_gss")
        s_grs = sem("s_grs")
        s_mf = sem("s_mf")
        s_mhi = sem("s_mhi")
        s_mix = sem("s_mix")
        s_nsq = sem("s_nsq")
        s_nss = sem("s_nss")
        s_nrs = sem("s_nrs")
        s_qn = sem("s_qn")
        s_rot = sem("s_rot")
        s_rope = sem("s_rope")
        s_kcos = sem("s_kcos")
        s_krot = sem("s_krot")
        s_svT = sem("s_svT")
        s_sv = sem("s_sv")
        s_sc = sem("s_sc")
        s_mx = sem("s_mx")
        s_ex = sem("s_ex")
        s_wt = sem("s_wt")
        s_tp = sem("s_tp")
        s_tpc = sem("s_tpc")
        s_pv = sem("s_pv")
        s_osq = sem("s_osq")
        s_oss = sem("s_oss")
        s_ors = sem("s_ors")
        s_out = sem("s_out")

        block = ctx.enter_context(nc.Block())

        @block.sync
        def _(sp):
            unit = Count()

            def load(dst_slot, src, shape):
                sp.wait_ge(s_lo, unit.at(1))
                sp.dma_start(raw[:, dst_slot, :].rearrange(shape[0], **shape[1]), src).then_inc(s_raw[dst_slot], 16)
                unit.n += 1

            def rows(w, layer, r0, c0):
                return w[layer, bass.ds(r0 * P, UK * P), bass.ds(c0, G)].rearrange("(k p) n -> p k n", p=P)

            kn_shape = ("p (k n) -> p k n", dict(k=UK))

            sp.dma_start(xtok, x.rearrange("b (t p) c -> p (b t) c", p=P)).then_inc(s_x, 16)
            for l in range(DEPTH):
                at = l * R_ALL
                for r, src, n in ((R_MIX, norm_mix_g[l].rearrange("(j p) -> j p", p=P), KT),
                                  (R_FFN, norm_ffn_g[l].rearrange("(j p) -> j p", p=P), KT),
                                  (R_PLE, norm_ple_g[l].rearrange("(j p) -> j p", p=P), KT),
                                  (R_BAL, gla_b_alpha[l].rearrange("(j p) -> j p", p=P), GLA_H),
                                  (R_GLA, gla_norm_g[l].rearrange("(j p) -> j p", p=P), DV // P),
                                  (R_SUB, diff_subln_g[l:l + 1, :], 1)):
                    sp.dma_start(prm_rows[at + r:at + r + n, :], src).then_inc(s_small, 16)
                for r, src in ((R_DQ, diff_q_norm_g), (R_DK, diff_k_norm_g), (R_SQ, swa_q_norm_g),
                               (R_SK, swa_k_norm_g)):
                    for c in range(2):
                        sp.dma_start(prm_rows[at + r:at + r + 1, c * HD:(c + 1) * HD],
                                     src[l:l + 1, :]).then_inc(s_small, 16)
            sp.dma_start(cst[:, :], consts).then_inc(s_small, 16)
            sp.dma_start(pos_i[:, :], positions.to_broadcast([P, S])).then_inc(s_small, 16)
            sp.dma_start(sinks[:, :, :].rearrange("p l h -> p (l h)"),
                         swa_sinks.rearrange("(a l) h -> a (l h)", a=1).to_broadcast([P, DEPTH * SWA_H])
                         ).then_inc(s_small, 16)
            for n, src in enumerate((diff_lambda_q1, diff_lambda_k1, diff_lambda_q2, diff_lambda_k2)):
                sp.dma_start(lamv[:, n, :, :].rearrange("p l h -> p (l h)"),
                             src.rearrange("(a l) h -> a (l h)", a=1).to_broadcast([P, DEPTH * HD])
                             ).then_inc(s_small, 16)

            with turns(sp, DEPTH, [(unit, UNITS_PER_LAYER)], s_began) as layer:
                sp.wait_ge(s_hnew, layer * 24 + 1)
                sp.dma_start(walr_raw[:, :, :], w_in[layer, :, C_ALR:C_ALR + RANK].rearrange("(k p) n -> p k n", p=P)
                             ).then_inc(s_lay[0], 16)
                sp.dma_start(wal[:, :], gla_w_alpha[layer, :, :]).then_inc(s_lay[1], 16)
                for c in (C_SKV, C_SQ, C_SQ + G):
                    for k in range(4):
                        load(k, rows(w_in, layer, k * UK, c), kn_shape)
                for c, times in ((C_DQ, 6), (C_GQ, 4), (C_GATE, 4), (C_GV, 4)):
                    with turns(sp, times, [(unit, 4)], s_began) as i:
                        for k in range(4):
                            load(k, rows(w_in, layer, k * UK, i * G + c), kn_shape)
                for r in (8, 0):
                    with turns(sp, 4, [(unit, 4)], s_began) as i:
                        for g in range(2):
                            for k in range(2):
                                load(2 * g + k, rows(w_out, layer, r + k * UK, i * 2 * G + g * G), kn_shape)
                done = 0
                for n in ROUNDS:
                    with turns(sp, n // 2, [(unit, 8)], s_began) as i:
                        for c0 in (0, D_FF):
                            for k in range(4):
                                load(k, rows(w_ffn_in, layer, k * UK, i * G + (c0 + done * P)), kn_shape)
                    if n == 16:
                        with turns(sp, 8, [(unit, 4)], s_began) as i:
                            for k in range(4):
                                load(k, rows(w_ffn_out, layer, done + k * UK, i * G), kn_shape)
                    else:
                        with turns(sp, 2, [(unit, 12)], s_began) as i:
                            for g in range(4):
                                for k in range(3):
                                    load((3 * g + k) % RING, rows(w_ffn_out, layer, done + k * UK, i * 4 * G + g * G),
                                         kn_shape)
                    done += n
                sp.wait_ge(s_hnew, layer * 24 + 16)
                sp.dma_start(ptok[:, :, :], p[layer, 0, :, :].rearrange("(t p) c -> p t c", p=P)).then_inc(s_lay[2], 16)
                for k in range(4):
                    load(k, w_ple_proj[layer, :, k * 2 * G:(k + 1) * 2 * G].rearrange("(k p) n -> p k n", p=P),
                         ("p (k n) -> p k n", dict(k=2)))
                with turns(sp, 8, [(unit, 4)], s_began) as i:
                    for k in range(4):
                        load(k, rows(w_ple_gate, layer, k * UK, i * G), kn_shape)
            for k in range(AHEAD):
                sp.wait_ge(s_lo, unit.at(1 + k))
                sp.sem_inc(s_raw[k], 16)
            for g in range(8):
                sp.wait_ge(s_trc, 8 + g + 1)
                sp.dma_start(out.rearrange("b (t p) c -> p (b t) c", p=P)[:, :, g * G:(g + 1) * G],
                             xtok[:, :, g * G:(g + 1) * G]).then_inc(s_out, 16)
            sp.wait_ge(s_out, 8 * 16)

        n_small = 16 * (DEPTH * (6 + 8) + 7)

        @block.gpsimd
        def _(pool):
            norm = Count()
            step = Count()

            def squares():
                with turns(pool, 8, [(step, 4)], s_began) as g:
                    pool.wait_ge(s_hnew, norm.at() * 8 + g + 1)
                    for j in range(2):
                        hv = h[:, bass.ds(2 * g + j, 1), :].rearrange("p j t -> p (j t)")
                        nc.gpsimd.tensor_tensor(sqt[:, :], hv, hv, ALU.mult).then_inc(s_sqt, 1)
                        pool.wait_ge(s_sqt, step.at(1))
                        nc.gpsimd.tensor_tensor(ssq[:, :], ssq[:, :], sqt[:, :], ALU.add).then_inc(s_sqt, 1)
                        step.n += 2
                        pool.wait_ge(s_sqt, step.at())
                pool.sem_inc(s_ssq, 1)
                norm.n += 1

            nc.gpsimd.memset(ssq[:, :], 0.0).then_inc(s_sqt, 1)
            step.n += 1
            pool.wait_ge(s_sqt, 1)
            squares()
            with turns(pool, DEPTH, [(norm, 3), (step, 3 * 33)], s_began) as layer:
                for n in range(3):
                    pool.wait_ge(s_nmm, norm.at())
                    pool.sem_inc(s_began, 1)
                    nc.gpsimd.memset(ssq[:, :], 0.0).then_inc(s_sqt, 1)
                    step.n += 1
                    pool.wait_ge(s_sqt, step.at())
                    squares()

        @block.scalar
        def _(act):
            unit, group, norm, hn, chain = Count(), Count(), Count(), Count(), Count()
            silu, hidc = Count(), Count()

            def link(ins):
                chain.n += 1
                ins.then_inc(s_act, 1)
                act.wait_ge(s_act, chain.at())

            def split(slot):
                act.wait_ge(s_used, unit.at(1))
                act.wait_ge(s_raw[slot], raw_landed(slot))
                nc.scalar.activation(wsp[:, slot, :, 0, :], raw[:, slot, :].rearrange("p (k n) -> p k n", k=UK),
                                     ACT.Copy).then_inc(s_hi, 1)
                unit.n += 1

            def raw_landed(slot):
                assert unit.n % RING == slot
                value = (unit.n // RING + 1) * 16
                for reg, per in unit.terms:
                    assert per % RING == 0
                    value = reg * (per // RING * 16) + value
                return value

            def units(n):
                for _ in range(n):
                    split(unit.n % RING)

            def take_cross(scale=None, done=None):
                par = group.n % 2
                act.wait_ge(*(done or (s_used, unit.at(1))))
                if scale is None:
                    nc.scalar.activation(cross[:, par, :].rearrange("p (a t) -> p a t", a=2),
                                         pd[:, par, :, S:2 * S], ACT.Copy).then_inc(s_cross, 1)
                else:
                    for tt in range(TT):
                        ins = nc.scalar.activation(cross[:, par, tt * S:(tt + 1) * S], pd[:, par, tt, S:2 * S],
                                                   ACT.Copy, scale=rstdC[:, tt:tt + 1])
                    ins.then_inc(s_cross, 1)
                group.n += 1

            def make_u(g, gain, wait):
                act.wait_ge(s_hnew, wait)
                for j in range(2):
                    ins = nc.scalar.activation(u[:, bass.ds(2 * g + j, 1), 0, :], h[:, bass.ds(2 * g + j, 1), :],
                                               ACT.Copy, scale=gain(2 * g + j))
                ins.then_inc(s_uhi, 1)

            def rms(token_major):
                nc.scalar.preload_act_table_set(LN_EXP)
                norm.n += 1
                act.wait_ge(s_nmm, norm.at())
                link(nc.scalar.activation(rstdB[:, :], pm[:, 0, 0:S], ACT.Ln, scale=1.0 / D, bias=epst[:, 0:1]))
                if token_major:
                    link(nc.scalar.activation(rstdC[:, :], pm[:, 0, S:S + TT], ACT.Ln, scale=1.0 / D,
                                              bias=epst[:, 0:1]))
                    link(nc.scalar.activation(rstdC[:, :], rstdC[:, :], ACT.Exp, scale=-0.5))
                nc.scalar.activation(rstdB[:, :], rstdB[:, :], ACT.Exp, scale=-0.5).then_inc(s_rstd, 1)
                act.wait_ge(s_rstd, norm.at())

            act.wait_ge(s_small, n_small)
            act.wait_ge(s_init, 1)
            nc.scalar.activation(sinB[:, :], sinB[:, :], ACT.Sin)
            nc.scalar.activation(cosB[:, :], cosB[:, :], ACT.Sin).then_inc(s_inita, 1)
            nc.scalar.activation(lam[:, 0:2, :], lam[:, 0:2, :], ACT.Exp).then_inc(s_inita, 1)
            act.wait_ge(s_init, 2)
            units(AHEAD)

            with turns(act, DEPTH, [(unit, UNITS_PER_LAYER), (group, GROUPS_PER_LAYER), (norm, 3), (hn, 24),
                                    (chain, ACT_LINKS), (silu, 31), (hidc, 22)], s_began) as layer:
                lp = layer * R_ALL

                def column(r):
                    return prm[:, bass.ds(lp + r, 1)]

                act.wait_ge(s_used, unit.at(1))
                with turns(act, 8, [(hn, 1)], s_began) as g:
                    hn.n += 1
                    make_u(g, lambda j: prm[:, bass.ds(j + (lp + R_MIX), 1)], hn.at())
                act.wait_ge(s_lay[0], layer * 16 + 16)
                nc.scalar.activation(walr[:, :, 0, :], walr_raw[:, :, :], ACT.Copy).then_inc(s_walr, 1)

                def rank(_):
                    act.wait_ge(s_alrT, layer + 1)
                    nc.scalar.activation(alrT[:, :], pm[0:RANK, 2, 0:S], ACT.Copy).then_inc(s_alrTc, 1)

                def logits(_):
                    act.wait_ge(s_xa, layer + 1)
                    for hh in range(GLA_H):
                        ins = nc.scalar.activation(gt[:, hh, :], pm[:, hh // 2, hh % 2 * S:(hh % 2 + 1) * S],
                                                   ACT.Identity, bias=column(R_BAL + hh))
                    link(ins)
                    link(nc.scalar.activation(bc[:, :, 1:], gt, ACT.Abs))
                    link(nc.scalar.activation(bc[:, :, 1:], bc[:, :, 1:], ACT.Exp, scale=-1.0))
                    nc.scalar.activation(bc[:, :, 1:], bc[:, :, 1:], ACT.Ln, bias=epst[:, 1:2]).then_inc(s_xs, 1)

                def block_decay(_):
                    act.wait_ge(s_bd, layer + 1)
                    nc.scalar.activation(gt, gt, ACT.Exp).then_inc(s_eq, 1)

                def squares(n):
                    item = items(dq, dk, sq, sk)[n]
                    act.wait_ge(s_ev, layer * EV + EV_ITEM[n])
                    nc.scalar.activation(nsq[:, 0:item.shape[-1]], item, ACT.Square).then_inc(s_nsq, 1)

                def norm_item(n):
                    w = items(dq, dk, sq, sk)[n].shape[-1]
                    act.wait_ge(s_nss, layer * 7 + (n + 1))
                    link(nc.scalar.activation(lnt[:, 0:w], pm[:, 3, 0:w], ACT.Ln, bias=epst[:, 0:1]))
                    if n:
                        act.wait_ge(s_qn, layer * 7 + n)
                    nc.scalar.activation(rsn[:, 0:w], lnt[:, 0:w], ACT.Exp, scale=-0.5).then_inc(s_nrs, 1)

                def mixer_hi(tile, n, src, wait_for, value):
                    act.wait_ge(wait_for, value)
                    nc.scalar.activation(hid[:, tile:tile + n, 0, :], src, ACT.Copy).then_inc(s_mhi, 1)

                def scores(z):
                    act.wait_ge(s_mx, layer * 16 + (z + 1))
                    j = z % 2
                    diff, k0 = z >= 8, 0 if z >= 8 or j == 0 else CHUNK
                    kw = (j + 1) * P
                    for c in range(2):
                        ins = nc.scalar.activation(pe_buf[:, z % 2, c, k0:kw], pm[:, c, k0:kw], ACT.Exp,
                                                   scale=SCALE, bias=st[:, z % 2, c:c + 1],
                                                   accum_out=st[:, z % 2, 2 + c:3 + c])
                    if not diff:
                        ins = nc.scalar.activation(st[:, z % 2, 4:6], st[:, z % 2, 6:8], ACT.Exp)
                    ins.then_inc(s_ex, 1)

                def transpose(z):
                    j = z % 2
                    act.wait_ge(s_tp, layer * 16 + (z + 1))
                    if z >= 8:
                        nc.scalar.activation(wT[:, z % 2, 0:j + 1, :],
                                             pm[:, 0, 0:(j + 1) * P].rearrange("p (a t) -> p a t", t=P),
                                             ACT.Copy).then_inc(s_tpc, 1)
                    else:
                        nc.scalar.activation(wT[:, z % 2, :, :].rearrange("p (e k) t -> p e k t", e=2)[:, :, 0:j + 1, :],
                                             pm[:, 0, :].rearrange("p (e k t) -> p e k t", e=2, k=2)[:, :, 0:j + 1, :],
                                             ACT.Copy).then_inc(s_tpc, 1)

                def values(z):
                    if z % 2 == 1 and z < 8:
                        mixer_hi(12 + z // 2, 1, pm[:, 2, 0:S], s_pv, layer * 8 + (z // 2 + 1))
                    elif z % 2 == 1:
                        act.wait_ge(s_pv, layer * 8 + (z // 2 + 1))
                        nc.scalar.activation(osq, pm[:, 2, 0:S], ACT.Square).then_inc(s_osq, 1)

                def diff_norm(hh):
                    act.wait_ge(s_oss, layer * DIFF_H + (hh + 1))
                    link(nc.scalar.activation(lnt[:, 0:S], pm[:, 0, 0:S], ACT.Ln, scale=1.0 / P, bias=epst[:, 0:1]))
                    nc.scalar.activation(rsn[:, 0:S], lnt[:, 0:S], ACT.Exp, scale=-0.5).then_inc(s_ors, 1)
                    mixer_hi(8 + hh, 1, hf[:, 0:S], s_mf, layer * 8 + (hh + 1))

                def gate(_):
                    silu.n += 1
                    act.wait_ge(s_gate, silu.at())
                    nc.scalar.activation(sgate[:, :, :], sgate[:, :, :], ACT.Silu).then_inc(s_silu, 1)
                    nc.scalar.preload_act_table_set(LN_EXP)

                def keys(i):
                    hh = i // 4
                    for idx in range(4 * i, 4 * i + 4):
                        n = idx % NBLK
                        if idx >= 8:
                            act.wait_ge(s_am, layer * 64 + (idx - 7))
                        at, width = (P, BLK * (n + 1)) if n < 8 else (0, BLK * (n + 1))
                        nc.scalar.activation(kn[:, n % 8, at:at + width], bc[:, hh, 1:1 + width], ACT.Exp,
                                             bias=bc[:, hh, BLK * n:BLK * n + 1], scale=-1.0).then_inc(s_ke, 1)

                def gla_out(hh):
                    act.wait_ge(s_go, layer * GLA_H + (hh + 1))
                    nc.scalar.activation(pe_buf[:, 0, :, :], pm[:, 2, :].rearrange("p (a t) -> p a t", a=2),
                                         ACT.Square).then_inc(s_gsq, 1)

                def gla_norm(hh):
                    act.wait_ge(s_gss, layer * GLA_H + (hh + 1))
                    link(nc.scalar.activation(lnt[:, 0:S], pm[:, 0, 0:S], ACT.Ln, scale=1.0 / DV, bias=epst[:, 0:1]))
                    nc.scalar.activation(rsn[:, 0:S], lnt[:, 0:S], ACT.Exp, scale=-0.5).then_inc(s_grs, 1)
                    mixer_hi(2 * hh, 2, hf[:, :].rearrange("p (a t) -> p a t", a=2), s_mf, layer * 8 + (DIFF_H + hh + 1))

                steps = dict(rank=rank, logits=logits, block_decay=block_decay, squares=squares, norm=norm_item,
                             scores=scores, transpose=transpose, values=values, diff_norm=diff_norm, gate=gate,
                             keys=keys, gla_out=gla_out, gla_norm=gla_norm)

                def beside(slot, n):
                    for q in range(n):
                        units(1)
                        for step, i in BESIDE.get(slot + q, ()):
                            if step in steps:
                                steps[step](i)

                units(4)
                rms(True)
                take_cross()
                act.wait_ge(s_half, layer * 5 + 1)
                for tt in range(TT):
                    ins = nc.scalar.activation(cross[:, 1, tt * RANK:(tt + 1) * RANK], pd[:, 1, tt, RANK:2 * RANK],
                                               ACT.Copy, scale=rstdC[:, tt:tt + 1])
                ins.then_inc(s_cross, 1)
                group.n += 1
                for g in range(1, 21):
                    beside(4 * g, 4)
                    take_cross(rstdC if g in BY_TOKEN else None)

                for g in range(2):
                    beside(84 + 2 * g, 2)
                    group.n += 1
                with turns(act, 3, [(unit, 4), (group, 2)], s_began) as i:
                    units(4)
                    group.n += 2
                with turns(act, 4, [(unit, 4), (group, 2), (hn, 2)], s_began) as i:
                    for g in range(2):
                        units(2)
                        group.n += 1
                        hn.n += 1
                        make_u(i * 2 + g, lambda j: prm[:, bass.ds(j + (lp + R_FFN), 1)], hn.at())

                def hidden_pair(i, first=False):
                    units(4)
                    if first:
                        rms(False)
                    take_cross()
                    silu.n += 1
                    act.wait_ge(s_gate, silu.at())
                    nc.scalar.activation(sg[:, :], ta[:, :], ACT.Silu).then_inc(s_silu, 1)
                    units(4)
                    take_cross()
                    hidc.n += 1
                    act.wait_ge(s_hf, hidc.at())
                    nc.scalar.activation(hid[:, bass.ds(i * 2, 2), 0, :], hf[:, :].rearrange("p (a t) -> p a t", a=2),
                                         ACT.Copy).then_inc(s_hidhi, 1)

                for r, n in enumerate(ROUNDS):
                    peeled = int(r == 0)
                    if peeled:
                        hidden_pair(0, first=True)
                    with turns(act, n // 2 - peeled, [(unit, 8), (group, 2), (silu, 1), (hidc, 1)], s_began) as i:
                        hidden_pair(i + peeled)
                    last = r == len(ROUNDS) - 1
                    per = 2 if n == 16 else 4
                    with turns(act, 8 // per, [(unit, n // 4 * per), (group, per)] + [(hn, per)] * last, s_began) as i:
                        for g in range(per):
                            units(n // UK)
                            group.n += 1
                            if last:
                                hn.n += 1
                                make_u(i * per + g, lambda j: prm[:, bass.ds(j + (lp + R_PLE), 1)], hn.at())

                act.wait_ge(s_p, layer + 1)
                nc.scalar.activation(pT[:, :, 0, :], pm[:, 1, :].rearrange("p (a t) -> p a t", a=2),
                                     ACT.Copy).then_inc(s_phi, 1)
                for g in range(8):
                    if g % 2 == 0:
                        units(1)
                    take_cross(done=(s_half, layer * 5 + (2 + g // 2)) if g % 2 == 0 else None)

                def ple_group(g, first=False):
                    units(4)
                    if first:
                        rms(False)
                    take_cross()
                    silu.n += 1
                    act.wait_ge(s_gate, silu.at())
                    nc.scalar.activation(sg[:, :], ta[:, :], ACT.Sigmoid).then_inc(s_silu, 1)

                ple_group(0, first=True)
                ple_group(1)
                with turns(act, 3, [(unit, 8), (group, 2), (silu, 2)], s_began) as i:
                    ple_group(i * 2 + 2)
                    ple_group(i * 2 + 3)

        @block.vector
        def _(dve):
            unit, group, norm, hn, chain = Count(), Count(), Count(), Count(), Count()
            silu, hidc, evc, crossed = Count(), Count(), Count(), Count()

            def link(ins):
                chain.n += 1
                ins.then_inc(s_dve, 1)
                dve.wait_ge(s_dve, chain.at())

            def split(slot):
                dve.wait_ge(s_hi, unit.at(1))
                nc.vector.tensor_tensor(wsp[:, slot, :, 1, :], raw[:, slot, :].rearrange("p (k n) -> p k n", k=UK),
                                        wsp[:, slot, :, 0, :].bitcast(F32), ALU.subtract).then_inc(s_lo, 1)
                unit.n += 1

            def units(n):
                for _ in range(n):
                    split(unit.n % RING)

            def halves(t):
                return t[:, :].rearrange("p (a t) -> p a t", a=2)

            def both(t):
                return t[:, :].unsqueeze(1).to_broadcast([P, 2, S])

            def main_plus_cross(dst):
                par = group.n % 2
                crossed.n += 1
                dve.wait_ge(s_cross, crossed.at())
                group.n += 1
                nc.vector.tensor_tensor(dst, pd[:, par, :, 0:S], halves_of(cross[:, par, :]), ALU.add
                                        ).then_inc(s_psfree, 1)
                dve.wait_ge(s_psfree, group.at(2))

            def halves_of(ap):
                return ap.rearrange("p (a t) -> p a t", a=2)

            def feature_major(dst):
                main_plus_cross(halves(ta))
                nc.vector.tensor_tensor(dst, halves(ta), both(rstdB), ALU.mult).then_inc(s_ev, 1)
                evc.n += 1
                dve.wait_ge(s_ev, evc.at())

            def token_major(dst):
                par = group.n % 2
                crossed.n += 1
                dve.wait_ge(s_cross, crossed.at())
                for tt in range(TT):
                    ins = nc.vector.scalar_tensor_tensor(dst(tt), pd[:, par, tt, 0:S], rstdC[:, tt:tt + 1],
                                                         cross[:, par, tt * S:(tt + 1) * S], ALU.mult, ALU.add)
                ins.then_inc(s_psfree, 1)
                group.n += 1
                evc.n += 1
                dve.wait_ge(s_psfree, group.at(2))
                dve.sem_inc(s_ev, 1)

            def add_to_h(g):
                par = group.n % 2
                dve.wait_ge(s_used, unit.at(1))
                hv = h[:, bass.ds(2 * g, 2), :]
                link(nc.vector.tensor_tensor(hv, pd[:, par, :, 0:S], hv, ALU.add))
                ins = nc.vector.tensor_tensor(hv, pd[:, par, :, S:2 * S], hv, ALU.add)
                ins.then_inc(s_psfree, 1)
                group.n += 1
                dve.wait_ge(s_psfree, group.at(2))

            def make_u(g, gain):
                hn.n += 1
                dve.wait_ge(s_uhi, hn.at())
                for j in range(2):
                    k = bass.ds(2 * g + j, 1)
                    ins = nc.vector.scalar_tensor_tensor(u[:, k, 1, :], h[:, k, :], gain(2 * g + j),
                                                         u[:, k, 0, :].bitcast(F32), ALU.mult, ALU.subtract)
                ins.then_inc(s_u, 1)

            dve.memset(ones[:, :], 1.0)
            dve.memset(epst[:, 0:1], EPS)
            dve.memset(epst[:, 1:2], 1.0)
            dve.memset(bc[:, :, 0:1], 0.0)
            dve.memset(kn[:, :, :], 0.0)
            dve.memset(pe_buf[:, :, :, :], 0.0)
            dve.wait_ge(s_small, n_small)
            link(nc.vector.tensor_copy(ta[:, 0:S], pos_i[:, :]))
            link(nc.vector.tensor_scalar(ta[:, 0:S], ta[:, 0:S], cst[:, K_INV:K_INV + 1], None, ALU.mult))
            for dst, turn, shift in ((sinB, 0.0, 0.0), (cosB, 0.25, 1.5707963267948966)):
                link(nc.vector.tensor_scalar(tb[:, 0:S], ta[:, 0:S], INV_2PI, turn, ALU.mult, ALU.add))
                link(nc.vector.tensor_scalar(tb[:, 0:S], tb[:, 0:S], MAGIC, None, ALU.add))
                link(nc.vector.tensor_scalar(tb[:, 0:S], tb[:, 0:S], MAGIC, None, ALU.subtract))
                link(nc.vector.scalar_tensor_tensor(hf[:, 0:S], tb[:, 0:S], -PI2_A, ta[:, 0:S], ALU.mult, ALU.add))
                link(nc.vector.scalar_tensor_tensor(hf[:, 0:S], tb[:, 0:S], -PI2_B, hf[:, 0:S], ALU.mult, ALU.add))
                link(nc.vector.scalar_tensor_tensor(hf[:, 0:S], tb[:, 0:S], -PI2_C, hf[:, 0:S], ALU.mult, ALU.add))
                link(nc.vector.tensor_scalar(hf[:, 0:S], hf[:, 0:S], shift, PI_LO, ALU.add, ALU.min))
                link(nc.vector.tensor_scalar(dst[:, :], hf[:, 0:S], -PI_LO, None, ALU.max))
            link(nc.vector.tensor_tensor(lamp[:, 0], lamv[:, 0], lamv[:, 1], ALU.mult))
            link(nc.vector.tensor_tensor(lamp[:, 1], lamv[:, 2], lamv[:, 3], ALU.mult))
            link(nc.vector.tensor_reduce(lam[:, 0:2, :], lamp[:, :, :, :], AX.X, ALU.add))
            dve.sem_inc(s_init, 1)
            dve.wait_ge(s_inita, 2)
            link(nc.vector.tensor_tensor(lam[:, 2, :], lam[:, 0, :], lam[:, 1, :], ALU.subtract))
            link(nc.vector.tensor_tensor(lam[:, 2, :], lam[:, 2, :], cst[:, K_LAM:K_LAM + 2], ALU.add))
            link(nc.vector.tensor_scalar(lam[:, 3, :], lam[:, 2, :], -1.0, None, ALU.mult))
            dve.wait_ge(s_tr, 1)
            link(nc.vector.tensor_copy(prm[:, 0:DEPTH * R_ALL], pm[:, 0, 0:DEPTH * R_ALL]))
            for l in range(DEPTH):
                at = l * R_ALL + R_SUB
                link(nc.vector.tensor_tensor(prm[:, at:at + 1], prm[:, at:at + 1],
                                             cst[:, K_ONE_LAM + l:K_ONE_LAM + l + 1], ALU.mult))
            dve.sem_inc(s_init, 1)
            for g in range(8):
                dve.wait_ge(s_tr, 2 + g)
                link(nc.vector.tensor_copy(h[:, 2 * g:2 * g + 2, :], halves_of(pm[:, g % 4, :])))
                dve.sem_inc(s_trc, 1)
                dve.sem_inc(s_hnew, 1)
            dve.sem_inc(s_lo, RING)
            dve.sem_inc(s_psfree, 2)
            units(AHEAD)

            with turns(dve, DEPTH, [(unit, UNITS_PER_LAYER), (group, GROUPS_PER_LAYER), (norm, 3), (hn, 24),
                                    (chain, DVE_LINKS), (silu, 31), (hidc, 22), (evc, EV), (crossed, CROSSED)], s_began) as layer:
                lp = layer * R_ALL

                def column(r):
                    return prm[:, bass.ds(lp + r, 1)]

                with turns(dve, 8, [(hn, 1)], s_began) as g:
                    make_u(g, lambda j: prm[:, bass.ds(j + (lp + R_MIX), 1)])
                nc.vector.memset(pe_buf[:, 1, :, 0:CHUNK], 0.0)
                dve.wait_ge(s_walr, layer * 2 + 1)
                nc.vector.tensor_tensor(walr[:, :, 1, :], walr_raw[:, :, :], walr[:, :, 0, :].bitcast(F32),
                                        ALU.subtract).then_inc(s_walr, 1)

                def log_decay(_):
                    dve.wait_ge(s_xs, layer + 1)
                    link(nc.vector.scalar_tensor_tensor(gt, gt, 0.0, bc[:, :, 1:], ALU.min, ALU.subtract))
                    link(nc.vector.tensor_scalar(gt, gt, 1.0 / GLA_TAU, None, ALU.mult))

                def decay_sums(_):
                    for hh in range(GLA_H):
                        ins = nc.vector.tensor_tensor_scan(bc[:, hh, 1:], ones[:, 0:1].to_broadcast([P, S]), gt[:, hh, :],
                                                           0.0, ALU.mult, ALU.add)
                    ins.then_inc(s_la, 1)

                def block_decay(_):
                    dve.wait_ge(s_la, layer + 1)
                    for hh in range(GLA_H):
                        start = bc[:, hh, 0:S].rearrange("p (n b) -> p n b", b=BLK)[:, :, 0:1].to_broadcast([P, NBLK, BLK])
                        ins = nc.vector.tensor_tensor(gt[:, hh, :].rearrange("p (n b) -> p n b", b=BLK),
                                                      bc[:, hh, 1:].rearrange("p (n b) -> p n b", b=BLK), start, ALU.subtract)
                    ins.then_inc(s_bd, 1)

                def norm_item(n):
                    item = items(dq, dk, sq, sk)[n]
                    dve.wait_ge(s_nrs, layer * 7 + (n + 1))
                    nc.vector.scalar_tensor_tensor(item, item, column(ITEM_GAINS[n]), rsn[:, 0:item.shape[-1]], ALU.mult,
                                                   ALU.mult).then_inc(s_qn, 1)

                def rope(n):
                    item = items(dq, dk, sq, sk)[n]
                    dve.wait_ge(s_rot, layer * 7 + (n + 1))
                    if n == 0:
                        nc.vector.tensor_tensor(kd, halves_of(pm[:, 3, :]), both(cosB), ALU.mult).then_inc(s_kcos, 1)
                        return
                    dve.wait_ge(s_qn, layer * 7 + (n + 1))
                    link(nc.vector.tensor_tensor(halves(ta), halves_of(item), both(cosB), ALU.mult))
                    link(nc.vector.tensor_tensor(halves(tb), halves_of(pm[:, 3, :]), both(sinB), ALU.mult))
                    nc.vector.tensor_tensor(item, ta[:, :], tb[:, :], ALU.add).then_inc(s_rope, 1)
                    dve.wait_ge(s_rope, layer * 7 + (n + 1))

                def swa_k(_):
                    dve.wait_ge(s_kcos, layer + 1)
                    dve.wait_ge(s_krot, layer + 1)
                    link(nc.vector.tensor_tensor(halves(tb), halves_of(pm[:, 3, :]), both(sinB), ALU.mult))
                    nc.vector.tensor_tensor(kd, kd, halves(tb), ALU.add).then_inc(s_rope, 1)
                    dve.wait_ge(s_rope, layer * 7 + 1)

                def swa_v(_):
                    dve.wait_ge(s_svT, layer + 1)
                    nc.vector.tensor_copy(sv.rearrange("p a c -> p (a c)"), pm[:, 3, 0:2 * P]).then_inc(s_sv, 1)

                def scores(z):
                    j, zp = z % 2, z % 2
                    kw = (j + 1) * P
                    dve.wait_ge(s_sc, layer * 16 + (z + 1))
                    tail = pm[0:CHUNK, 0:2, kw - CHUNK:kw]
                    link(nc.vector.tensor_scalar(tail, tail, NEG, None, ALU.add))
                    if z >= 8:
                        link(nc.vector.tensor_reduce(st[:, zp, 8:10], pm[:, 0:2, 0:kw], AX.X, ALU.max))
                        nc.vector.tensor_scalar(st[:, zp, 0:2], st[:, zp, 8:10], -SCALE, None, ALU.mult).then_inc(s_mx, 1)
                        dve.wait_ge(s_ex, layer * 16 + (z + 1))
                        link(nc.vector.reciprocal(st[:, zp, 8:10], st[:, zp, 2:4]))
                        link(nc.vector.tensor_tensor(st[:, zp, 10:11], st[:, zp, 9:10], lam[:, 3, bass.ds(layer, 1)], ALU.mult))
                        link(nc.vector.tensor_scalar(ta[:, 0:kw], pe_buf[:, zp, 1, 0:kw], st[:, zp, 10:11], None, ALU.mult))
                        nc.vector.scalar_tensor_tensor(pe_buf[:, zp, 0, 0:kw], pe_buf[:, zp, 0, 0:kw], st[:, zp, 8:9],
                                                       ta[:, 0:kw], ALU.mult, ALU.add).then_inc(s_wt, 1)
                        dve.wait_ge(s_wt, layer * 16 + (z + 1))
                        return
                    t = z // 2
                    k0 = CHUNK * j
                    if j == 1:
                        head = pm[CHUNK:P, 0:2, k0:k0 + CHUNK]
                        link(nc.vector.tensor_scalar(head, head, NEG, None, ALU.add))
                    link(nc.vector.tensor_reduce(st[:, zp, 8:10], pm[:, 0:2, k0:kw], AX.X, ALU.max))
                    sink = sinks[:, bass.ds(layer, 1), 2 * t:2 * t + 2].rearrange("p a b -> p (a b)")
                    link(nc.vector.scalar_tensor_tensor(st[:, zp, 10:12], st[:, zp, 8:10], SCALE, sink, ALU.mult, ALU.max))
                    link(nc.vector.tensor_tensor(st[:, zp, 6:8], sink, st[:, zp, 10:12], ALU.subtract))
                    nc.vector.tensor_scalar(st[:, zp, 0:2], st[:, zp, 10:12], -1.0, None, ALU.mult).then_inc(s_mx, 1)
                    dve.wait_ge(s_ex, layer * 16 + (z + 1))
                    link(nc.vector.tensor_tensor(st[:, zp, 8:10], st[:, zp, 2:4], st[:, zp, 4:6], ALU.add))
                    link(nc.vector.reciprocal(st[:, zp, 10:12], st[:, zp, 8:10]))
                    for e in range(2):
                        pv = pe_buf[:, zp, e, k0:kw]
                        ins = nc.vector.tensor_scalar(pv, pv, st[:, zp, 10 + e:11 + e], None, ALU.mult)
                    ins.then_inc(s_wt, 1)

                def values(z):
                    if z % 2 == 1 and z < 8:
                        t = z // 2
                        dve.wait_ge(s_mhi, layer * 12 + (t + 1))
                        nc.vector.tensor_tensor(hid[:, 12 + t, 1, :], pm[:, 2, 0:S], hid[:, 12 + t, 0, :].bitcast(F32),
                                                ALU.subtract).then_inc(s_mix, 1)

                def diff_norm(hh):
                    dve.wait_ge(s_ors, layer * DIFF_H + (hh + 1))
                    nc.vector.scalar_tensor_tensor(hf[:, 0:S], pm[:, 2, 0:S], column(R_SUB), rsn[:, 0:S],
                                                   ALU.mult, ALU.mult).then_inc(s_mf, 1)
                    dve.wait_ge(s_mhi, layer * 12 + (4 + hh + 1))
                    nc.vector.tensor_tensor(hid[:, 8 + hh, 1, :], hf[:, 0:S], hid[:, 8 + hh, 0, :].bitcast(F32),
                                            ALU.subtract).then_inc(s_mix, 1)
                    dve.wait_ge(s_mix, layer * 12 + (4 + hh + 1))

                def queries(_):
                    dve.wait_ge(s_eq, layer + 1)
                    nc.vector.scalar_tensor_tensor(qg, qg, GLA_SCALE, gt, ALU.mult, ALU.mult).then_inc(s_qd, 1)

                def keys(i):
                    for idx in range(4 * i, 4 * i + 4):
                        n = idx % NBLK
                        at, width = (P, BLK * (n + 1)) if n < 8 else (0, BLK * (n + 1))
                        dve.wait_ge(s_ke, layer * 64 + (idx + 1))
                        kv = kn[:, n % 8, at:at + width]
                        nc.vector.tensor_tensor(kv, kv, kg[:, i // 4, 0:width], ALU.mult).then_inc(s_kn, 1)

                def mask(hh):
                    if hh:
                        dve.wait_ge(s_go, layer * GLA_H + hh)
                    dve.wait_ge(s_am, layer * 64 + (hh + 1) * NBLK)
                    nc.vector.tensor_tensor(att, pm[:, 3, 0:3 * P], cst[:, K_TRI:K_TRI + 3 * P], ALU.mult).then_inc(s_att, 1)

                def gla_norm(hh):
                    dve.wait_ge(s_silu, silu.at())
                    dve.wait_ge(s_grs, layer * GLA_H + (hh + 1))
                    for b in range(2):
                        ins = nc.vector.scalar_tensor_tensor(ta[:, b * S:(b + 1) * S], pm[:, 2, b * S:(b + 1) * S],
                                                             column(R_GLA + b), rsn[:, 0:S], ALU.mult, ALU.mult)
                    link(ins)
                    nc.vector.tensor_tensor(halves(hf), halves(ta), sgate[:, 2 * hh:2 * hh + 2, :], ALU.mult
                                            ).then_inc(s_mf, 1)
                    dve.wait_ge(s_mhi, layer * 12 + (8 + hh + 1))
                    nc.vector.tensor_tensor(hid[:, 2 * hh:2 * hh + 2, 1, :], halves(hf),
                                            hid[:, 2 * hh:2 * hh + 2, 0, :].bitcast(F32), ALU.subtract).then_inc(s_mix, 1)
                    dve.wait_ge(s_mix, layer * 12 + (8 + hh + 1))

                steps = dict(log_decay=log_decay, decay_sums=decay_sums, block_decay=block_decay, norm=norm_item,
                             rope=rope, swa_k=swa_k, swa_v=swa_v, scores=scores, values=values, diff_norm=diff_norm,
                             queries=queries, keys=keys, mask=mask, gla_norm=gla_norm)

                def beside(slot, n):
                    for q in range(n):
                        units(1)
                        for step, i in BESIDE.get(slot + q, ()):
                            if step in steps:
                                steps[step](i)

                units(4)
                norm.n += 1
                dve.wait_ge(s_rstd, norm.at())
                main_plus_cross(halves(ta))
                link(nc.vector.tensor_tensor(sk, ta[:, 0:S], rstdB[:, :], ALU.mult))
                nc.vector.tensor_tensor(svT, ta[:, S:2 * S], rstdB[:, :], ALU.mult).then_inc(s_ev, 1)
                evc.n += 1
                dve.wait_ge(s_ev, evc.at())
                crossed.n += 1
                dve.wait_ge(s_cross, crossed.at())
                for tt in range(TT):
                    ins = nc.vector.scalar_tensor_tensor(alr[:, tt, :], pd[:, 1, tt, 0:RANK], rstdC[:, tt:tt + 1],
                                                         cross[:, 1, tt * RANK:(tt + 1) * RANK], ALU.mult, ALU.add)
                ins.then_inc(s_psfree, 1)
                group.n += 1
                evc.n += 1
                dve.wait_ge(s_psfree, group.at(2))
                dve.sem_inc(s_ev, 1)
                slot = 4
                for dst in (sq, dq, dk):
                    for g in range(2):
                        beside(slot, 4)
                        feature_major(dst[:, 2 * g:2 * g + 2, :])
                        slot += 4
                for g in range(2):
                    beside(slot, 4)
                    token_major(lambda tt: dv[:, tt, g * G:(g + 1) * G])
                    slot += 4
                for dst in (qg, kg):
                    for g in range(2):
                        beside(slot, 4)
                        feature_major(dst[:, 2 * g:2 * g + 2, :])
                        slot += 4
                for g in range(4):
                    beside(slot, 4)
                    main_plus_cross(halves(ta))
                    link(nc.vector.tensor_tensor(sgate[:, 2 * g:2 * g + 2, :], halves(ta), both(rstdB), ALU.mult))
                    slot += 4
                silu.n += 1
                dve.sem_inc(s_gate, 1)
                for g in range(4):
                    beside(slot, 4)
                    token_major(lambda tt: vg[:, tt, g * G:(g + 1) * G])
                    slot += 4

                for g in range(2):
                    beside(slot, 2)
                    add_to_h(g)
                    slot += 2
                with turns(dve, 3, [(unit, 4), (group, 2), (chain, 2)], s_began) as i:
                    for g in range(2):
                        units(2)
                        add_to_h(i * 2 + g + 2)
                with turns(dve, 4, [(unit, 4), (group, 2), (chain, 2), (hn, 2)], s_began) as i:
                    for g in range(2):
                        units(2)
                        add_to_h(i * 2 + g)
                        dve.sem_inc(s_hnew, 1)
                        make_u(i * 2 + g, lambda j: prm[:, bass.ds(j + (lp + R_FFN), 1)])

                norm.n += 1
                for r, n in enumerate(ROUNDS):
                    with turns(dve, n // 2, [(unit, 8), (group, 2), (silu, 1), (hidc, 1), (chain, 2), (crossed, 2)], s_began) as i:
                        units(4)
                        dve.wait_ge(s_rstd, norm.at())
                        main_plus_cross(halves(tb))
                        nc.vector.tensor_tensor(halves(ta), halves(tb), both(rstdB), ALU.mult).then_inc(s_gate, 1)
                        silu.n += 1
                        dve.wait_ge(s_silu, silu.at())
                        link(nc.vector.tensor_tensor(halves(sg), halves(sg), both(rstdB), ALU.mult))
                        units(4)
                        main_plus_cross(halves(tb))
                        nc.vector.tensor_tensor(hf[:, :], tb[:, :], sg[:, :], ALU.mult).then_inc(s_hf, 1)
                        hidc.n += 1
                        dve.wait_ge(s_hidhi, hidc.at())
                        hv = bass.ds(i * 2, 2)
                        link(nc.vector.tensor_tensor(hid[:, hv, 1, :], halves(hf), hid[:, hv, 0, :].bitcast(F32),
                                                     ALU.subtract))
                        dve.sem_inc(s_hid, 1)
                    last = r == len(ROUNDS) - 1
                    per = 2 if n == 16 else 4
                    with turns(dve, 8 // per, [(unit, n // 4 * per), (group, per), (chain, per)] + [(hn, per)] * last, s_began) as i:
                        for g in range(per):
                            units(n // UK)
                            add_to_h(i * per + g)
                            if last:
                                dve.sem_inc(s_hnew, 1)
                                make_u(i * per + g, lambda j: prm[:, bass.ds(j + (lp + R_PLE), 1)])

                dve.wait_ge(s_phi, layer + 1)
                nc.vector.tensor_tensor(pT[:, :, 1, :], halves_of(pm[:, 1, :]), pT[:, :, 0, :].bitcast(F32),
                                        ALU.subtract).then_inc(s_plo, 1)
                for g in range(8):
                    if g % 2 == 0:
                        units(1)
                    main_plus_cross(pleT[:, 2 * g:2 * g + 2, :])
                norm.n += 1
                with turns(dve, 4, [(unit, 8), (group, 2), (silu, 2), (chain, 4), (crossed, 2)], s_began) as i:
                    for g in range(2):
                        units(4)
                        dve.wait_ge(s_rstd, norm.at())
                        main_plus_cross(halves(tb))
                        nc.vector.tensor_tensor(halves(ta), halves(tb), both(rstdB), ALU.mult).then_inc(s_gate, 1)
                        silu.n += 1
                        dve.wait_ge(s_silu, silu.at())
                        gv = bass.ds(i * 4 + 2 * g, 2)
                        link(nc.vector.tensor_tensor(halves(tb), halves(sg), pleT[:, gv, :], ALU.mult))
                        link(nc.vector.tensor_tensor(h[:, gv, :], h[:, gv, :], halves(tb), ALU.add))
                        dve.sem_inc(s_hnew, 1)

            for g in range(8):
                dve.wait_ge(s_tr, 10 + g)
                nc.vector.tensor_copy(xtok[:, :, g * G:(g + 1) * G], halves_of(pm[:, g % 4, :])).then_inc(s_trc, 1)

        @block.tensor
        def _(pe):
            unit, group, norm, hn, hidc = Count(), Count(), Count(), Count(), Count()

            def mm(o, a, b, start, stop):
                return nc.tensor.matmul(o, a, b, start=start, stop=stop, skip_group_check=True)

            def stationary_weights(slot, k, x_pair, par, start, stop, cols=0, width=2):
                for n in range(2):
                    c = slice(cols + n * P, cols + (n + 1) * P)
                    mm(pd[:, par, n, :], wview(slot, k, 0, c, width), x_pair, start, False)
                    ins = mm(pd[:, par, n, 0:S], wview(slot, k, 1, c, width), x_pair[:, 0:S], False, stop)
                return ins

            def wview(slot, k, part, c, width):
                if width == 2:
                    return wsp[:, slot, k, part, c]
                col = c.start
                return wsp[:, slot, 2 * k + col // G, part, col % G:col % G + P]

            def moving_weights(slot, k, x_tile, par, start, stop):
                for tt in range(TT):
                    t = slice(tt * P, (tt + 1) * P)
                    mm(pd[:, par, tt, :], x_tile[:, 0, t], wsp[:, slot, k, :, :].rearrange("p a n -> p (a n)"), start, False)
                    ins = mm(pd[:, par, tt, 0:G], x_tile[:, 1, t], wsp[:, slot, k, 0, :], False, stop)
                return ins

            def dense(operand, n_units, tokens=False, ready=None, beside=None):
                par = group.n % 2
                pe.wait_ge(s_psfree, group.at(1))
                for q in range(n_units):
                    slot = unit.n % RING
                    if beside:
                        beside(q)
                    if ready:
                        ready(q)
                    pe.wait_ge(s_lo, unit.at(1 + RING))
                    for k in range(UK):
                        kk = q * UK + k
                        first, last = kk == 0, kk == n_units * UK - 1
                        if tokens:
                            ins = moving_weights(slot, k, operand[:, kk], par, first, last)
                        else:
                            ins = stationary_weights(slot, k, operand[:, kk, :, :].rearrange("p a t -> p (a t)"), par,
                                                     first, last)
                        if k == UK - 1:
                            ins.then_inc(s_used, 1)
                    unit.n += 1
                group.n += 1

            def u_ready(q):
                pe.wait_ge(s_u, hn.at(2 * (q + 1)))

            def norm_sums(token_major):
                norm.n += 1
                pe.wait_ge(s_ssq, norm.at())
                ins = mm(pm[:, 0, 0:S], ones[:, :], ssq[:, :], True, True)
                if token_major:
                    for tt in range(TT):
                        ins = mm(pm[:, 0, S + tt:S + tt + 1], ssq[:, tt * P:(tt + 1) * P], ones[:, 0:1], True, True)
                ins.then_inc(s_nmm, 1)

            pe.sem_inc(s_used, RING)
            pe.wait_ge(s_small, n_small)
            rows_n = DEPTH * R_ALL
            nc.tensor.transpose(pm[:, 0, 0:rows_n], prm_rows[0:rows_n, :], ident[0:rows_n, 0:rows_n]).then_inc(s_tr, 1)
            pe.wait_ge(s_x, 16)
            pe.wait_ge(s_init, 2)
            for g in range(8):
                if g >= 4:
                    pe.wait_ge(s_trc, g - 3)
                for j in range(2):
                    for tt in range(TT):
                        c = (2 * g + j) * P
                        ins = nc.tensor.transpose(pm[:, g % 4, j * S + tt * P:j * S + (tt + 1) * P], xtok[:, tt, c:c + P],
                                                  ident)
                ins.then_inc(s_tr, 1)
            pe.wait_ge(s_trc, 8)

            with turns(pe, DEPTH, [(unit, UNITS_PER_LAYER), (group, GROUPS_PER_LAYER), (norm, 3), (hn, 24),
                                   (hidc, 22)], s_began) as layer:
                dense(u, 4, ready=u_ready)
                hn.n += 8
                norm_sums(True)
                pe.wait_ge(s_walr, layer * 2 + 2)
                pe.wait_ge(s_psfree, group.at(1))
                for tt in range(TT):
                    t = slice(tt * P, (tt + 1) * P)
                    for k in range(KT):
                        wv = walr[:, k, :, :].rearrange("p a n -> p (a n)")
                        mm(pd[:, 1, tt, 0:2 * RANK], u[:, k, 0, t], wv, k == 0, False)
                        ins = mm(pd[:, 1, tt, 0:RANK], u[:, k, 1, t], wv[:, 0:RANK], False, k == KT - 1)
                ins.then_inc(s_half, 1)
                group.n += 1

                def rank(_):
                    pe.wait_ge(s_ev, layer * EV + EV_RANK)
                    for tt in range(TT):
                        ins = nc.tensor.transpose(pm[0:RANK, 2, tt * P:(tt + 1) * P], alr[:, tt, :], ident)
                    ins.then_inc(s_alrT, 1)

                def logits(_):
                    pe.wait_ge(s_alrTc, layer + 1)
                    pe.wait_ge(s_lay[1], layer * 16 + 16)
                    for hh in range(GLA_H):
                        ins = mm(pm[:, hh // 2, hh % 2 * S:(hh % 2 + 1) * S], wal[:, hh * DK:(hh + 1) * DK], alrT[:, :],
                                 True, True)
                    ins.then_inc(s_xa, 1)

                def norm_item(n):
                    w = items(dq, dk, sq, sk)[n].shape[-1]
                    if n == 1:
                        pe.wait_ge(s_sv, layer + 1)
                    elif n:
                        pe.wait_ge(s_rope, layer * 7 + n)
                    pe.wait_ge(s_nsq, layer * 7 + (n + 1))
                    mm(pm[:, 3, 0:w], cst[:, K_BLK:K_BLK + P], nsq[:, 0:w], True, True).then_inc(s_nss, 1)

                def rope(n):
                    item = items(dq, dk, sq, sk)[n]
                    pe.wait_ge(s_qn, layer * 7 + (n + 1))
                    if n:
                        mm(pm[:, 3, :], cst[:, K_ROT:K_ROT + P], item, True, True).then_inc(s_rot, 1)
                    else:
                        for g in range(2):
                            ins = mm(pm[:, 3, g * S:(g + 1) * S], cst[:, K_SEL + g * P:K_SEL + (g + 1) * P], item, True, True)
                        ins.then_inc(s_rot, 1)

                def swa_k(_):
                    pe.wait_ge(s_kcos, layer + 1)
                    for g in range(2):
                        ins = mm(pm[:, 3, g * S:(g + 1) * S], cst[:, K_RSEL + g * P:K_RSEL + (g + 1) * P], sk, True, True)
                    ins.then_inc(s_krot, 1)

                def swa_v(_):
                    pe.wait_ge(s_rope, layer * 7 + 1)
                    for tt in range(TT):
                        ins = nc.tensor.transpose(pm[:, 3, tt * P:(tt + 1) * P], svT[:, tt * P:(tt + 1) * P], ident)
                    ins.then_inc(s_svT, 1)

                def scores(z):
                    j, half = z % 2, z // 2
                    kw = (j + 1) * P
                    if z == 0:
                        pe.wait_ge(s_xs, layer + 1)
                    elif j == 0:
                        pe.wait_ge(s_mix, layer * 12 + half)
                    if z < 8:
                        pe.wait_ge(s_rope, layer * 7 + (2 + half // 2))
                    else:
                        pe.wait_ge(s_rope, layer * 7 + (6 + (half - 4) // 2))
                    for e in range(2):
                        r = slice(e * HD, (e + 1) * HD)
                        if z < 8:
                            k0 = CHUNK * j
                            ins = mm(pm[:, e, k0:kw], sq[r, half, j * P:(j + 1) * P], kd[r, half // 2, k0:kw], True, True)
                        else:
                            ins = mm(pm[:, e, 0:kw], dq[r, half - 4, j * P:(j + 1) * P], dk[r, half - 4, 0:kw], True, True)
                    ins.then_inc(s_sc, 1)

                def transpose(z):
                    j = z % 2
                    pe.wait_ge(s_wt, layer * 16 + (z + 1))
                    for e in range(2 if z < 8 else 1):
                        for kt in range(j + 1):
                            c = (2 * e + kt) * P
                            ins = nc.tensor.transpose(pm[:, 0, c:c + P], pe_buf[:, j, e, kt * P:(kt + 1) * P], ident)
                    ins.then_inc(s_tp, 1)

                def values(z):
                    j = z % 2
                    if z < 8:
                        pe.wait_ge(s_sv, layer + 1)
                    else:
                        pe.wait_ge(s_ev, layer * EV + EV_DV)
                    pe.wait_ge(s_tpc, layer * 16 + (z + 1))
                    for e in range(2 if z < 8 else 1):
                        for kt in range(j + 1):
                            if z < 8:
                                g = z // 4
                                ins = mm(pm[e * HD:(e + 1) * HD, 2, j * P:(j + 1) * P], sv[:, kt, g * HD:(g + 1) * HD],
                                         wT[:, j, 2 * e + kt, :], kt == 0, kt == j)
                            else:
                                hh = z // 2 - 4
                                ins = mm(pm[:, 2, j * P:(j + 1) * P], dv[:, kt, hh * P:(hh + 1) * P], wT[:, j, kt, :],
                                         kt == 0, kt == j)
                    if j == 1:
                        ins.then_inc(s_pv, 1)

                def diff_norm(hh):
                    pe.wait_ge(s_osq, layer * DIFF_H + (hh + 1))
                    mm(pm[:, 0, 0:S], ones[:, :], osq, True, True).then_inc(s_oss, 1)

                def blocks(i):
                    hh = i // 4
                    if i == 0:
                        pe.wait_ge(s_qd, layer + 1)
                    elif i % 4 == 0:
                        pe.wait_ge(s_att, layer * GLA_H + hh)
                    for idx in range(4 * i, 4 * i + 4):
                        n = idx % NBLK
                        pe.wait_ge(s_kn, layer * 64 + (idx + 1))
                        q = qg[:, hh, BLK * n:BLK * (n + 1)]
                        if n < 8:
                            ins = mm(pm[:, 3, BLK * n:BLK * (n + 1)], kn[:, n, P:2 * P], q, True, True)
                        else:
                            mm(pm[:, 3, BLK * n:BLK * (n + 1)], kn[:, n - 8, 0:P], q, True, True)
                            ins = mm(pm[:, 3, S + BLK * (n - 8):S + BLK * (n - 7)], kn[:, n - 8, P:2 * P], q, True, True)
                        ins.then_inc(s_am, 1)

                def gla_out(hh):
                    pe.wait_ge(s_mf, layer * 8 + (DIFF_H + hh))
                    pe.wait_ge(s_ev, layer * EV + (EV_GV + hh + 1))
                    pe.wait_ge(s_att, layer * GLA_H + (hh + 1))
                    for vb in range(2):
                        c = hh * DV + vb * P
                        mm(pm[:, 2, vb * S:(vb + 1) * S], vg[:, 0, c:c + P], att[:, 0:S], True, False)
                        ins = mm(pm[:, 2, vb * S + P:(vb + 1) * S], vg[:, 1, c:c + P], att[:, S:S + P], False, True)
                    ins.then_inc(s_go, 1)

                def gla_norm(hh):
                    pe.wait_ge(s_gsq, layer * GLA_H + (hh + 1))
                    mm(pm[:, 0, 0:S], ones[:, :], pe_buf[:, 0, 0, :], True, False)
                    mm(pm[:, 0, 0:S], ones[:, :], pe_buf[:, 0, 1, :], False, True).then_inc(s_gss, 1)

                steps = dict(rank=rank, logits=logits, norm=norm_item, rope=rope, swa_k=swa_k, swa_v=swa_v,
                             scores=scores, transpose=transpose, values=values, diff_norm=diff_norm, blocks=blocks,
                             gla_out=gla_out, gla_norm=gla_norm)

                def beside(slot):
                    for step, i in BESIDE.get(slot, ()):
                        if step in steps:
                            steps[step](i)

                for g in range(1, 21):
                    dense(u, 4, tokens=g in BY_TOKEN, beside=lambda q: beside(4 * g + q))

                pe.wait_ge(s_mix, layer * 12 + 8)
                for g in range(2):
                    dense(hid[:, 8:16], 2, beside=lambda q: beside(84 + 2 * g + q))
                with turns(pe, 3, [(unit, 4), (group, 2)], s_began):
                    dense(hid[:, 8:16], 2)
                    dense(hid[:, 8:16], 2)
                pe.wait_ge(s_mix, layer * 12 + 12)
                with turns(pe, 4, [(unit, 4), (group, 2)], s_began):
                    dense(hid, 2)
                    dense(hid, 2)

                for r, n in enumerate(ROUNDS):
                    pairs = n // 2
                    if r == 0:
                        dense(u, 4, ready=u_ready)
                        hn.n += 8
                        norm_sums(False)
                        dense(u, 4)
                        pairs -= 1
                    with turns(pe, pairs, [(unit, 8), (group, 2)], s_began):
                        dense(u, 4)
                        dense(u, 4)

                    def hid_ready(q):
                        pe.wait_ge(s_hid, hidc.at(2 * (q + 1)))

                    per = 2 if n == 16 else 4
                    dense(hid, n // UK, ready=hid_ready)
                    for _ in range(per - 1):
                        dense(hid, n // UK)
                    with turns(pe, 8 // per - 1, [(unit, n // 4 * per), (group, per)], s_began):
                        for _ in range(per):
                            dense(hid, n // UK)
                    hidc.n += n // 2

                pe.wait_ge(s_lay[2], layer * 16 + 16)
                for j in range(2):
                    for tt in range(TT):
                        ins = nc.tensor.transpose(pm[:, 1, j * S + tt * P:j * S + (tt + 1) * P],
                                                  ptok[:, tt, j * P:(j + 1) * P], ident)
                ins.then_inc(s_p, 1)
                pe.wait_ge(s_plo, layer + 1)
                for g in range(8):
                    par = group.n % 2
                    pe.wait_ge(s_psfree, group.at(1))
                    if g % 2 == 0:
                        pe.wait_ge(s_lo, unit.at(1 + RING))
                    for k in range(2):
                        xp = pT[:, k, :, :].rearrange("p a t -> p (a t)")
                        ins = stationary_weights(unit.n % RING, k, xp, par, k == 0, k == 1, cols=g % 2 * G, width=4)
                    if g % 2 == 1:
                        ins.then_inc(s_used, 1)
                        unit.n += 1
                    else:
                        ins.then_inc(s_half, 1)
                    group.n += 1
                dense(u, 4, ready=u_ready)
                hn.n += 8
                norm_sums(False)
                dense(u, 4)
                with turns(pe, 3, [(unit, 8), (group, 2)], s_began):
                    dense(u, 4)
                    dense(u, 4)

            pe.wait_ge(s_hnew, 8 + 24 * DEPTH)
            for g in range(8):
                if g >= 4:
                    pe.wait_ge(s_trc, 8 + g - 3)
                for tt in range(TT):
                    for j in range(2):
                        ins = nc.tensor.transpose(pm[:, g % 4, tt * S + j * P:tt * S + (j + 1) * P],
                                                  h[:, 2 * g + j, tt * P:(tt + 1) * P], ident)
                ins.then_inc(s_tr, 1)


LN_EXP = "natural_log_exp_and_others"
ACT_LINKS = 23
DVE_LINKS = 216


def items(dq, dk, sq, sk):
    def pair(t, n):
        return t[:, 2 * n:2 * n + 2, :].rearrange("p a t -> p (a t)")
    return [sk, pair(sq, 0), pair(sq, 1), pair(dq, 0), pair(dq, 1), pair(dk, 0), pair(dk, 1)]


ITEM_GAINS = (R_SK, R_SQ, R_SQ, R_DQ, R_DQ, R_DK, R_DK)
BY_TOKEN = (7, 8, 17, 18, 19, 20)
BESIDE = schedule()


INPUTS = ["x", "p", "positions", "norm_mix_g", "w_in", "gla_w_alpha", "gla_b_alpha", "gla_norm_g",
          "diff_q_norm_g", "diff_k_norm_g", "diff_lambda_q1", "diff_lambda_k1", "diff_lambda_q2",
          "diff_lambda_k2", "diff_subln_g", "swa_q_norm_g", "swa_k_norm_g", "swa_sinks", "w_out",
          "norm_ffn_g", "w_ffn_in", "w_ffn_out", "norm_ple_g", "w_ple_gate", "w_ple_proj"]


def constants():
    import math

    import numpy as np
    c = np.zeros((P, K_COLS), np.float32)
    c[:, K_ID:K_ID + P] = np.eye(P)
    rot = np.zeros((P, P), np.float32)
    for m in range(P):
        d = m % HD
        if d < HALF:
            rot[m + HALF, m] = -1.0
        else:
            rot[m - HALF, m] = 1.0
    c[:, K_ROT:K_ROT + P] = rot
    for g in range(SWA_KV):
        sel = np.zeros((P, P), np.float32)
        for m in range(P):
            sel[g * HD + m % HD, m] = 1.0
        c[:, K_SEL + g * P:K_SEL + (g + 1) * P] = sel
        c[:, K_RSEL + g * P:K_RSEL + (g + 1) * P] = rot @ sel
    head = np.arange(P) // HD
    c[:, K_BLK:K_BLK + P] = (head[:, None] == head[None, :]) / HD
    tri = np.arange(P)[:, None] <= np.arange(P)[None, :]
    c[:, K_TRI:K_TRI + 3 * P] = np.concatenate([tri, np.ones((P, P)), tri], axis=1)
    inv = np.float32(1.0) / np.float32(10000.0) ** (np.arange(0, HD, 2, dtype=np.float32) / np.float32(HD))
    c[:, K_INV] = inv.astype(np.float32)[np.arange(P) % HALF]
    for i in range(DEPTH):
        c[:, K_LAM + i] = 0.8 - 0.6 * math.exp(-0.3 * i)
        c[:, K_ONE_LAM + i] = 1.0 - (0.8 - 0.6 * math.exp(-0.3 * i))
    return c


def kernel(**inputs):
    import numpy as np

    import concourse.bacc as bacc
    from concourse.bass_utils import run_bass_kernel_spmd as run

    nc = bacc.Bacc("TRN2", target_bir_lowering=False, num_devices=1)
    arrays = {f"in_{n}": np.ascontiguousarray(inputs[n]) for n in INPUTS}
    arrays["in_consts"] = constants()
    args = [nc.dram_tensor(n, a.shape, mybir.dt.from_np(a.dtype), kind="ExternalInput").ap() for n, a in arrays.items()]
    out = nc.dram_tensor("out", (1, S, D), F32, kind="ExternalOutput").ap()
    build(nc, *args, out)
    return run(nc, [arrays], core_ids=[0]).results[0]["out"]
```

```python
from contextlib import ExitStack, contextmanager

import concourse.bass as bass
from concourse import mybir

F32 = mybir.dt.float32
F32R = mybir.dt.float32r
I32 = mybir.dt.int32
ALU = mybir.AluOpType
ACT = mybir.ActivationFunctionType
AX = mybir.AxisListType

P = 128
D = 2048
S = 256
DEPTH = 2
HD = 64
HALF = HD // 2
CHUNK = 64
EPS = 1e-6
NEG = -1e30

GLA_H, DK, DV, RANK, BLK = 4, 128, 256, 16, 16
GLA_TAU = 16.0
DIFF_H = 4
SWA_H, SWA_KV = 8, 2
N_IN = 5392
MIX = 2048
D_FF = 5632
PLE = 256

KT = D // P
TT = S // P
G = 256
UK = 4
NBLK = S // BLK
SCALE = HD ** -0.5
GLA_SCALE = DK ** -0.5

C_GQ = 0
C_GV = 2 * GLA_H * DK
C_GATE = C_GV + GLA_H * DV
C_ALR = 2 * GLA_H * DK + 2 * GLA_H * DV
C_DQ = C_ALR + RANK
C_SKV = N_IN - 2 * SWA_KV * HD
C_SQ = C_SKV - SWA_H * HD

ROUNDS = (16, 16, 12)
assert sum(ROUNDS) * P == D_FF

UNITS_WIN = 21 * 4
UNITS_PER_LAYER = UNITS_WIN + 2 * 8 * 2 + sum(ROUNDS) * 4 + sum(ROUNDS) // UK * 8 + 4 + 8 * 4
GROUPS_PER_LAYER = 22 + 16 + sum(ROUNDS) + 8 * len(ROUNDS) + 8 + 8
CROSSED = 22 + sum(ROUNDS) + 16
EV = 18
EV_RANK, EV_DV, EV_GV = 2, 10, 14
EV_ITEM = (1, 3, 4, 5, 6, 7, 8)
AHEAD = 3
RING = 4

K_ID, K_INV, K_LAM, K_ONE_LAM = 0, 128, 129, 131
K_FIRST = 133
K_ROT, K_SEL, K_RSEL, K_BLK, K_TRI = 133, 261, 517, 773, 901
K_COLS = 1285

R_MIX, R_FFN, R_PLE = (0, KT), (2 * KT, KT), (4 * KT, KT)
R_BAL, R_GLA, R_SUB = (96, GLA_H), (104, DV // P), (108, 1)
R_DQ, R_DK, R_SQ, R_SK = (110, 1), (112, 1), (114, 1), (116, 1)
R_ALL = 118

INV_2PI = 0.15915494309189535
PI2_A, PI2_B = 6.28125, 0.0019350051879882812
PI2_C = 6.283185307179586 - PI2_A - PI2_B
MAGIC = 12582912.0
PI_LO = 3.1415925


def schedule():
    beside = {}

    def at(slot, step, i=0):
        beside.setdefault(slot, []).append((step, i))

    for z in range(16):
        first = 15 + 3 * z if z < 8 else 39 + 7 * ((z - 8) // 2) + 3 * (z % 2)
        for n, step in ((0, "scores"), (0, "weights"), (2, "transpose"), (3, "values")):
            at(first + n, step, z)
    for hh in range(DIFF_H):
        at(46 + 7 * hh, "diff_norm", hh)
    for n, slots in enumerate(((5, 6, 7), (9, 10, 11), (12, 13, 14), (16, 18, 19), (20, 21, 22), (24, 27, 28), (28, 30, 31))):
        for slot, step in zip(slots, ("squares", "norm", "rope")):
            at(slot, step, n)
    at(8, "swa_k")
    at(9, "swa_v")
    for slot, step in ((8, "logits"), (34, "exp_abs"), (37, "log1p"), (41, "log_decay"), (44, "decay_sums"),
                       (45, "block_decay"), (47, "decay_exp"), (54, "far_decay")):
        at(slot, step)
    at(55, "queries")
    at(58, "far_keys")
    at(68, "gate")
    for i in range(4 * GLA_H):
        at(67 + i if i > 1 else (61, 64)[i], "keys", i)
        at(69 + i, "blocks", i)
    for hh in range(GLA_H):
        at(72 + 4 * hh, "mask", hh)
        at(73 + 4 * hh, "gla_out", hh)
        at(74 + 4 * hh, "gla_norm", hh)
    return beside


def steps_before(step, n):
    mine, other = ("transpose", "rope") if step == "transpose" else ("norm", "transpose")
    slot = next(slot for slot, work in BESIDE.items() if (mine, n) in work)
    return sum(kind == other for s, work in BESIDE.items() if s < slot for kind, _ in work)


class Count:

    def __init__(self):
        self.n, self.terms = 0, []

    def at(self, k=0):
        value = self.n + k
        for reg, per in self.terms:
            value = reg * per + value
        return value


def turns(eng, times, counts, began):
    @contextmanager
    def run():
        starts = [c.n for c, _ in counts]
        eng.sem_inc(began, 1)
        with eng.Fori(0, times) as i:
            for c, per in counts:
                c.terms.append((i, per))
            yield i
            for (c, per), n0 in zip(counts, starts):
                assert c.n - n0 == per, (c.n - n0, per)
                c.terms.pop()
                c.n = n0 + per * times
    return run()


def build(nc, x, p, positions, norm_mix_g, w_in, gla_w_alpha, gla_b_alpha, gla_norm_g, diff_q_norm_g,
          diff_k_norm_g, diff_lambda_q1, diff_lambda_k1, diff_lambda_q2, diff_lambda_k2, diff_subln_g,
          swa_q_norm_g, swa_k_norm_g, swa_sinks, w_out, norm_ffn_g, w_ffn_in, w_ffn_out, norm_ple_g,
          w_ple_gate, w_ple_proj, consts, out):
    ctx = ExitStack()
    with ctx:
        def sb(name, shape, dt=F32):
            return ctx.enter_context(nc.sbuf_tensor(name, shape, dt))

        def sem(name):
            return ctx.enter_context(nc.semaphore(name))

        def over(name, shape, dt, offset):
            return nc.alloc_sbuf_tensor_at(name, shape, dt, offset=offset)

        hid_at = -(-nc.sbuf_base // 32) * 32
        hid = sb("hid", [P, KT, 2, S], F32R)
        h = sb("h", [P, KT, S])
        u = sb("u", [P, KT, 2, S], F32R)
        raw = sb("raw", [P, RING, UK * G])
        wsp = sb("wsp", [P, RING, UK, 2, G], F32R)
        wide = sb("wide", [P, 2 * D])
        cst = sb("cst", [P, K_COLS])
        prm = sb("prm", [P, R_ALL])
        ones = sb("ones", [P, P])
        epst = sb("epst", [P, 2])
        walr_raw = sb("walr_raw", [P, KT, RANK])
        walr = sb("walr", [P, KT, 2, RANK], F32R)
        wal = sb("wal", [2 * RANK, GLA_H * DK])
        lam = sb("lam", [P, 4, DEPTH])
        sinks = sb("sinks", [P, DEPTH, SWA_H])
        trig = sb("trig", [P, 2, S])
        sinB, cosB = trig[:, 0, :], trig[:, 1, :]
        rstdB = sb("rstdB", [P, S])
        rstdC = sb("rstdC", [P, TT])
        sqt = sb("sqt", [P, S])
        ssq = sb("ssq", [P, S])
        cross = sb("cross", [P, 2, 2 * S])
        ta = sb("ta", [P, 2 * S])
        tb = sb("tb", [P, 2 * S])
        sg = sb("sg", [P, 2 * S])
        hf = sb("hf", [P, 2 * S])
        rsn = sb("rsn", [P, 2 * S])
        lnt = sg
        bc = sb("bc", [P, GLA_H, S + 1])
        pe_buf = sb("pe_buf", [P, 2, 2, S])
        xss = sb("xss", [P, 2, TT])
        st = sb("st", [P, 2, 16])

        gl = over("gl", [P, GLA_H, 4 * S], F32, hid_at)
        qg, kg, gt = gl[:, :, 0:S], gl[:, :, S:2 * S], gl[:, :, 2 * S:3 * S]
        sk, svT = gl[:, 0, 3 * S:4 * S], gl[:, 1, 3 * S:4 * S]
        att = gl[:, 3, 2 * S:2 * S + 3 * P]
        prm_rows = over("prm_rows", [P, P], F32, hid_at)
        pos_i = over("pos_i", [P, S], I32, hid_at + 1024)
        lamv = over("lamv", [P, 4, DEPTH, HD], F32, hid_at + 4096)
        xsq = over("xsq", [P, D // 2], F32, hid_at + 8192)
        lamp = over("lamp", [P, 2, DEPTH, HD], F32, hid_at + 6144)

        kn = sb("kn", [P, 8, P])
        kfar = sb("kfar", [P, GLA_H, P])
        qfar = sb("qfar", [P, GLA_H, P])
        bneg = sb("bneg", [P, GLA_H, 1])

        dq_at = -(-nc.sbuf_base // 32) * 32
        dq = sb("dq", [P, DIFF_H, S])
        dk = sb("dk", [P, DIFF_H, S])
        dv = sb("dv", [P, TT, DIFF_H * P])
        sq = sb("sq", [P, SWA_H // 2, S])
        ptok = over("ptok", [P, TT, PLE], F32, dq_at)
        pT = over("pT", [P, 2, 2, S], F32R, dq_at + 4096)
        alrT = sb("alrT", [2 * RANK, S])

        vg = wide[:, 0:D].rearrange("p (t c) -> p t c", t=TT)
        sgate = wide[:, D:2 * D].rearrange("p (j t) -> p j t", t=S)
        pleT = wide[:, :].rearrange("p (j t) -> p j t", t=S)
        xtok = wide[:, :].rearrange("p (t c) -> p t c", t=TT)
        kd = wide[:, 0:2 * S].rearrange("p (g t) -> p g t", g=2)
        sv = wide[:, 2 * S:3 * S].rearrange("p (a c) -> p a c", a=TT)
        wT = wide[:, 3 * S:7 * S].rearrange("p (b e t) -> p b e t", b=2, e=4)
        osq = wide[:, 7 * S:8 * S]
        nsq = wide[:, D:D + 2 * S]

        ident = cst[:, K_ID:K_ID + P]

        pd = ctx.enter_context(nc.psum_tensor("pd", [P, 2, 2, 512], F32))
        pm = ctx.enter_context(nc.psum_tensor("pm", [P, 4, 512], F32))

        s_began = sem("s_began")
        s_small = sem("s_small")
        s_cst = sem("s_cst")
        s_gain = sem("s_gain")
        s_xss = sem("s_xss")
        s_rest = sem("s_rest")
        s_lamv = sem("s_lamv")
        s_pos = sem("s_pos")
        s_x = [sem(f"s_x{i}") for i in range(2)]
        s_raw = [sem(f"s_raw{i}") for i in range(RING)]
        s_hi = sem("s_hi")
        s_lo = sem("s_lo")
        s_used = sem("s_used")
        s_half = sem("s_half")
        s_lay = [sem(f"s_lay{i}") for i in range(3)]
        s_walr = sem("s_walr")
        s_p = sem("s_p")
        s_phi = sem("s_phi")
        s_plo = sem("s_plo")
        s_psfree = sem("s_psfree")
        s_cross = sem("s_cross")
        s_hnew = sem("s_hnew")
        s_uhi = sem("s_uhi")
        s_u = sem("s_u")
        s_sqt = sem("s_sqt")
        s_ssq = sem("s_ssq")
        s_nmm = sem("s_nmm")
        s_rstd = sem("s_rstd")
        s_dve = sem("s_dve")
        s_act = sem("s_act")
        s_init = sem("s_init")
        s_inita = sem("s_inita")
        s_tr = sem("s_tr")
        s_trc = sem("s_trc")
        s_gate = sem("s_gate")
        s_silu = sem("s_silu")
        s_hf = sem("s_hf")
        s_hidhi = sem("s_hidhi")
        s_hid = sem("s_hid")
        s_ev = sem("s_ev")
        s_xa = sem("s_xa")
        s_xc = sem("s_xc")
        s_xs = sem("s_xs")
        s_la = sem("s_la")
        s_bd = sem("s_bd")
        s_eq = sem("s_eq")
        s_qd = sem("s_qd")
        s_far = sem("s_far")
        s_kfar = sem("s_kfar")
        s_ke = sem("s_ke")
        s_kn = sem("s_kn")
        s_am = sem("s_am")
        s_att = sem("s_att")
        s_go = sem("s_go")
        s_gsq = sem("s_gsq")
        s_gss = sem("s_gss")
        s_grs = sem("s_grs")
        s_mf = sem("s_mf")
        s_mhi = sem("s_mhi")
        s_mix = sem("s_mix")
        s_nsq = sem("s_nsq")
        s_nss = sem("s_nss")
        s_nrs = sem("s_nrs")
        s_qn = sem("s_qn")
        s_rot = sem("s_rot")
        s_rope = sem("s_rope")
        s_kcos = sem("s_kcos")
        s_krot = sem("s_krot")
        s_svT = sem("s_svT")
        s_sv = sem("s_sv")
        s_sc = sem("s_sc")
        s_mx = sem("s_mx")
        s_ex = sem("s_ex")
        s_wt = sem("s_wt")
        s_tp = sem("s_tp")
        s_tpc = sem("s_tpc")
        s_pv = sem("s_pv")
        s_osq = sem("s_osq")
        s_oss = sem("s_oss")
        s_ors = sem("s_ors")
        s_out = sem("s_out")

        block = ctx.enter_context(nc.Block())

        @block.sync
        def _(sp):
            unit = Count()

            def load(dst_slot, src, shape):
                sp.wait_ge(s_lo, unit.at(1))
                sp.dma_start(raw[:, dst_slot, :].rearrange(shape[0], **shape[1]), src).then_inc(s_raw[dst_slot], 16)
                unit.n += 1

            def rows(w, layer, r0, c0):
                return w[layer, bass.ds(r0 * P, UK * P), bass.ds(c0, G)].rearrange("(k p) n -> p k n", p=P)

            kn_shape = ("p (k n) -> p k n", dict(k=UK))

            sp.dma_start(cst[:, 0:K_FIRST], consts[:, 0:K_FIRST]).then_inc(s_cst, 16)
            sp.dma_start(pos_i[:, :], positions.to_broadcast([P, S])).then_inc(s_pos, 16)
            sp.dma_start(prm_rows[0:DEPTH * KT, :], norm_mix_g.rearrange("l (j p) -> (l j) p", p=P)).then_inc(s_gain, 16)
            for c in range(2):
                sp.dma_start(xtok[:, :, c * D // 2:(c + 1) * D // 2],
                             x.rearrange("b (t p) c -> p (b t) c", p=P)[:, :, c * D // 2:(c + 1) * D // 2]
                             ).then_inc(s_x[c], 16)
            for (r, n), src in ((R_FFN, norm_ffn_g), (R_PLE, norm_ple_g)):
                sp.dma_start(prm_rows[r:r + DEPTH * n, :], src.rearrange("l (j p) -> (l j) p", p=P)).then_inc(s_rest, 16)
            sp.dma_start(cst[:, K_FIRST:], consts[:, K_FIRST:]).then_inc(s_rest, 16)

            with turns(sp, DEPTH, [(unit, UNITS_PER_LAYER)], s_began) as layer:
                for c in (C_SKV, C_SQ, C_SQ + G):
                    for k in range(4):
                        load(k, rows(w_in, layer, k * UK, c), kn_shape)
                    if c == C_SKV:
                        sp.wait_ge(s_hnew, layer * 24 + 1)
                        sp.dma_start(walr_raw[:, :, :], w_in[layer, :, C_ALR:C_ALR + RANK].rearrange("(k p) n -> p k n", p=P)
                                     ).then_inc(s_lay[0], 16)
                        for part in range(2):
                            sp.dma_start(wal[part * RANK:(part + 1) * RANK, :], gla_w_alpha[layer, :, :]
                                         ).then_inc(s_lay[1], 16)
                for c, times in ((C_DQ, 6), (C_GQ, 4), (C_GATE, 4), (C_GV, 4)):
                    with turns(sp, times, [(unit, 4)], s_began) as i:
                        for k in range(4):
                            load(k, rows(w_in, layer, k * UK, i * G + c), kn_shape)
                for r in (8, 0):
                    with turns(sp, 4, [(unit, 4)], s_began) as i:
                        for g in range(2):
                            for k in range(2):
                                load(2 * g + k, rows(w_out, layer, r + k * UK, i * 2 * G + g * G), kn_shape)
                done = 0
                for r, n in enumerate(ROUNDS):
                    if r == 1:
                        sp.wait_ge(s_hnew, layer * 24 + 16)
                        sp.dma_start(ptok[:, :, :], p[layer, 0, :, :].rearrange("(t p) c -> p t c", p=P)
                                     ).then_inc(s_lay[2], 16)
                    with turns(sp, n // 2, [(unit, 8)], s_began) as i:
                        for c0 in (0, D_FF):
                            for k in range(4):
                                load(k, rows(w_ffn_in, layer, k * UK, i * G + (c0 + done * P)), kn_shape)
                    if n == 16:
                        with turns(sp, 8, [(unit, 4)], s_began) as i:
                            for k in range(4):
                                load(k, rows(w_ffn_out, layer, done + k * UK, i * G), kn_shape)
                    else:
                        with turns(sp, 2, [(unit, 12)], s_began) as i:
                            for g in range(4):
                                for k in range(3):
                                    load((3 * g + k) % RING, rows(w_ffn_out, layer, done + k * UK, i * 4 * G + g * G),
                                         kn_shape)
                    done += n
                for k in range(4):
                    load(k, w_ple_proj[layer, :, k * 2 * G:(k + 1) * 2 * G].rearrange("(k p) n -> p k n", p=P),
                         ("p (k n) -> p k n", dict(k=2)))
                with turns(sp, 8, [(unit, 4)], s_began) as i:
                    for k in range(4):
                        load(k, rows(w_ple_gate, layer, k * UK, i * G), kn_shape)
            for k in range(AHEAD):
                sp.wait_ge(s_lo, unit.at(1 + k))
                sp.sem_inc(s_raw[k], 16)
            for g in range(8):
                sp.wait_ge(s_trc, g + 1)
                sp.dma_start(out.rearrange("b (t p) c -> p (b t) c", p=P)[:, :, g * G:(g + 1) * G],
                             xtok[:, :, g * G:(g + 1) * G]).then_inc(s_out, 16)
            sp.wait_ge(s_out, 8 * 16)

        n_small = 16 * (3 + 4 + 1)

        @block.gpsimd
        def _(pool):
            norm = Count()
            step = Count()

            def squares():
                with turns(pool, 8, [(step, 4)], s_began) as g:
                    pool.wait_ge(s_hnew, norm.at() * 8 + g + 1)
                    for j in range(2):
                        hv = h[:, bass.ds(2 * g + j, 1), :].rearrange("p j t -> p (j t)")
                        nc.gpsimd.tensor_tensor(sqt[:, :], hv, hv, ALU.mult).then_inc(s_sqt, 1)
                        pool.wait_ge(s_sqt, step.at(1))
                        nc.gpsimd.tensor_tensor(ssq[:, :], ssq[:, :], sqt[:, :], ALU.add).then_inc(s_sqt, 1)
                        step.n += 2
                        pool.wait_ge(s_sqt, step.at())
                pool.sem_inc(s_ssq, 1)
                norm.n += 1

            for (r, n), src in ((R_BAL, gla_b_alpha), (R_GLA, gla_norm_g), (R_SUB, diff_subln_g)):
                pool.dma_start(prm_rows[r:r + DEPTH * n, :], src.rearrange("l (j p) -> (l j) p", p=P)).then_inc(s_small, 16)
            for (r, _), src in ((R_DQ, diff_q_norm_g), (R_DK, diff_k_norm_g), (R_SQ, swa_q_norm_g), (R_SK, swa_k_norm_g)):
                pool.dma_start(prm_rows[r:r + DEPTH, :].rearrange("l (c h) -> l c h", c=2),
                               src.unsqueeze(1).to_broadcast([DEPTH, 2, HD])).then_inc(s_small, 16)
            pool.dma_start(sinks[:, :, :].rearrange("p l h -> p (l h)"),
                          swa_sinks.rearrange("(a l) h -> a (l h)", a=1).to_broadcast([P, DEPTH * SWA_H])
                          ).then_inc(s_small, 16)
            for n, src in enumerate((diff_lambda_q1, diff_lambda_k1, diff_lambda_q2, diff_lambda_k2)):
                pool.dma_start(lamv[:, n, :, :].rearrange("p l h -> p (l h)"),
                              src.rearrange("(a l) h -> a (l h)", a=1).to_broadcast([P, DEPTH * HD])
                              ).then_inc(s_lamv, 16)
            norm.n = 1
            with turns(pool, DEPTH, [(norm, 3), (step, 3 * 33)], s_began) as layer:
                for n in range(3):
                    pool.wait_ge(s_nmm, norm.at())
                    pool.sem_inc(s_began, 1)
                    nc.gpsimd.memset(ssq[:, :], 0.0).then_inc(s_sqt, 1)
                    step.n += 1
                    pool.wait_ge(s_sqt, step.at())
                    squares()

        @block.scalar
        def _(act):
            unit, group, norm, hn, chain = Count(), Count(), Count(), Count(), Count()
            silu, hidc = Count(), Count()

            def link(ins):
                chain.n += 1
                ins.then_inc(s_act, 1)
                act.wait_ge(s_act, chain.at())

            def split(slot):
                act.wait_ge(s_used, unit.at(1))
                act.wait_ge(s_raw[slot], raw_landed(slot))
                nc.scalar.activation(wsp[:, slot, :, 0, :], raw[:, slot, :].rearrange("p (k n) -> p k n", k=UK),
                                     ACT.Copy).then_inc(s_hi, 1)
                unit.n += 1

            def raw_landed(slot):
                assert unit.n % RING == slot
                value = (unit.n // RING + 1) * 16
                for reg, per in unit.terms:
                    assert per % RING == 0
                    value = reg * (per // RING * 16) + value
                return value

            def units(n):
                for _ in range(n):
                    split(unit.n % RING)

            def take_cross(scale=None, done=None):
                par = group.n % 2
                act.wait_ge(*(done or (s_used, unit.at(1))))
                if scale is None:
                    nc.scalar.activation(cross[:, par, :].rearrange("p (a t) -> p a t", a=2),
                                         pd[:, par, :, S:2 * S], ACT.Copy).then_inc(s_cross, 1)
                else:
                    for tt in range(TT):
                        ins = nc.scalar.activation(cross[:, par, tt * S:(tt + 1) * S], pd[:, par, tt, S:2 * S],
                                                   ACT.Copy, scale=rstdC[:, tt:tt + 1])
                    ins.then_inc(s_cross, 1)
                group.n += 1

            def make_u(g, gain, wait):
                act.wait_ge(s_hnew, wait)
                for j in range(2):
                    ins = nc.scalar.activation(u[:, bass.ds(2 * g + j, 1), 0, :], h[:, bass.ds(2 * g + j, 1), :],
                                               ACT.Copy, scale=gain(2 * g + j))
                ins.then_inc(s_uhi, 1)

            def rms(token_major):
                nc.scalar.preload_act_table_set(LN_EXP)
                norm.n += 1
                act.wait_ge(s_nmm, norm.at())
                link(nc.scalar.activation(rstdB[:, :], pm[:, 0, 0:S], ACT.Ln, scale=1.0 / D, bias=epst[:, 0:1]))
                if token_major:
                    link(nc.scalar.activation(rstdC[:, :], pm[:, 0, S:S + TT], ACT.Ln, scale=1.0 / D,
                                              bias=epst[:, 0:1]))
                    link(nc.scalar.activation(rstdC[:, :], rstdC[:, :], ACT.Exp, scale=-0.5))
                nc.scalar.activation(rstdB[:, :], rstdB[:, :], ACT.Exp, scale=-0.5).then_inc(s_rstd, 1)
                act.wait_ge(s_rstd, norm.at())

            def x_squares(c):
                act.wait_ge(s_x[c], 16)
                for tt in range(TT):
                    link(nc.scalar.activation(xsq[:, :], xtok[:, tt, c * D // 2:(c + 1) * D // 2], ACT.Square,
                                              accum_out=xss[:, c, tt:tt + 1]))

            x_squares(0)
            act.wait_ge(s_init, 1)
            nc.scalar.activation(trig[:, :, :], trig[:, :, :], ACT.Sin).then_inc(s_inita, 1)
            act.wait_ge(s_init, 2)
            units(AHEAD)
            for g in range(8):
                hn.n += 1
                make_u(g, lambda j: prm[:, R_MIX[0] + j:R_MIX[0] + j + 1], hn.at())
            x_squares(1)
            act.sem_inc(s_xss, 1)
            nc.scalar.preload_act_table_set(LN_EXP)
            act.wait_ge(s_init, 3)
            nc.scalar.activation(lam[:, 0:2, :], lam[:, 0:2, :], ACT.Exp).then_inc(s_inita, 1)

            with turns(act, DEPTH, [(unit, UNITS_PER_LAYER), (group, GROUPS_PER_LAYER), (norm, 3), (hn, 24),
                                    (chain, ACT_LINKS), (silu, 31), (hidc, 22)], s_began) as layer:

                def column(row, j=0):
                    first, per_layer = row
                    return prm[:, bass.ds(layer * per_layer + (j + first), 1)]

                act.wait_ge(s_lay[0], layer * 16 + 16)
                nc.scalar.activation(walr[:, :, 0, :], walr_raw[:, :, :], ACT.Copy).then_inc(s_walr, 1)

                def logits(_):
                    act.wait_ge(s_xa, layer + 1)
                    for hh in range(GLA_H):
                        ins = nc.scalar.activation(gt[:, hh, :], pm[:, hh // 2, hh % 2 * S:(hh % 2 + 1) * S],
                                                   ACT.Identity, bias=column(R_BAL, hh))
                    ins.then_inc(s_xc, 1)

                def exp_abs(_):
                    act.wait_ge(s_xc, layer + 1)
                    link(nc.scalar.activation(bc[:, :, 1:], gt, ACT.Abs))
                    link(nc.scalar.activation(bc[:, :, 1:], bc[:, :, 1:], ACT.Exp, scale=-1.0))

                def log1p(_):
                    nc.scalar.activation(bc[:, :, 1:], bc[:, :, 1:], ACT.Ln, bias=epst[:, 1:2]).then_inc(s_xs, 1)

                def decay_exp(_):
                    act.wait_ge(s_bd, layer + 1)
                    nc.scalar.activation(gt, gt, ACT.Exp).then_inc(s_eq, 1)

                def far_decay(_):
                    for hh in range(GLA_H):
                        nc.scalar.activation(qfar[:, hh, :], bc[:, hh, P + 1:2 * P + 1], ACT.Exp, bias=bneg[:, hh, :])
                        ins = nc.scalar.activation(kfar[:, hh, :], bc[:, hh, 1:P + 1], ACT.Exp, bias=bc[:, hh, P:P + 1],
                                                   scale=-1.0)
                    ins.then_inc(s_far, 1)

                def squares(n):
                    item = items(dq, dk, sq, sk)[n]
                    act.wait_ge(s_ev, layer * EV + EV_ITEM[n])
                    nc.scalar.activation(nsq[:, 0:item.shape[-1]], item, ACT.Square).then_inc(s_nsq, 1)

                def norm_item(n):
                    w = items(dq, dk, sq, sk)[n].shape[-1]
                    act.wait_ge(s_nss, layer * 7 + (n + 1))
                    link(nc.scalar.activation(lnt[:, 0:w], pm[:, 3, 0:w], ACT.Ln, bias=epst[:, 0:1]))
                    if n:
                        act.wait_ge(s_qn, layer * 7 + n)
                    nc.scalar.activation(rsn[:, 0:w], lnt[:, 0:w], ACT.Exp, scale=-0.5).then_inc(s_nrs, 1)

                def mixer_hi(tile, n, src, wait_for, value):
                    act.wait_ge(wait_for, value)
                    nc.scalar.activation(hid[:, tile:tile + n, 0, :], src, ACT.Copy).then_inc(s_mhi, 1)

                def scores(z):
                    act.wait_ge(s_mx, layer * 16 + (z + 1))
                    j = z % 2
                    diff, k0 = z >= 8, 0 if z >= 8 or j == 0 else CHUNK
                    kw = (j + 1) * P
                    for c in range(2):
                        ins = nc.scalar.activation(pe_buf[:, z % 2, c, k0:kw], pm[:, c, k0:kw], ACT.Exp,
                                                   scale=SCALE, bias=st[:, z % 2, c:c + 1],
                                                   accum_out=st[:, z % 2, 2 + c:3 + c])
                    if not diff:
                        ins = nc.scalar.activation(st[:, z % 2, 4:6], st[:, z % 2, 6:8], ACT.Exp)
                    ins.then_inc(s_ex, 1)

                def transpose(z):
                    j = z % 2
                    act.wait_ge(s_tp, layer * 16 + (z + 1))
                    if z >= 8:
                        nc.scalar.activation(wT[:, z % 2, 0:j + 1, :],
                                             pm[:, 3, 0:(j + 1) * P].rearrange("p (a t) -> p a t", t=P),
                                             ACT.Copy).then_inc(s_tpc, 1)
                    else:
                        nc.scalar.activation(wT[:, z % 2, :, :].rearrange("p (e k) t -> p e k t", e=2)[:, :, 0:j + 1, :],
                                             pm[:, 3, :].rearrange("p (e k t) -> p e k t", e=2, k=2)[:, :, 0:j + 1, :],
                                             ACT.Copy).then_inc(s_tpc, 1)

                def values(z):
                    if z % 2 == 1 and z < 8:
                        mixer_hi(12 + z // 2, 1, pm[:, 2, 0:S], s_pv, layer * 8 + (z // 2 + 1))
                    elif z % 2 == 1:
                        act.wait_ge(s_pv, layer * 8 + (z // 2 + 1))
                        nc.scalar.activation(osq, pm[:, 2, 0:S], ACT.Square).then_inc(s_osq, 1)

                def diff_norm(hh):
                    act.wait_ge(s_oss, layer * DIFF_H + (hh + 1))
                    link(nc.scalar.activation(lnt[:, 0:S], pm[:, 3, 0:S], ACT.Ln, scale=1.0 / P, bias=epst[:, 0:1]))
                    nc.scalar.activation(rsn[:, 0:S], lnt[:, 0:S], ACT.Exp, scale=-0.5).then_inc(s_ors, 1)
                    mixer_hi(8 + hh, 1, hf[:, 0:S], s_mf, layer * 8 + (hh + 1))

                def gate(_):
                    silu.n += 1
                    act.wait_ge(s_gate, silu.at())
                    nc.scalar.activation(sgate[:, :, :], sgate[:, :, :], ACT.Silu).then_inc(s_silu, 1)
                    nc.scalar.preload_act_table_set(LN_EXP)

                def keys(i):
                    hh = i // 4
                    if i >= 2:
                        act.wait_ge(s_am, layer * 16 + (i - 1))
                    for n in range(4 * i % NBLK, 4 * i % NBLK + 4):
                        t0, width = n // 8 * P, BLK * (n % 8 + 1)
                        ins = nc.scalar.activation(kn[:, n % 8, 0:width], bc[:, hh, t0 + 1:t0 + 1 + width], ACT.Exp,
                                                   bias=bc[:, hh, BLK * n:BLK * n + 1], scale=-1.0)
                    ins.then_inc(s_ke, 1)

                def gla_out(hh):
                    act.wait_ge(s_go, layer * GLA_H + (hh + 1))
                    nc.scalar.activation(pe_buf[:, 0, :, :], pm[:, 2, :].rearrange("p (a t) -> p a t", a=2),
                                         ACT.Square).then_inc(s_gsq, 1)

                def gla_norm(hh):
                    act.wait_ge(s_gss, layer * GLA_H + (hh + 1))
                    link(nc.scalar.activation(lnt[:, 0:S], pm[:, 0, 0:S], ACT.Ln, scale=1.0 / DV, bias=epst[:, 0:1]))
                    nc.scalar.activation(rsn[:, 0:S], lnt[:, 0:S], ACT.Exp, scale=-0.5).then_inc(s_grs, 1)
                    mixer_hi(2 * hh, 2, hf[:, :].rearrange("p (a t) -> p a t", a=2), s_mf, layer * 8 + (DIFF_H + hh + 1))

                steps = dict(logits=logits, exp_abs=exp_abs, log1p=log1p, decay_exp=decay_exp, far_decay=far_decay, squares=squares, norm=norm_item,
                             scores=scores, transpose=transpose, values=values, diff_norm=diff_norm, gate=gate,
                             keys=keys, gla_out=gla_out, gla_norm=gla_norm)

                def beside(slot, n):
                    for q in range(n):
                        for step, i in BESIDE.get(slot + q, ()):
                            if step in steps:
                                steps[step](i)
                        units(1)

                units(4)
                rms(True)
                take_cross()
                act.wait_ge(s_half, layer * 5 + 1)
                nc.scalar.activation(cross[0:2 * RANK, 1, 0:S], pd[0:2 * RANK, 1, 0, S:2 * S], ACT.Copy
                                     ).then_inc(s_cross, 1)
                group.n += 1
                for g in range(1, 21):
                    beside(4 * g, 4)
                    take_cross(rstdC if g in BY_TOKEN else None)

                for g in range(2):
                    beside(84 + 2 * g, 2)
                    group.n += 1
                with turns(act, 3, [(unit, 4), (group, 2)], s_began) as i:
                    units(4)
                    group.n += 2
                def ffn_u(g):
                    hn.n += 1
                    make_u(g, lambda j: column(R_FFN, j), hn.at())

                units(2)
                group.n += 1
                with turns(act, 3, [(unit, 4), (group, 2), (hn, 2)], s_began) as i:
                    for g in range(2):
                        units(2)
                        group.n += 1
                        ffn_u(i * 2 + g)
                units(2)
                group.n += 1
                ffn_u(6)
                ffn_u(7)

                def hidden_pair(i, first=False):
                    units(4)
                    if first:
                        rms(False)
                    take_cross()
                    silu.n += 1
                    act.wait_ge(s_gate, silu.at())
                    nc.scalar.activation(sg[:, :], ta[:, :], ACT.Silu).then_inc(s_silu, 1)
                    units(4)
                    take_cross()
                    hidc.n += 1
                    act.wait_ge(s_hf, hidc.at())
                    nc.scalar.activation(hid[:, bass.ds(i * 2, 2), 0, :], hf[:, :].rearrange("p (a t) -> p a t", a=2),
                                         ACT.Copy).then_inc(s_hidhi, 1)

                for r, n in enumerate(ROUNDS):
                    if r == len(ROUNDS) - 1:
                        act.wait_ge(s_p, layer + 1)
                        nc.scalar.activation(pT[:, :, 0, :], pm[:, 1, :].rearrange("p (a t) -> p a t", a=2),
                                             ACT.Copy).then_inc(s_phi, 1)
                    peeled = int(r == 0)
                    if peeled:
                        hidden_pair(0, first=True)
                    with turns(act, n // 2 - peeled, [(unit, 8), (group, 2), (silu, 1), (hidc, 1)], s_began) as i:
                        hidden_pair(i + peeled)
                    last = r == len(ROUNDS) - 1
                    per = 2 if n == 16 else 4
                    with turns(act, 8 // per, [(unit, n // 4 * per), (group, per)] + [(hn, per)] * last, s_began) as i:
                        for g in range(per):
                            units(n // UK)
                            group.n += 1
                            if last:
                                hn.n += 1
                                make_u(i * per + g, lambda j: column(R_PLE, j), hn.at())

                for g in range(8):
                    if g % 2 == 0:
                        units(1)
                    take_cross(done=(s_half, layer * 5 + (2 + g // 2)) if g % 2 == 0 else None)

                def ple_group(g, first=False, last=False):
                    if last:
                        units(1)
                        for q in range(3):
                            units(1)
                            next_u(2 * q)
                            next_u(2 * q + 1)
                    else:
                        units(4)
                    if first:
                        rms(False)
                    take_cross()
                    silu.n += 1
                    act.wait_ge(s_gate, silu.at())
                    nc.scalar.activation(sg[:, :], ta[:, :], ACT.Sigmoid).then_inc(s_silu, 1)

                def next_u(g):
                    hn.n += 1
                    make_u(g, lambda j: column(R_MIX, KT + j), hn.at())

                ple_group(0, first=True)
                ple_group(1)
                with turns(act, 2, [(unit, 8), (group, 2), (silu, 2)], s_began) as i:
                    ple_group(i * 2 + 2)
                    ple_group(i * 2 + 3)
                ple_group(6)
                ple_group(7, last=True)
                next_u(6)
                next_u(7)

        @block.vector
        def _(dve):
            unit, group, norm, hn, chain = Count(), Count(), Count(), Count(), Count()
            silu, hidc, evc, crossed = Count(), Count(), Count(), Count()

            def link(ins):
                chain.n += 1
                ins.then_inc(s_dve, 1)
                dve.wait_ge(s_dve, chain.at())

            def split(slot):
                dve.wait_ge(s_hi, unit.at(1))
                nc.vector.tensor_tensor(wsp[:, slot, :, 1, :], raw[:, slot, :].rearrange("p (k n) -> p k n", k=UK),
                                        wsp[:, slot, :, 0, :].bitcast(F32), ALU.subtract).then_inc(s_lo, 1)
                unit.n += 1

            def units(n):
                for _ in range(n):
                    split(unit.n % RING)

            def halves(t):
                return t[:, :].rearrange("p (a t) -> p a t", a=2)

            def both(t):
                return t[:, 0:S].unsqueeze(1).to_broadcast([P, 2, S])

            def main_plus_cross(dst):
                par = group.n % 2
                crossed.n += 1
                dve.wait_ge(s_cross, crossed.at())
                group.n += 1
                nc.vector.tensor_tensor(dst, pd[:, par, :, 0:S], halves_of(cross[:, par, :]), ALU.add
                                        ).then_inc(s_psfree, 1)
                dve.wait_ge(s_psfree, group.at(2))

            def halves_of(ap):
                return ap.rearrange("p (a t) -> p a t", a=2)

            def feature_major(dst):
                main_plus_cross(halves(ta))
                nc.vector.tensor_tensor(dst, halves(ta), both(rstdB), ALU.mult).then_inc(s_ev, 1)
                evc.n += 1
                dve.wait_ge(s_ev, evc.at())

            def token_major(dst):
                par = group.n % 2
                crossed.n += 1
                dve.wait_ge(s_cross, crossed.at())
                for tt in range(TT):
                    ins = nc.vector.scalar_tensor_tensor(dst(tt), pd[:, par, tt, 0:S], rstdC[:, tt:tt + 1],
                                                         cross[:, par, tt * S:(tt + 1) * S], ALU.mult, ALU.add)
                ins.then_inc(s_psfree, 1)
                group.n += 1
                evc.n += 1
                dve.wait_ge(s_psfree, group.at(2))
                dve.sem_inc(s_ev, 1)

            def add_to_h(g):
                par = group.n % 2
                dve.wait_ge(s_used, unit.at(1))
                hv = h[:, bass.ds(2 * g, 2), :]
                link(nc.vector.tensor_tensor(hv, pd[:, par, :, 0:S], hv, ALU.add))
                ins = nc.vector.tensor_tensor(hv, pd[:, par, :, S:2 * S], hv, ALU.add)
                ins.then_inc(s_psfree, 1)
                group.n += 1
                dve.wait_ge(s_psfree, group.at(2))

            def make_u(g, gain):
                hn.n += 1
                dve.wait_ge(s_uhi, hn.at())
                for j in range(2):
                    k = bass.ds(2 * g + j, 1)
                    ins = nc.vector.scalar_tensor_tensor(u[:, k, 1, :], h[:, k, :], gain(2 * g + j),
                                                         u[:, k, 0, :].bitcast(F32), ALU.mult, ALU.subtract)
                ins.then_inc(s_u, 1)

            dve.sem_inc(s_lo, RING)
            dve.memset(ones[:, :], 1.0)
            dve.memset(epst[:, 0:1], EPS)
            dve.memset(epst[:, 1:2], 1.0)
            dve.memset(bc[:, :, 0:1], 0.0)
            dve.memset(kn[:, :, :], 0.0)
            dve.memset(pe_buf[:, :, :, :], 0.0)
            dve.sem_inc(s_psfree, 1)
            dve.wait_ge(s_cst, 16)
            dve.wait_ge(s_pos, 16)
            link(nc.vector.tensor_copy(ta[:, 0:S], pos_i[:, :]))
            link(nc.vector.tensor_scalar(ta[:, 0:S], ta[:, 0:S], cst[:, K_INV:K_INV + 1], None, ALU.mult))
            for half, turn in ((0, 0.0), (1, 0.25)):
                link(nc.vector.tensor_scalar(tb[:, half * S:(half + 1) * S], ta[:, 0:S], INV_2PI, turn, ALU.mult, ALU.add))
            link(nc.vector.tensor_scalar(tb[:, :], tb[:, :], MAGIC, None, ALU.add))
            link(nc.vector.tensor_scalar(tb[:, :], tb[:, :], MAGIC, None, ALU.subtract))
            link(nc.vector.scalar_tensor_tensor(halves(hf), halves(tb), -PI2_A, both(ta), ALU.mult, ALU.add))
            link(nc.vector.scalar_tensor_tensor(halves(hf), halves(tb), -PI2_B, halves(hf), ALU.mult, ALU.add))
            link(nc.vector.scalar_tensor_tensor(halves(hf), halves(tb), -PI2_C, halves(hf), ALU.mult, ALU.add))
            for half, shift in ((0, 0.0), (1, 1.5707963267948966)):
                hv = hf[:, half * S:(half + 1) * S]
                link(nc.vector.tensor_scalar(hv, hv, shift, PI_LO, ALU.add, ALU.min))
            link(nc.vector.tensor_scalar(trig[:, :, :], halves(hf), -PI_LO, None, ALU.max))
            dve.sem_inc(s_init, 1)
            dve.wait_ge(s_tr, 1)
            link(nc.vector.tensor_copy(prm[:, 0:DEPTH * KT], pd[:, 0, 0, 0:DEPTH * KT]))
            dve.sem_inc(s_init, 1)
            dve.sem_inc(s_psfree, 1)
            for g in range(8):
                dve.wait_ge(s_tr, 2 + g)
                nc.vector.tensor_copy(h[:, 2 * g:2 * g + 2, :], halves_of(pm[:, g % 4, :])).then_inc(s_hnew, 1)
            units(AHEAD)
            for g in range(8):
                make_u(g, lambda j: prm[:, R_MIX[0] + j:R_MIX[0] + j + 1])
            dve.wait_ge(s_lamv, 4 * 16)
            link(nc.vector.tensor_tensor(lamp[:, 0], lamv[:, 0], lamv[:, 1], ALU.mult))
            link(nc.vector.tensor_tensor(lamp[:, 1], lamv[:, 2], lamv[:, 3], ALU.mult))
            link(nc.vector.tensor_reduce(lam[:, 0:2, :], lamp[:, :, :, :], AX.X, ALU.add))
            dve.sem_inc(s_init, 1)
            dve.wait_ge(s_xss, 1)
            link(nc.vector.tensor_tensor(xss[:, 0, :], xss[:, 0, :], xss[:, 1, :], ALU.add))
            for tt in range(TT):
                ins = nc.vector.tensor_scalar(ssq[:, tt * P:(tt + 1) * P], ident, xss[:, 0, tt:tt + 1], None, ALU.mult)
            ins.then_inc(s_ssq, 1)
            dve.wait_ge(s_small, n_small)
            dve.wait_ge(s_tr, 10)
            link(nc.vector.tensor_copy(prm[:, DEPTH * KT:R_ALL], pm[:, 1, DEPTH * KT:R_ALL]))
            for l in range(DEPTH):
                at = R_SUB[0] + l
                link(nc.vector.tensor_tensor(prm[:, at:at + 1], prm[:, at:at + 1],
                                             cst[:, K_ONE_LAM + l:K_ONE_LAM + l + 1], ALU.mult))
            dve.wait_ge(s_inita, 2)
            link(nc.vector.tensor_tensor(lam[:, 2, :], lam[:, 0, :], lam[:, 1, :], ALU.subtract))
            link(nc.vector.tensor_tensor(lam[:, 2, :], lam[:, 2, :], cst[:, K_LAM:K_LAM + 2], ALU.add))
            link(nc.vector.tensor_scalar(lam[:, 3, :], lam[:, 2, :], -1.0, None, ALU.mult))

            with turns(dve, DEPTH, [(unit, UNITS_PER_LAYER), (group, GROUPS_PER_LAYER), (norm, 3), (hn, 24),
                                    (chain, DVE_LINKS), (silu, 31), (hidc, 22), (evc, EV), (crossed, CROSSED)], s_began) as layer:

                def column(row, j=0):
                    first, per_layer = row
                    return prm[:, bass.ds(layer * per_layer + (j + first), 1)]

                nc.vector.memset(pe_buf[:, 1, :, 0:CHUNK], 0.0)
                dve.wait_ge(s_walr, layer * 2 + 1)
                nc.vector.tensor_tensor(walr[:, :, 1, :], walr_raw[:, :, :], walr[:, :, 0, :].bitcast(F32),
                                        ALU.subtract).then_inc(s_walr, 1)

                def log_decay(_):
                    dve.wait_ge(s_xs, layer + 1)
                    link(nc.vector.scalar_tensor_tensor(gt, gt, 0.0, bc[:, :, 1:], ALU.min, ALU.subtract))
                    link(nc.vector.tensor_scalar(gt, gt, 1.0 / GLA_TAU, None, ALU.mult))

                def decay_sums(_):
                    for hh in range(GLA_H):
                        ins = nc.vector.tensor_tensor_scan(bc[:, hh, 1:], ones[:, 0:1].to_broadcast([P, S]), gt[:, hh, :],
                                                           0.0, ALU.mult, ALU.add)
                    ins.then_inc(s_la, 1)

                def block_decay(_):
                    dve.wait_ge(s_la, layer + 1)
                    for hh in range(GLA_H):
                        start = bc[:, hh, 0:S].rearrange("p (n b) -> p n b", b=BLK)[:, :, 0:1].to_broadcast([P, NBLK, BLK])
                        nc.vector.tensor_tensor(gt[:, hh, :].rearrange("p (n b) -> p n b", b=BLK),
                                                      bc[:, hh, 1:].rearrange("p (n b) -> p n b", b=BLK), start, ALU.subtract)
                    nc.vector.tensor_scalar(bneg[:, :, :], bc[:, :, P:P + 1], -1.0, None, ALU.mult).then_inc(s_bd, 1)

                def norm_item(n):
                    item = items(dq, dk, sq, sk)[n]
                    dve.wait_ge(s_nrs, layer * 7 + (n + 1))
                    nc.vector.scalar_tensor_tensor(item, item, column(ITEM_GAINS[n]), rsn[:, 0:item.shape[-1]], ALU.mult,
                                                   ALU.mult).then_inc(s_qn, 1)

                def rope(n):
                    item = items(dq, dk, sq, sk)[n]
                    dve.wait_ge(s_rot, layer * 7 + (n + 1))
                    if n == 0:
                        nc.vector.tensor_tensor(kd, halves_of(pm[:, 3, :]), both(cosB), ALU.mult).then_inc(s_kcos, 1)
                        return
                    dve.wait_ge(s_qn, layer * 7 + (n + 1))
                    link(nc.vector.tensor_tensor(halves(ta), halves_of(item), both(cosB), ALU.mult))
                    link(nc.vector.tensor_tensor(halves(tb), halves_of(pm[:, 3, :]), both(sinB), ALU.mult))
                    nc.vector.tensor_tensor(item, ta[:, :], tb[:, :], ALU.add).then_inc(s_rope, 1)
                    dve.wait_ge(s_rope, layer * 7 + (n + 1))

                def swa_k(_):
                    dve.wait_ge(s_kcos, layer + 1)
                    dve.wait_ge(s_krot, layer + 1)
                    link(nc.vector.tensor_tensor(halves(tb), halves_of(pm[:, 3, :]), both(sinB), ALU.mult))
                    nc.vector.tensor_tensor(kd, kd, halves(tb), ALU.add).then_inc(s_rope, 1)
                    dve.wait_ge(s_rope, layer * 7 + 1)

                def swa_v(_):
                    dve.wait_ge(s_svT, layer + 1)
                    nc.vector.tensor_copy(sv.rearrange("p a c -> p (a c)"), pm[:, 3, 0:2 * P]).then_inc(s_sv, 1)

                def scores(z):
                    j, zp = z % 2, z % 2
                    kw = (j + 1) * P
                    dve.wait_ge(s_sc, layer * 16 + (z + 1))
                    tail = pm[0:CHUNK, 0:2, kw - CHUNK:kw]
                    link(nc.vector.tensor_scalar(tail, tail, NEG, None, ALU.add))
                    if z >= 8:
                        link(nc.vector.tensor_reduce(st[:, zp, 8:10], pm[:, 0:2, 0:kw], AX.X, ALU.max))
                        nc.vector.tensor_scalar(st[:, zp, 0:2], st[:, zp, 8:10], -SCALE, None, ALU.mult).then_inc(s_mx, 1)
                        return
                    t = z // 2
                    k0 = CHUNK * j
                    if j == 1:
                        head = pm[CHUNK:P, 0:2, k0:k0 + CHUNK]
                        link(nc.vector.tensor_scalar(head, head, NEG, None, ALU.add))
                    link(nc.vector.tensor_reduce(st[:, zp, 8:10], pm[:, 0:2, k0:kw], AX.X, ALU.max))
                    sink = sinks[:, bass.ds(layer, 1), 2 * t:2 * t + 2].rearrange("p a b -> p (a b)")
                    link(nc.vector.scalar_tensor_tensor(st[:, zp, 10:12], st[:, zp, 8:10], SCALE, sink, ALU.mult, ALU.max))
                    link(nc.vector.tensor_tensor(st[:, zp, 6:8], sink, st[:, zp, 10:12], ALU.subtract))
                    nc.vector.tensor_scalar(st[:, zp, 0:2], st[:, zp, 10:12], -1.0, None, ALU.mult).then_inc(s_mx, 1)

                def weights(z):
                    zp = z % 2
                    kw, k0 = (zp + 1) * P, CHUNK * zp
                    dve.wait_ge(s_ex, layer * 16 + (z + 1))
                    if z >= 8:
                        link(nc.vector.reciprocal(st[:, zp, 8:10], st[:, zp, 2:4]))
                        link(nc.vector.tensor_tensor(st[:, zp, 10:11], st[:, zp, 9:10], lam[:, 3, bass.ds(layer, 1)], ALU.mult))
                        link(nc.vector.tensor_scalar(ta[:, 0:kw], pe_buf[:, zp, 1, 0:kw], st[:, zp, 10:11], None, ALU.mult))
                        nc.vector.scalar_tensor_tensor(pe_buf[:, zp, 0, 0:kw], pe_buf[:, zp, 0, 0:kw], st[:, zp, 8:9],
                                                       ta[:, 0:kw], ALU.mult, ALU.add).then_inc(s_wt, 1)
                        dve.wait_ge(s_wt, layer * 16 + (z + 1))
                        return
                    link(nc.vector.tensor_tensor(st[:, zp, 8:10], st[:, zp, 2:4], st[:, zp, 4:6], ALU.add))
                    link(nc.vector.reciprocal(st[:, zp, 10:12], st[:, zp, 8:10]))
                    for e in range(2):
                        pv = pe_buf[:, zp, e, k0:kw]
                        ins = nc.vector.tensor_scalar(pv, pv, st[:, zp, 10 + e:11 + e], None, ALU.mult)
                    ins.then_inc(s_wt, 1)

                def values(z):
                    if z % 2 == 1 and z < 8:
                        t = z // 2
                        dve.wait_ge(s_mhi, layer * 12 + (t + 1))
                        nc.vector.tensor_tensor(hid[:, 12 + t, 1, :], pm[:, 2, 0:S], hid[:, 12 + t, 0, :].bitcast(F32),
                                                ALU.subtract).then_inc(s_mix, 1)

                def diff_norm(hh):
                    dve.wait_ge(s_ors, layer * DIFF_H + (hh + 1))
                    nc.vector.scalar_tensor_tensor(hf[:, 0:S], pm[:, 2, 0:S], column(R_SUB), rsn[:, 0:S],
                                                   ALU.mult, ALU.mult).then_inc(s_mf, 1)
                    dve.wait_ge(s_mhi, layer * 12 + (4 + hh + 1))
                    nc.vector.tensor_tensor(hid[:, 8 + hh, 1, :], hf[:, 0:S], hid[:, 8 + hh, 0, :].bitcast(F32),
                                            ALU.subtract).then_inc(s_mix, 1)
                    dve.wait_ge(s_mix, layer * 12 + (4 + hh + 1))

                def queries(_):
                    dve.wait_ge(s_eq, layer + 1)
                    dve.wait_ge(s_far, layer + 1)
                    link(nc.vector.scalar_tensor_tensor(qfar[:, :, :], qg[:, :, P:2 * P], GLA_SCALE, qfar[:, :, :], ALU.mult,
                                                        ALU.mult))
                    nc.vector.scalar_tensor_tensor(qg, qg, GLA_SCALE, gt, ALU.mult, ALU.mult).then_inc(s_qd, 1)

                def far_keys(_):
                    nc.vector.tensor_tensor(kfar[:, :, :], kfar[:, :, :], kg[:, :, 0:P], ALU.mult).then_inc(s_kfar, 1)

                def keys(i):
                    slot, t0 = 4 * i % 8, 4 * i % NBLK // 8 * P
                    width = (slot + 4) * BLK
                    dve.wait_ge(s_ke, layer * 16 + (i + 1))
                    kv = kn[:, slot:slot + 4, 0:width]
                    nc.vector.tensor_tensor(kv, kv, kg[:, i // 4, t0:t0 + width].unsqueeze(1).to_broadcast([P, 4, width]),
                                            ALU.mult).then_inc(s_kn, 1)

                def mask(hh):
                    if hh:
                        dve.wait_ge(s_go, layer * GLA_H + hh)
                    dve.wait_ge(s_am, layer * 16 + (hh + 1) * 4)
                    nc.vector.tensor_tensor(att, pm[:, 3, 0:3 * P], cst[:, K_TRI:K_TRI + 3 * P], ALU.mult).then_inc(s_att, 1)

                def gla_norm(hh):
                    dve.wait_ge(s_silu, silu.at())
                    dve.wait_ge(s_grs, layer * GLA_H + (hh + 1))
                    for b in range(2):
                        ins = nc.vector.scalar_tensor_tensor(ta[:, b * S:(b + 1) * S], pm[:, 2, b * S:(b + 1) * S],
                                                             column(R_GLA, b), rsn[:, 0:S], ALU.mult, ALU.mult)
                    link(ins)
                    nc.vector.tensor_tensor(halves(hf), halves(ta), sgate[:, 2 * hh:2 * hh + 2, :], ALU.mult
                                            ).then_inc(s_mf, 1)
                    dve.wait_ge(s_mhi, layer * 12 + (8 + hh + 1))
                    nc.vector.tensor_tensor(hid[:, 2 * hh:2 * hh + 2, 1, :], halves(hf),
                                            hid[:, 2 * hh:2 * hh + 2, 0, :].bitcast(F32), ALU.subtract).then_inc(s_mix, 1)
                    dve.wait_ge(s_mix, layer * 12 + (8 + hh + 1))

                steps = dict(log_decay=log_decay, decay_sums=decay_sums, block_decay=block_decay, norm=norm_item,
                             rope=rope, swa_k=swa_k, swa_v=swa_v, scores=scores, weights=weights, values=values,
                             diff_norm=diff_norm, queries=queries, far_keys=far_keys, keys=keys, mask=mask, gla_norm=gla_norm)

                def beside(slot, n):
                    for q in range(n):
                        for step, i in BESIDE.get(slot + q, ()):
                            if step in steps:
                                steps[step](i)
                        units(1)

                units(4)
                norm.n += 1
                dve.wait_ge(s_rstd, norm.at())
                main_plus_cross(halves(ta))
                link(nc.vector.tensor_tensor(sk, ta[:, 0:S], rstdB[:, :], ALU.mult))
                nc.vector.tensor_tensor(svT, ta[:, S:2 * S], rstdB[:, :], ALU.mult).then_inc(s_ev, 1)
                evc.n += 1
                dve.wait_ge(s_ev, evc.at())
                crossed.n += 1
                dve.wait_ge(s_cross, crossed.at())
                nc.vector.tensor_tensor(alrT[:, :], pd[0:2 * RANK, 1, 0, 0:S], cross[0:2 * RANK, 1, 0:S], ALU.add
                                        ).then_inc(s_psfree, 1)
                group.n += 1
                dve.wait_ge(s_psfree, group.at(2))
                nc.vector.tensor_tensor(alrT[:, :], alrT[:, :], rstdB[0:2 * RANK, :], ALU.mult).then_inc(s_ev, 1)
                evc.n += 1
                slot = 4
                for dst in (sq, dq, dk):
                    for g in range(2):
                        beside(slot, 4)
                        feature_major(dst[:, 2 * g:2 * g + 2, :])
                        slot += 4
                for g in range(2):
                    beside(slot, 4)
                    token_major(lambda tt: dv[:, tt, g * G:(g + 1) * G])
                    slot += 4
                for dst in (qg, kg):
                    for g in range(2):
                        beside(slot, 4)
                        feature_major(dst[:, 2 * g:2 * g + 2, :])
                        slot += 4
                for g in range(4):
                    beside(slot, 4)
                    main_plus_cross(halves(ta))
                    link(nc.vector.tensor_tensor(sgate[:, 2 * g:2 * g + 2, :], halves(ta), both(rstdB), ALU.mult))
                    slot += 4
                silu.n += 1
                dve.sem_inc(s_gate, 1)
                for g in range(4):
                    beside(slot, 4)
                    token_major(lambda tt: vg[:, tt, g * G:(g + 1) * G])
                    slot += 4

                for g in range(2):
                    beside(slot, 2)
                    add_to_h(g)
                    slot += 2
                with turns(dve, 3, [(unit, 4), (group, 2), (chain, 2)], s_began) as i:
                    for g in range(2):
                        units(2)
                        add_to_h(i * 2 + g + 2)
                def w_out_group(g, last_u=None):
                    units(2)
                    if last_u is not None:
                        make_u(last_u, lambda j: column(R_FFN, j))
                    add_to_h(g)
                    dve.sem_inc(s_hnew, 1)

                w_out_group(0)
                with turns(dve, 3, [(unit, 4), (group, 2), (chain, 2), (hn, 2)], s_began) as i:
                    for g in range(2):
                        w_out_group(i * 2 + (g + 1), i * 2 + g)
                w_out_group(7, 6)
                make_u(7, lambda j: column(R_FFN, j))

                norm.n += 1
                for r, n in enumerate(ROUNDS):
                    if r == len(ROUNDS) - 1:
                        dve.wait_ge(s_phi, layer + 1)
                        nc.vector.tensor_tensor(pT[:, :, 1, :], halves_of(pm[:, 1, :]), pT[:, :, 0, :].bitcast(F32),
                                                ALU.subtract).then_inc(s_plo, 1)
                    with turns(dve, n // 2, [(unit, 8), (group, 2), (silu, 1), (hidc, 1), (chain, 2), (crossed, 2)], s_began) as i:
                        units(4)
                        dve.wait_ge(s_rstd, norm.at())
                        main_plus_cross(halves(tb))
                        nc.vector.tensor_tensor(halves(ta), halves(tb), both(rstdB), ALU.mult).then_inc(s_gate, 1)
                        silu.n += 1
                        dve.wait_ge(s_silu, silu.at())
                        link(nc.vector.tensor_tensor(halves(sg), halves(sg), both(rstdB), ALU.mult))
                        units(4)
                        main_plus_cross(halves(tb))
                        nc.vector.tensor_tensor(hf[:, :], tb[:, :], sg[:, :], ALU.mult).then_inc(s_hf, 1)
                        hidc.n += 1
                        dve.wait_ge(s_hidhi, hidc.at())
                        hv = bass.ds(i * 2, 2)
                        link(nc.vector.tensor_tensor(hid[:, hv, 1, :], halves(hf), hid[:, hv, 0, :].bitcast(F32),
                                                     ALU.subtract))
                        dve.sem_inc(s_hid, 1)
                    last = r == len(ROUNDS) - 1
                    per = 2 if n == 16 else 4
                    with turns(dve, 8 // per, [(unit, n // 4 * per), (group, per), (chain, per)] + [(hn, per)] * last, s_began) as i:
                        for g in range(per):
                            units(n // UK)
                            add_to_h(i * per + g)
                            if last:
                                dve.sem_inc(s_hnew, 1)
                                make_u(i * per + g, lambda j: column(R_PLE, j))

                for g in range(8):
                    if g % 2 == 0:
                        units(1)
                    main_plus_cross(pleT[:, 2 * g:2 * g + 2, :])
                norm.n += 1
                def next_u(g):
                    make_u(g, lambda j: column(R_MIX, KT + j))

                def ple_group(g, last=False):
                    if last:
                        units(1)
                        for q in range(3):
                            units(1)
                            next_u(2 * q)
                            next_u(2 * q + 1)
                    else:
                        units(4)
                    dve.wait_ge(s_rstd, norm.at())
                    main_plus_cross(halves(tb))
                    nc.vector.tensor_tensor(halves(ta), halves(tb), both(rstdB), ALU.mult).then_inc(s_gate, 1)
                    silu.n += 1
                    dve.wait_ge(s_silu, silu.at())
                    gv = bass.ds(g * 2, 2)
                    link(nc.vector.tensor_tensor(halves(tb), halves(sg), pleT[:, gv, :], ALU.mult))
                    link(nc.vector.tensor_tensor(h[:, gv, :], h[:, gv, :], halves(tb), ALU.add))
                    dve.sem_inc(s_hnew, 1)

                with turns(dve, 3, [(unit, 8), (group, 2), (silu, 2), (chain, 4), (crossed, 2)], s_began) as i:
                    ple_group(i * 2)
                    ple_group(i * 2 + 1)
                ple_group(6)
                ple_group(7, last=True)
                next_u(6)
                next_u(7)

            for g in range(8):
                dve.wait_ge(s_tr, 10 + g + 1)
                nc.vector.tensor_copy(xtok[:, :, g * G:(g + 1) * G], halves_of(pm[:, g % 4, :])).then_inc(s_trc, 1)

        @block.tensor
        def _(pe):
            unit, group, norm, hn, hidc = Count(), Count(), Count(), Count(), Count()

            def mm(o, a, b, start, stop):
                return nc.tensor.matmul(o, a, b, start=start, stop=stop, skip_group_check=True)

            def stationary_weights(slot, k, x_pair, par, start, stop, cols=0, width=2):
                for n in range(2):
                    c = slice(cols + n * P, cols + (n + 1) * P)
                    mm(pd[:, par, n, :], wview(slot, k, 0, c, width), x_pair, start, False)
                    ins = mm(pd[:, par, n, 0:S], wview(slot, k, 1, c, width), x_pair[:, 0:S], False, stop)
                return ins

            def wview(slot, k, part, c, width):
                if width == 2:
                    return wsp[:, slot, k, part, c]
                col = c.start
                return wsp[:, slot, 2 * k + col // G, part, col % G:col % G + P]

            def moving_weights(slot, k, x_tile, par, start, stop):
                for tt in range(TT):
                    t = slice(tt * P, (tt + 1) * P)
                    mm(pd[:, par, tt, :], x_tile[:, 0, t], wsp[:, slot, k, :, :].rearrange("p a n -> p (a n)"), start, False)
                    ins = mm(pd[:, par, tt, 0:G], x_tile[:, 1, t], wsp[:, slot, k, 0, :], False, stop)
                return ins

            def dense(operand, n_units, tokens=False, ready=None, beside=None):
                par = group.n % 2
                pe.wait_ge(s_psfree, group.at(1))
                for q in range(n_units):
                    slot = unit.n % RING
                    if beside:
                        beside(q)
                    if ready:
                        ready(q)
                    pe.wait_ge(s_lo, unit.at(1 + RING))
                    for k in range(UK):
                        kk = q * UK + k
                        first, last = kk == 0, kk == n_units * UK - 1
                        if tokens:
                            ins = moving_weights(slot, k, operand[:, kk], par, first, last)
                        else:
                            ins = stationary_weights(slot, k, operand[:, kk, :, :].rearrange("p a t -> p (a t)"), par,
                                                     first, last)
                        if k == UK - 1:
                            ins.then_inc(s_used, 1)
                    unit.n += 1
                group.n += 1

            def u_ready(q):
                pe.wait_ge(s_u, hn.at(2 * (q + 1)))

            def norm_sums(token_major):
                norm.n += 1
                pe.wait_ge(s_ssq, norm.at())
                ins = mm(pm[:, 0, 0:S], ones[:, :], ssq[:, :], True, True)
                if token_major:
                    for tt in range(TT):
                        ins = mm(pm[:, 0, S + tt:S + tt + 1], ssq[:, tt * P:(tt + 1) * P], ones[:, 0:1], True, True)
                ins.then_inc(s_nmm, 1)

            pe.sem_inc(s_used, RING)
            pe.wait_ge(s_cst, 16)
            pe.wait_ge(s_gain, 16)
            n = DEPTH * KT
            nc.tensor.transpose(pd[:, 0, 0, 0:n], prm_rows[0:n, :], ident[0:n, 0:n]).then_inc(s_tr, 1)
            for g in range(8):
                pe.wait_ge(s_x[g // 4], 16)
                if g >= 4:
                    pe.wait_ge(s_hnew, g - 3)
                for j in range(2):
                    for tt in range(TT):
                        c = (2 * g + j) * P
                        ins = nc.tensor.transpose(pm[:, g % 4, j * S + tt * P:j * S + (tt + 1) * P], xtok[:, tt, c:c + P],
                                                  ident)
                ins.then_inc(s_tr, 1)
            pe.wait_ge(s_hnew, 8)
            pe.wait_ge(s_rest, 3 * 16)
            pe.wait_ge(s_small, n_small)
            nc.tensor.transpose(pm[:, 1, 0:R_ALL], prm_rows[0:R_ALL, :], ident[0:R_ALL, 0:R_ALL]).then_inc(s_tr, 1)

            with turns(pe, DEPTH, [(unit, UNITS_PER_LAYER), (group, GROUPS_PER_LAYER), (norm, 3), (hn, 24),
                                   (hidc, 22)], s_began) as layer:
                dense(u, 4, ready=u_ready)
                hn.n += 8
                norm_sums(True)
                pe.wait_ge(s_walr, layer * 2 + 2)
                pe.wait_ge(s_psfree, group.at(1))
                for k in range(KT):
                    ins = mm(pd[0:2 * RANK, 1, 0, :], walr[:, k, :, :].rearrange("p a n -> p (a n)"),
                             u[:, k, :, :].rearrange("p a t -> p (a t)"), k == 0, k == KT - 1)
                ins.then_inc(s_half, 1)
                group.n += 1

                def logits(_):
                    pe.wait_ge(s_ev, layer * EV + EV_RANK)
                    pe.wait_ge(s_lay[1], layer * 16 + 16)
                    for hh in range(GLA_H):
                        ins = mm(pm[:, hh // 2, hh % 2 * S:(hh % 2 + 1) * S], wal[:, hh * DK:(hh + 1) * DK], alrT[:, :],
                                 True, True)
                    ins.then_inc(s_xa, 1)

                def norm_item(n):
                    w = items(dq, dk, sq, sk)[n].shape[-1]
                    if n == 1:
                        pe.wait_ge(s_sv, layer + 1)
                    elif n:
                        pe.wait_ge(s_rope, layer * 7 + n)
                    if steps_before("norm", n):
                        pe.wait_ge(s_tpc, layer * 16 + steps_before("norm", n))
                    pe.wait_ge(s_nsq, layer * 7 + (n + 1))
                    mm(pm[:, 3, 0:w], cst[:, K_BLK:K_BLK + P], nsq[:, 0:w], True, True).then_inc(s_nss, 1)

                def rope(n):
                    item = items(dq, dk, sq, sk)[n]
                    pe.wait_ge(s_qn, layer * 7 + (n + 1))
                    if n:
                        mm(pm[:, 3, :], cst[:, K_ROT:K_ROT + P], item, True, True).then_inc(s_rot, 1)
                    else:
                        for g in range(2):
                            ins = mm(pm[:, 3, g * S:(g + 1) * S], cst[:, K_SEL + g * P:K_SEL + (g + 1) * P], item, True, True)
                        ins.then_inc(s_rot, 1)

                def swa_k(_):
                    pe.wait_ge(s_kcos, layer + 1)
                    for g in range(2):
                        ins = mm(pm[:, 3, g * S:(g + 1) * S], cst[:, K_RSEL + g * P:K_RSEL + (g + 1) * P], sk, True, True)
                    ins.then_inc(s_krot, 1)

                def swa_v(_):
                    pe.wait_ge(s_rope, layer * 7 + 1)
                    for tt in range(TT):
                        ins = nc.tensor.transpose(pm[:, 3, tt * P:(tt + 1) * P], svT[:, tt * P:(tt + 1) * P], ident)
                    ins.then_inc(s_svT, 1)

                def scores(z):
                    j, half = z % 2, z // 2
                    kw = (j + 1) * P
                    if z == 0:
                        pe.wait_ge(s_xc, layer + 1)
                    else:
                        pe.wait_ge(s_ex, layer * 16 + z)
                    if z < 8:
                        pe.wait_ge(s_rope, layer * 7 + (2 + half // 2))
                    else:
                        pe.wait_ge(s_rope, layer * 7 + (6 + (half - 4) // 2))
                    for e in range(2):
                        r = slice(e * HD, (e + 1) * HD)
                        if z < 8:
                            k0 = CHUNK * j
                            ins = mm(pm[:, e, k0:kw], sq[r, half, j * P:(j + 1) * P], kd[r, half // 2, k0:kw], True, True)
                        else:
                            ins = mm(pm[:, e, 0:kw], dq[r, half - 4, j * P:(j + 1) * P], dk[r, half - 4, 0:kw], True, True)
                    ins.then_inc(s_sc, 1)

                def transpose(z):
                    j = z % 2
                    pe.wait_ge(s_rope, layer * 7 + steps_before("transpose", z))
                    if z > 9 and j == 0:
                        pe.wait_ge(s_ors, layer * DIFF_H + (z // 2 - 4))
                    pe.wait_ge(s_wt, layer * 16 + (z + 1))
                    for e in range(2 if z < 8 else 1):
                        for kt in range(j + 1):
                            c = (2 * e + kt) * P
                            ins = nc.tensor.transpose(pm[:, 3, c:c + P], pe_buf[:, j, e, kt * P:(kt + 1) * P], ident)
                    ins.then_inc(s_tp, 1)

                def values(z):
                    j = z % 2
                    if z < 8:
                        pe.wait_ge(s_sv, layer + 1)
                    else:
                        pe.wait_ge(s_ev, layer * EV + EV_DV)
                    if j == 0 and z:
                        pe.wait_ge(s_mix, layer * 12 + z // 2)
                    pe.wait_ge(s_tpc, layer * 16 + (z + 1))
                    for e in range(2 if z < 8 else 1):
                        for kt in range(j + 1):
                            if z < 8:
                                g = z // 4
                                ins = mm(pm[e * HD:(e + 1) * HD, 2, j * P:(j + 1) * P], sv[:, kt, g * HD:(g + 1) * HD],
                                         wT[:, j, 2 * e + kt, :], kt == 0, kt == j)
                            else:
                                hh = z // 2 - 4
                                ins = mm(pm[:, 2, j * P:(j + 1) * P], dv[:, kt, hh * P:(hh + 1) * P], wT[:, j, kt, :],
                                         kt == 0, kt == j)
                    if j == 1:
                        ins.then_inc(s_pv, 1)

                def diff_norm(hh):
                    pe.wait_ge(s_osq, layer * DIFF_H + (hh + 1))
                    mm(pm[:, 3, 0:S], ones[:, :], osq, True, True).then_inc(s_oss, 1)

                def blocks(i):
                    hh = i // 4
                    if i % 4 == 0:
                        if i == 0:
                            pe.wait_ge(s_qd, layer + 1)
                            pe.wait_ge(s_kfar, layer + 1)
                            pe.wait_ge(s_mf, layer * 8 + DIFF_H)
                        else:
                            pe.wait_ge(s_att, layer * GLA_H + hh)
                        mm(pm[:, 3, P:2 * P], kfar[:, hh, :], qfar[:, hh, :], True, True)
                    pe.wait_ge(s_kn, layer * 16 + (i + 1))
                    for n in range(4 * i % NBLK, 4 * i % NBLK + 4):
                        c = n // 8 * S + n % 8 * BLK
                        ins = mm(pm[:, 3, c:c + BLK], kn[:, n % 8, :], qg[:, hh, BLK * n:BLK * (n + 1)], True, True)
                    ins.then_inc(s_am, 1)

                def gla_out(hh):
                    pe.wait_ge(s_mf, layer * 8 + (DIFF_H + hh))
                    pe.wait_ge(s_ev, layer * EV + (EV_GV + hh + 1))
                    pe.wait_ge(s_att, layer * GLA_H + (hh + 1))
                    for vb in range(2):
                        c = hh * DV + vb * P
                        mm(pm[:, 2, vb * S:(vb + 1) * S], vg[:, 0, c:c + P], att[:, 0:S], True, False)
                        ins = mm(pm[:, 2, vb * S + P:(vb + 1) * S], vg[:, 1, c:c + P], att[:, S:S + P], False, True)
                    ins.then_inc(s_go, 1)

                def gla_norm(hh):
                    pe.wait_ge(s_gsq, layer * GLA_H + (hh + 1))
                    mm(pm[:, 0, 0:S], ones[:, :], pe_buf[:, 0, 0, :], True, False)
                    mm(pm[:, 0, 0:S], ones[:, :], pe_buf[:, 0, 1, :], False, True).then_inc(s_gss, 1)

                steps = dict(logits=logits, norm=norm_item, rope=rope, swa_k=swa_k, swa_v=swa_v,
                             scores=scores, transpose=transpose, values=values, diff_norm=diff_norm, blocks=blocks,
                             gla_out=gla_out, gla_norm=gla_norm)

                def beside(slot):
                    for step, i in BESIDE.get(slot, ()):
                        if step in steps:
                            steps[step](i)

                for g in range(1, 21):
                    dense(u, 4, tokens=g in BY_TOKEN, beside=lambda q: beside(4 * g + q))

                pe.wait_ge(s_mix, layer * 12 + 8)
                for g in range(2):
                    dense(hid[:, 8:16], 2, beside=lambda q: beside(84 + 2 * g + q))
                with turns(pe, 3, [(unit, 4), (group, 2)], s_began):
                    dense(hid[:, 8:16], 2)
                    dense(hid[:, 8:16], 2)
                pe.wait_ge(s_mix, layer * 12 + 12)
                with turns(pe, 4, [(unit, 4), (group, 2)], s_began):
                    dense(hid, 2)
                    dense(hid, 2)

                for r, n in enumerate(ROUNDS):
                    pairs = n // 2
                    if r == len(ROUNDS) - 1:
                        pe.wait_ge(s_lay[2], layer * 16 + 16)
                        for j in range(2):
                            for tt in range(TT):
                                ins = nc.tensor.transpose(pm[:, 1, j * S + tt * P:j * S + (tt + 1) * P],
                                                          ptok[:, tt, j * P:(j + 1) * P], ident)
                        ins.then_inc(s_p, 1)
                    if r == 0:
                        dense(u, 4, ready=u_ready)
                        hn.n += 8
                        norm_sums(False)
                        dense(u, 4)
                        pairs -= 1
                    with turns(pe, pairs, [(unit, 8), (group, 2)], s_began):
                        dense(u, 4)
                        dense(u, 4)

                    def hid_ready(q):
                        pe.wait_ge(s_hid, hidc.at(2 * (q + 1)))

                    per = 2 if n == 16 else 4
                    dense(hid, n // UK, ready=hid_ready)
                    for _ in range(per - 1):
                        dense(hid, n // UK)
                    with turns(pe, 8 // per - 1, [(unit, n // 4 * per), (group, per)], s_began):
                        for _ in range(per):
                            dense(hid, n // UK)
                    hidc.n += n // 2

                pe.wait_ge(s_plo, layer + 1)
                for g in range(8):
                    par = group.n % 2
                    pe.wait_ge(s_psfree, group.at(1))
                    if g % 2 == 0:
                        pe.wait_ge(s_lo, unit.at(1 + RING))
                    for k in range(2):
                        xp = pT[:, k, :, :].rearrange("p a t -> p (a t)")
                        ins = stationary_weights(unit.n % RING, k, xp, par, k == 0, k == 1, cols=g % 2 * G, width=4)
                    if g % 2 == 1:
                        ins.then_inc(s_used, 1)
                        unit.n += 1
                    else:
                        ins.then_inc(s_half, 1)
                    group.n += 1
                dense(u, 4, ready=u_ready)
                hn.n += 8
                norm_sums(False)
                dense(u, 4)
                with turns(pe, 3, [(unit, 8), (group, 2)], s_began):
                    dense(u, 4)
                    dense(u, 4)

            for g in range(8):
                pe.wait_ge(s_hnew, 24 * DEPTH + g + 1)
                if g >= 4:
                    pe.wait_ge(s_trc, g - 3)
                for tt in range(TT):
                    for j in range(2):
                        ins = nc.tensor.transpose(pm[:, g % 4, tt * S + j * P:tt * S + (j + 1) * P],
                                                  h[:, 2 * g + j, tt * P:(tt + 1) * P], ident)
                ins.then_inc(s_tr, 1)


LN_EXP = "natural_log_exp_and_others"
ACT_LINKS = 22
DVE_LINKS = 217


def items(dq, dk, sq, sk):
    def pair(t, n):
        return t[:, 2 * n:2 * n + 2, :].rearrange("p a t -> p (a t)")
    return [sk, pair(sq, 0), pair(sq, 1), pair(dq, 0), pair(dq, 1), pair(dk, 0), pair(dk, 1)]


ITEM_GAINS = (R_SK, R_SQ, R_SQ, R_DQ, R_DQ, R_DK, R_DK)
BY_TOKEN = (7, 8, 17, 18, 19, 20)
BESIDE = schedule()


INPUTS = ["x", "p", "positions", "norm_mix_g", "w_in", "gla_w_alpha", "gla_b_alpha", "gla_norm_g",
          "diff_q_norm_g", "diff_k_norm_g", "diff_lambda_q1", "diff_lambda_k1", "diff_lambda_q2",
          "diff_lambda_k2", "diff_subln_g", "swa_q_norm_g", "swa_k_norm_g", "swa_sinks", "w_out",
          "norm_ffn_g", "w_ffn_in", "w_ffn_out", "norm_ple_g", "w_ple_gate", "w_ple_proj"]


def constants():
    import math

    import numpy as np
    c = np.zeros((P, K_COLS), np.float32)
    c[:, K_ID:K_ID + P] = np.eye(P)
    rot = np.zeros((P, P), np.float32)
    for m in range(P):
        d = m % HD
        if d < HALF:
            rot[m + HALF, m] = -1.0
        else:
            rot[m - HALF, m] = 1.0
    c[:, K_ROT:K_ROT + P] = rot
    for g in range(SWA_KV):
        sel = np.zeros((P, P), np.float32)
        for m in range(P):
            sel[g * HD + m % HD, m] = 1.0
        c[:, K_SEL + g * P:K_SEL + (g + 1) * P] = sel
        c[:, K_RSEL + g * P:K_RSEL + (g + 1) * P] = rot @ sel
    head = np.arange(P) // HD
    c[:, K_BLK:K_BLK + P] = (head[:, None] == head[None, :]) / HD
    tri = np.arange(P)[:, None] <= np.arange(P)[None, :]
    c[:, K_TRI:K_TRI + 3 * P] = np.concatenate([tri, np.ones((P, P)), tri], axis=1)
    inv = np.float32(1.0) / np.float32(10000.0) ** (np.arange(0, HD, 2, dtype=np.float32) / np.float32(HD))
    c[:, K_INV] = inv.astype(np.float32)[np.arange(P) % HALF]
    for i in range(DEPTH):
        c[:, K_LAM + i] = 0.8 - 0.6 * math.exp(-0.3 * i)
        c[:, K_ONE_LAM + i] = 1.0 - (0.8 - 0.6 * math.exp(-0.3 * i))
    return c


def kernel(**inputs):
    import numpy as np

    import concourse.bacc as bacc
    from concourse.bass_utils import run_bass_kernel_spmd as run

    nc = bacc.Bacc("TRN2", target_bir_lowering=False, num_devices=1)
    arrays = {f"in_{n}": np.ascontiguousarray(inputs[n]) for n in INPUTS}
    arrays["in_consts"] = constants()
    args = [nc.dram_tensor(n, a.shape, mybir.dt.from_np(a.dtype), kind="ExternalInput").ap() for n, a in arrays.items()]
    out = nc.dram_tensor("out", (1, S, D), F32, kind="ExternalOutput").ap()
    build(nc, *args, out)
    return run(nc, [arrays], core_ids=[0]).results[0]["out"]
```
